# Optimizing a Trainium2 kernel written in Bass

```python
import jax, jax.numpy as jnp
from jax import lax
import numpy as np

D_MODEL = 2048
BATCH = 1
SEQ = 256
DEPTH = 1

N_BRANCH = 4
BRANCH_WIDTH = D_MODEL // 4
LRU_WIDTH = BRANCH_WIDTH
LRU_BLOCKS = 8
LRU_BLOCK_DIM = LRU_WIDTH // LRU_BLOCKS
LRU_CONV = 4
LRU_C = 8.0
POOL_WIDTH = BRANCH_WIDTH
POOL_WINDOWS = (2, 4, 8, 16)
POOL_GROUPS = 4
POOL_GROUP_DIM = POOL_WIDTH // POOL_GROUPS
SCONV_WIDTH = BRANCH_WIDTH
SCONV_K = 3
ATTN_HEADS = 8
HEAD_DIM = BRANCH_WIDTH // ATTN_HEADS
ATTN_WIDTH = ATTN_HEADS * HEAD_DIM
Q_BLOCK = 128
D_FF = 4 * D_MODEL
EPS = 1e-6
IN_SIZES = (LRU_WIDTH, POOL_WIDTH, 3 * SCONV_WIDTH, 3 * ATTN_WIDTH, ATTN_HEADS, N_BRANCH * D_MODEL)
N_IN = sum(IN_SIZES)


def _split_points():
    return [int(v) for v in np.cumsum(IN_SIZES)[:-1]]

def rms_norm(x, g):
    xf = x.astype(jnp.float32)
    y = xf * lax.rsqrt(jnp.mean(xf * xf, axis=-1, keepdims=True) + EPS)
    return (y * g.astype(jnp.float32)).astype(x.dtype)

def causal_depthwise_conv(x, w):
    k_width = w.shape[0]
    s = x.shape[1]
    xp = jnp.pad(x, ((0, 0), (k_width - 1, 0), (0, 0)))
    return sum(w[k] * xp[:, k:k + s] for k in range(k_width))

def rglru_branch(xa, conv_w, conv_b, wr, br, wi, bi, lam):
    b, s, _ = xa.shape
    u = causal_depthwise_conv(xa, conv_w) + conv_b
    ub = u.reshape(b, s, LRU_BLOCKS, LRU_BLOCK_DIM)
    r = jax.nn.sigmoid(jnp.einsum('bshi,hij->bshj', ub, wr).reshape(b, s, LRU_WIDTH) + br)
    gi = jax.nn.sigmoid(jnp.einsum('bshi,hij->bshj', ub, wi).reshape(b, s, LRU_WIDTH) + bi)
    log_a = (-LRU_C * r.astype(jnp.float32)) * jax.nn.softplus(-lam.astype(jnp.float32))
    a = jnp.exp(log_a)
    inp = jnp.sqrt(-jnp.expm1(2.0 * log_a)) * (gi * u).astype(jnp.float32)

    def combine(c1, c2):
        a1, b1 = c1
        a2, b2 = c2
        return a1 * a2, a2 * b1 + b2

    _, h = lax.associative_scan(combine, (a, inp), axis=1)
    return h.astype(xa.dtype)

def pool_branch(xp, w_grp, scale):
    b, s, _ = xp.shape
    xf = xp.astype(jnp.float32)
    csum = jnp.pad(jnp.cumsum(xf, axis=1), ((0, 0), (1, 0), (0, 0)))
    t = jnp.arange(s)
    outs = []
    for gidx, win in enumerate(POOL_WINDOWS):
        sl = slice(gidx * POOL_GROUP_DIM, (gidx + 1) * POOL_GROUP_DIM)
        start = jnp.maximum(t + 1 - win, 0)
        win_sum = csum[:, 1:, sl] - csum[:, start, sl]
        count = jnp.minimum(t + 1, win).astype(jnp.float32)[None, :, None]
        outs.append(win_sum / count - xf[:, :, sl])
    pooled = jnp.stack(outs, axis=2)
    mixed = jnp.einsum('bsgi,gij->bsgj', pooled, w_grp.astype(jnp.float32)).reshape(b, s, POOL_WIDTH)
    return (mixed * scale.astype(jnp.float32)).astype(xp.dtype)

def shortconv_branch(xsc, w):
    gate_b, gate_c, xc = jnp.split(xsc, 3, axis=-1)
    return gate_b * causal_depthwise_conv(gate_c * xc, w)

def forgetting_attention(qkv, f_logit, f_bias, q_g, k_g):
    b, s, _ = qkv.shape
    q, k, v = jnp.split(qkv, 3, axis=-1)
    q = rms_norm(q.reshape(b, s, ATTN_HEADS, HEAD_DIM), q_g)
    k = rms_norm(k.reshape(b, s, ATTN_HEADS, HEAD_DIM), k_g)
    v = v.reshape(b, s, ATTN_HEADS, HEAD_DIM)
    log_f = jax.nn.log_sigmoid((f_logit + f_bias).astype(jnp.float32))
    cum = jnp.cumsum(log_f, axis=1).transpose(0, 2, 1)
    n_blk = s // Q_BLOCK
    qb = q.reshape(b, n_blk, Q_BLOCK, ATTN_HEADS, HEAD_DIM).transpose(1, 0, 2, 3, 4)
    cqb = cum.reshape(b, ATTN_HEADS, n_blk, Q_BLOCK).transpose(2, 0, 1, 3)
    key_pos = jnp.arange(s)
    scale = HEAD_DIM ** -0.5

    def one_block(args):
        qi, cqi, blk = args
        logits = jnp.einsum('bqhd,bkhd->bhqk', qi, k).astype(jnp.float32) * scale
        logits = logits + (cqi[..., :, None] - cum[..., None, :])
        q_pos = blk * Q_BLOCK + jnp.arange(Q_BLOCK)
        logits = jnp.where(key_pos[None, :] <= q_pos[:, None], logits, -jnp.inf)
        p = jax.nn.softmax(logits, axis=-1)
        return jnp.einsum('bhqk,bkhd->bqhd', p.astype(v.dtype), v)

    out = lax.map(one_block, (qb, cqb, jnp.arange(n_blk)))
    return out.transpose(1, 0, 2, 3, 4).reshape(b, s, ATTN_WIDTH)

def first_inputs(seed: int = 0) -> dict:
    key = jax.random.key(seed)
    ks = jax.random.split(key, 24)
    L, D, W = DEPTH, D_MODEL, BRANCH_WIDTH
    nrm = lambda k, shape, fan: jax.random.normal(k, shape, jnp.float32) * (fan ** -0.5)
    u = jax.random.uniform(ks[9], (L, LRU_WIDTH), jnp.float32, 0.9, 0.999)
    a0 = u ** (1.0 / LRU_C)
    return {
        "x": jax.random.normal(ks[0], (BATCH, SEQ, D), jnp.float32),
        "norm_mix_g": 1.0 + 0.1 * jax.random.normal(ks[1], (L, D), jnp.float32),
        "w_in": nrm(ks[2], (L, D, N_IN), D),
        "lru_conv_w": nrm(ks[3], (L, LRU_CONV, LRU_WIDTH), LRU_CONV),
        "lru_conv_b": 0.02 * jax.random.normal(ks[4], (L, LRU_WIDTH), jnp.float32),
        "lru_wr": nrm(ks[5], (L, LRU_BLOCKS, LRU_BLOCK_DIM, LRU_BLOCK_DIM), LRU_BLOCK_DIM),
        "lru_br": 0.02 * jax.random.normal(ks[6], (L, LRU_WIDTH), jnp.float32),
        "lru_wi": nrm(ks[7], (L, LRU_BLOCKS, LRU_BLOCK_DIM, LRU_BLOCK_DIM), LRU_BLOCK_DIM),
        "lru_bi": 0.02 * jax.random.normal(ks[8], (L, LRU_WIDTH), jnp.float32),
        "lru_lambda": jnp.log(a0) - jnp.log1p(-a0),
        "pool_w": nrm(ks[10], (L, POOL_GROUPS, POOL_GROUP_DIM, POOL_GROUP_DIM), POOL_GROUP_DIM),
        "pool_scale": 1.0 + 0.1 * jax.random.normal(ks[11], (L, POOL_WIDTH), jnp.float32),
        "sconv_w": nrm(ks[12], (L, SCONV_K, SCONV_WIDTH), SCONV_K),
        "q_norm_g": 1.0 + 0.1 * jax.random.normal(ks[13], (L, HEAD_DIM), jnp.float32),
        "k_norm_g": 1.0 + 0.1 * jax.random.normal(ks[14], (L, HEAD_DIM), jnp.float32),
        "forget_b": jax.random.uniform(ks[15], (L, ATTN_HEADS), jnp.float32, 1.0, 5.0),
        "w_branch": nrm(ks[16], (L, N_BRANCH, W, D), W),
        "w_out": nrm(ks[17], (L, D, D), D),
        "norm_mlp_g": 1.0 + 0.1 * jax.random.normal(ks[18], (L, D), jnp.float32),
        "w_mlp_up": nrm(ks[19], (L, D, D_FF), D),
        "w_mlp_down": nrm(ks[20], (L, D_FF, D), D_FF),
    }

def first_block(x, norm_mix_g, w_in, lru_conv_w, lru_conv_b, lru_wr, lru_br, lru_wi, lru_bi,
              lru_lambda, pool_w, pool_scale, sconv_w, q_norm_g, k_norm_g, forget_b,
              w_branch, w_out, norm_mlp_g, w_mlp_up, w_mlp_down):
    b, s, d = x.shape
    split_pts = _split_points()
    for l in range(DEPTH):
        xn = rms_norm(x, norm_mix_g[l])
        proj = xn @ w_in[l]
        xa, xpool, xsc, qkv, f_logit, gate_logits = jnp.split(proj, split_pts, axis=-1)
        y_a = rglru_branch(xa, lru_conv_w[l], lru_conv_b[l], lru_wr[l], lru_br[l],
                           lru_wi[l], lru_bi[l], lru_lambda[l])
        y_b = pool_branch(xpool, pool_w[l], pool_scale[l])
        y_c = shortconv_branch(xsc, sconv_w[l])
        y_d = forgetting_attention(qkv, f_logit, forget_b[l], q_norm_g[l], k_norm_g[l])
        ys = jnp.stack([y_a, y_b, y_c, y_d], axis=2)
        branches = jnp.einsum('bskw,kwd->bskd', ys, w_branch[l])
        gates = jax.nn.sigmoid(gate_logits.reshape(b, s, N_BRANCH, d))
        merged = jnp.sum(gates * branches, axis=2)
        x = x + merged @ w_out[l]
        h = rms_norm(x, norm_mlp_g[l]) @ w_mlp_up[l]
        x = x + jnp.square(jax.nn.relu(h)) @ w_mlp_down[l]
    return x


HEAD_DIM_2 = 64
A_HEADS = 8
A_WIDTH = A_HEADS * HEAD_DIM_2
DILATED_PAIRS = ((128, 1), (512, 4), (2048, 16))
B_WIDTH = 512
CONV_WIDTH = 31
C_Q_HEADS = 16
C_KV_HEADS = 2
C_WIDTH = C_Q_HEADS * HEAD_DIM_2
C_WINDOW = 128
MIX_WIDTH = A_WIDTH + B_WIDTH + C_WIDTH
IN_WIDTHS = (A_WIDTH, A_WIDTH, A_WIDTH,
             B_WIDTH, B_WIDTH,
             C_WIDTH, C_KV_HEADS * HEAD_DIM_2, C_KV_HEADS * HEAD_DIM_2)
IN_WIDTH = sum(IN_WIDTHS)
D_FF_2 = -(-(8 * D_MODEL) // (3 * 256)) * 256
BLOCK = 128


def _rms_norm(x, g):
    xf = x.astype(jnp.float32)
    y = xf * lax.rsqrt(jnp.mean(xf * xf, axis=-1, keepdims=True) + EPS)
    return (y * g.astype(jnp.float32)).astype(x.dtype)

def _layer_norm(x, g, b):
    xf = x.astype(jnp.float32)
    mu = jnp.mean(xf, axis=-1, keepdims=True)
    var = jnp.mean(jnp.square(xf - mu), axis=-1, keepdims=True)
    y = (xf - mu) * lax.rsqrt(var + EPS)
    return (y * g.astype(jnp.float32) + b.astype(jnp.float32)).astype(x.dtype)

def _band_attention(q, k, v, max_dist, sinks=None):
    N, L, Hq, hd = q.shape
    Hk = k.shape[2]
    G = Hq // Hk
    blk = min(BLOCK, L)
    nb = -(-L // blk)
    Lp = nb * blk
    C = blk + max_dist
    qb = jnp.pad(q, ((0, 0), (0, Lp - L), (0, 0), (0, 0))).reshape(N, nb, blk, Hk, G, hd)
    kp = jnp.pad(k, ((0, 0), (max_dist, Lp - L), (0, 0), (0, 0)))
    vp = jnp.pad(v, ((0, 0), (max_dist, Lp - L), (0, 0), (0, 0)))
    idx = jnp.arange(nb)[:, None] * blk + jnp.arange(C)[None, :]
    kb = kp[:, idx]
    vb = vp[:, idx]
    s = jnp.einsum('nbqhgd,nbkhd->nbhgqk', qb, kb,
                   preferred_element_type=jnp.float32) * (hd ** -0.5)
    qpos = jnp.arange(nb)[:, None] * blk + jnp.arange(blk)[None, :]
    kpos = idx - max_dist
    dist = qpos[:, :, None] - kpos[:, None, :]
    valid = (dist >= 0) & (dist <= max_dist) & (kpos[:, None, :] >= 0)
    s = jnp.where(valid[None, :, None, None], s, -jnp.inf)
    m = jnp.max(s, axis=-1)
    if sinks is not None:
        sk = sinks.astype(jnp.float32).reshape(Hk, G)[None, None, :, :, None]
        m = jnp.maximum(m, sk)
    p = jnp.exp(s - m[..., None])
    denom = jnp.sum(p, axis=-1)
    if sinks is not None:
        denom = denom + jnp.exp(sk - m)
    o = jnp.einsum('nbhgqk,nbkhd->nbqhgd', p, vb.astype(jnp.float32))
    denom_t = jnp.transpose(denom, (0, 1, 4, 2, 3))
    o = o / denom_t[..., None]
    lse = jnp.transpose(m, (0, 1, 4, 2, 3)) + jnp.log(denom_t)
    o = o.reshape(N, Lp, Hq, hd)[:, :L]
    lse = lse.reshape(N, Lp, Hq)[:, :L]
    return o, lse

def _dilated_mixture(q, k, v):
    B, S, H, hd = q.shape
    outs, lses = [], []
    for (w, d) in DILATED_PAIRS:
        def to_res(t):
            return t.reshape(B, S // d, d, H, hd).transpose(0, 2, 1, 3, 4).reshape(B * d, S // d, H, hd)
        o, lse = _band_attention(to_res(q), to_res(k), to_res(v), w // d)
        outs.append(o.reshape(B, d, S // d, H, hd).transpose(0, 2, 1, 3, 4).reshape(B, S, H, hd))
        lses.append(lse.reshape(B, d, S // d, H).transpose(0, 2, 1, 3).reshape(B, S, H))
    wts = jax.nn.softmax(jnp.stack(lses, axis=0), axis=0)
    return jnp.einsum('cbsh,cbshd->bshd', wts, jnp.stack(outs, axis=0))

def _conformer_conv(u, gate, conv_w, conv_b, ln_g, ln_b):
    h = u * jax.nn.sigmoid(gate)
    C = h.shape[-1]
    y = lax.conv_general_dilated(h, conv_w[:, None, :].astype(h.dtype), window_strides=(1,),
                                 padding=[(CONV_WIDTH - 1, 0)],
                                 dimension_numbers=('NWC', 'WIO', 'NWC'),
                                 feature_group_count=C)
    y = y + conv_b
    return jax.nn.silu(_layer_norm(y, ln_g, ln_b))

def second_inputs(seed: int = 0) -> dict:
    key = jax.random.key(seed)
    ks = jax.random.split(key, 17)
    f32 = jnp.float32
    nrm = lambda k, shp: jax.random.normal(k, shp, dtype=f32)
    return {
        "x": nrm(ks[0], (BATCH, SEQ, D_MODEL)),
        "norm1_g": 1.0 + 0.02 * nrm(ks[1], (DEPTH, D_MODEL)),
        "w_in": nrm(ks[2], (DEPTH, D_MODEL, IN_WIDTH)) * D_MODEL ** -0.5,
        "a_q_g": 1.0 + 0.02 * nrm(ks[3], (DEPTH, HEAD_DIM_2)),
        "a_k_g": 1.0 + 0.02 * nrm(ks[4], (DEPTH, HEAD_DIM_2)),
        "conv_w": nrm(ks[5], (DEPTH, CONV_WIDTH, B_WIDTH)) * CONV_WIDTH ** -0.5,
        "conv_b": 0.02 * nrm(ks[6], (DEPTH, B_WIDTH)),
        "conv_ln_g": 1.0 + 0.02 * nrm(ks[7], (DEPTH, B_WIDTH)),
        "conv_ln_b": 0.02 * nrm(ks[8], (DEPTH, B_WIDTH)),
        "c_q_g": 1.0 + 0.02 * nrm(ks[9], (DEPTH, HEAD_DIM_2)),
        "c_k_g": 1.0 + 0.02 * nrm(ks[10], (DEPTH, HEAD_DIM_2)),
        "c_sinks": 0.5 * nrm(ks[11], (DEPTH, C_Q_HEADS)),
        "w_out": nrm(ks[12], (DEPTH, MIX_WIDTH, D_MODEL)) * MIX_WIDTH ** -0.5,
        "norm2_g": 1.0 + 0.02 * nrm(ks[13], (DEPTH, D_MODEL)),
        "w_gate": nrm(ks[14], (DEPTH, D_MODEL, D_FF_2)) * D_MODEL ** -0.5,
        "w_up": nrm(ks[15], (DEPTH, D_MODEL, D_FF_2)) * D_MODEL ** -0.5,
        "w_down": nrm(ks[16], (DEPTH, D_FF_2, D_MODEL)) * D_FF_2 ** -0.5,
    }

def second_block(x, norm1_g, w_in, a_q_g, a_k_g, conv_w, conv_b, conv_ln_g, conv_ln_b,
              c_q_g, c_k_g, c_sinks, w_out, norm2_g, w_gate, w_up, w_down):
    B, S, _ = x.shape
    splits = [int(s) for s in np.cumsum(IN_WIDTHS)[:-1]]
    for l in range(DEPTH):
        h = _rms_norm(x, norm1_g[l])
        proj = h @ w_in[l]
        aq, ak, av, bu, bg, cq, ck, cv = jnp.split(proj, splits, axis=-1)
        aq = _rms_norm(aq.reshape(B, S, A_HEADS, HEAD_DIM_2), a_q_g[l])
        ak = _rms_norm(ak.reshape(B, S, A_HEADS, HEAD_DIM_2), a_k_g[l])
        av = av.reshape(B, S, A_HEADS, HEAD_DIM_2)
        out_a = _dilated_mixture(aq, ak, av).reshape(B, S, A_WIDTH)
        out_b = _conformer_conv(bu, bg, conv_w[l], conv_b[l], conv_ln_g[l], conv_ln_b[l])
        cq = _rms_norm(cq.reshape(B, S, C_Q_HEADS, HEAD_DIM_2), c_q_g[l])
        ck = _rms_norm(ck.reshape(B, S, C_KV_HEADS, HEAD_DIM_2), c_k_g[l])
        cv = cv.reshape(B, S, C_KV_HEADS, HEAD_DIM_2)
        out_c, _ = _band_attention(cq, ck, cv, C_WINDOW - 1, sinks=c_sinks[l])
        out_c = out_c.reshape(B, S, C_WIDTH)
        mix = jnp.concatenate([out_a.astype(x.dtype), out_b.astype(x.dtype),
                               out_c.astype(x.dtype)], axis=-1)
        x = x + mix @ w_out[l]
        h2 = _rms_norm(x, norm2_g[l])
        x = x + (jax.nn.silu(h2 @ w_gate[l]) * (h2 @ w_up[l])) @ w_down[l]
    return x


def setup_inputs(seed=0):
    out = dict(first_inputs(seed))
    for name, value in second_inputs(seed + 1).items():
        if name != "x":
            out[name + "_2"] = value
    return out


def reference(
    x, norm_mix_g, w_in, lru_conv_w, lru_conv_b, lru_wr, lru_br, lru_wi, lru_bi, lru_lambda,
    pool_w, pool_scale, sconv_w, q_norm_g, k_norm_g, forget_b, w_branch, w_out, norm_mlp_g,
    w_mlp_up, w_mlp_down, norm1_g_2, w_in_2, a_q_g_2, a_k_g_2, conv_w_2, conv_b_2, conv_ln_g_2,
    conv_ln_b_2, c_q_g_2, c_k_g_2, c_sinks_2, w_out_2, norm2_g_2, w_gate_2, w_up_2, w_down_2,
):
    x = first_block(
        x, norm_mix_g, w_in, lru_conv_w, lru_conv_b, lru_wr, lru_br, lru_wi, lru_bi, lru_lambda,
        pool_w, pool_scale, sconv_w, q_norm_g, k_norm_g, forget_b, w_branch, w_out, norm_mlp_g,
        w_mlp_up, w_mlp_down,
    )
    return second_block(
        x, norm1_g_2, w_in_2, a_q_g_2, a_k_g_2, conv_w_2, conv_b_2, conv_ln_g_2, conv_ln_b_2,
        c_q_g_2, c_k_g_2, c_sinks_2, w_out_2, norm2_g_2, w_gate_2, w_up_2, w_down_2,
    )


_drawn_inputs = setup_inputs


def setup_inputs(seed=0):
    import zlib

    import numpy as np

    out = dict(_drawn_inputs(seed))
    spreads = {}
    factors = {'lru_br': 8.0,
     'lru_bi': 8.0,
     'q_norm_g': 4.522,
     'k_norm_g': 4.631,
     'norm1_g_2': 8.0,
     'a_q_g_2': 8.0,
     'a_k_g_2': 8.0,
     'conv_b_2': 26.001,
     'conv_ln_g_2': 45.395,
     'conv_ln_b_2': 43.936,
     'c_q_g_2': 8.0,
     'c_k_g_2': 8.0,
     'c_sinks_2': 129.716,
     'norm2_g_2': 6.291}
    for name, (base, spread) in spreads.items():
        noise = np.random.default_rng([zlib.crc32(name.encode()), seed]).standard_normal(out[name].shape)
        drawn = base * np.exp(spread * noise) if base else spread * noise
        out[name] = __import__('jax').numpy.asarray(drawn.astype(out[name].dtype))
    for name, factor in factors.items():
        out[name] = (out[name] * factor).astype(out[name].dtype)
    return out
```

```python
from contextlib import ExitStack

import numpy as np

import concourse.bass as bass
from concourse import mybir

F32 = mybir.dt.float32
F32R = mybir.dt.float32r
I32 = mybir.dt.int32
ALU = mybir.AluOpType
ACT = mybir.ActivationFunctionType
AX = mybir.AxisListType

P = 128
T = 256
MT = T // P
D = 2048
KT = D // P
NW = 512
UK = 4
UN = KT // UK
RAW = 4
SPL = 2
W = 512
CT = W // P
NB = 4
HEADS = 8
HD = 64
AUG = HD + 2
FF = 4 * D
FF2 = 5632
EPS = 1e-6
NEG = -1e30
LRU_C = 8.0
LRU_TAPS, SC_TAPS, CONV_TAPS = 4, 3, 31
LP, PP, SP_, CP = LRU_TAPS - 1, 15, SC_TAPS - 1, CONV_TAPS - 1
KB = 1024

IN_XA, IN_POOL, IN_GB, IN_GC, IN_XC, IN_Q, IN_K, IN_V, IN_F, IN_GATE = (
    0, 512, 1024, 1536, 2048, 2560, 3072, 3584, 4096, 4104)
HEAD1 = [IN_XA, IN_POOL, IN_GC, IN_XC, IN_GB, IN_Q, IN_K, IN_V]
I2_AQ, I2_AK, I2_AV, I2_BU, I2_BG, I2_CQ0, I2_CQ1, I2_CKV = 0, 512, 1024, 1536, 2048, 2560, 3072, 3584
HEAD2 = [I2_BU, I2_BG, I2_CQ0, I2_CKV, I2_CQ1, I2_AQ, I2_AK, I2_AV]

R_CONV, R_CONVB, R_BR, R_BI, R_LAM, R_PSCALE, R_SC = 0, 4, 5, 6, 7, 8, 9
R_CONV2, R_CONV2B, R_LNG, R_LNB = 12, 43, 44, 45
NPAR = 46
B_QG, B_KG, B_AQG, B_AKG, B_CQG, B_CKG, B_FB, B_SINK = 0, 64, 128, 192, 256, 320, 384, 392
NBC = 408

READERS = (
    "AAADAAAA"
    + ("AAAA" + "DDDD") * 4
    + "DDDD"
    + "AAAA" + ("DDDD" + "AAAA") * 3 + "DDDD"
    + "AAAAAAAA"
    + "DDDD" * 3
    + "AD" * 3 + "DDDD"
    + ("AD" * 4 + "DDDD") * 2
)
GROUPS = [(0, (0, 2, 4, 6)), (0, (1, 3, 5, 7)), (1, (0, 2)), (1, (4, 6)), (1, (1, 3)), (1, (5, 7))]


K_DIL, K_CONV, K_WIN0, K_WIN1 = 0, 4, 8, 12
CH2_FIRST, CH2_LOOP = 3, 4


def readers_before(run, who):
    return READERS[:run].count(who)


def blocks_of(group):
    tile, heads = group
    return [(h, kt) for h in heads for kt in range(tile + 1)]


def build(nc, t, out):
    ctx = ExitStack()
    with ctx:
        sem = lambda name: ctx.enter_context(nc.semaphore(name))

        base = -(-nc.sbuf_base // 32) * 32
        room = (nc.sbuf_usable_end - base) // KB - 1
        ctx.enter_context(nc.sbuf_tensor("arena", [P, room * 256], F32))

        def at(name, kb, shape, dtype=F32):
            return nc.alloc_sbuf_tensor_at(name, shape, dtype, offset=base + int(kb * KB))

        raw = at("raw", 0, [P, RAW, UK, NW])
        whi = at("whi", 32, [P, SPL, UK, NW], F32R)
        wlo = at("wlo", 48, [P, SPL, UK, NW], F32R)
        opA_hi = at("opA_hi", 64, [P, KT, T], F32R)
        opA_lo = at("opA_lo", 80, [P, KT, T], F32R)
        opB_hi = at("opB_hi", 96, [P, KT, T], F32R)
        opB_lo = at("opB_lo", 112, [P, KT, T], F32R)
        xres = at("xres", 128, [P, MT, D])
        stage = at("stage", 144, [P, MT, NW])
        gainB = at("gainB", 148, [P, D])
        gates = at("gates", 156, [P, NB, MT, NW])
        c0 = 172
        ident = at("ident", c0, [P, P])
        tri = at("tri", c0 + 0.5, [P, P])
        ones = at("ones", c0 + 1, [P, P])
        mask = at("mask", c0 + 1.5, [P, T])
        par = at("par", c0 + 2.5, [P, CT, NPAR])
        bcast = at("bcast", c0 + 3.25, [P, NBC])
        f_raw = at("f_raw", c0 + 5, [P, KT, HEADS])
        steps = at("steps", c0 + 8, [P, 16], I32)
        f_hi = at("f_hi", c0 + 5.5, [P, KT, HEADS], F32R)
        f_lo = at("f_lo", c0 + 6, [P, KT, HEADS], F32R)
        smalls = at("smalls", c0 + 6.5, [P, 384])
        c1 = c0 + 8.25
        used = [0]

        def small(n):
            used[0] += n
            assert used[0] <= 384
            return smalls[:, used[0] - n:used[0]]

        sumsq = small(8).rearrange("p (m c) -> p m c", m=MT)
        msq, rms, rstd = small(2), small(2), small(2)
        ftok = small(16)
        sp_neg, sp_abs, sp_e, sp_t, sp_r, sp_s, sp_s2, sp_p, logf = [small(16) for _ in range(9)]
        l_neg, l_abs, l_e, l_t, l_r, l_s, l_s2, l_p, l_c, l_c2 = [small(4) for _ in range(10)]
        recip_count = small(16 * CT).rearrange("p (g t) -> p g t", g=CT)
        negmax, rowsum, rinv = small(16), small(16), small(16)
        hsum, hroot, hinv = small(16), small(16), small(16)

        rows_par = at("rows_par", 156, [P, W])
        junk = at("junk", 160, [P, MT, NW])
        pool_a = at("pool_a", c1, [P, PP + T])
        pool_b = at("pool_b", c1 + 1.25, [P, PP + T])
        xaT = at("xaT", c1, [P, CT, LP + T])
        xpT = at("xpT", c1 + 4.25, [P, CT, PP + T])
        zT = at("zT", c1 + 8.75, [P, CT, SP_ + T])
        gbT = at("gbT", c1 + 13, [P, CT, T])
        lru_u = at("lru_u", c1 + 17, [P, CT, T])
        lru_om = at("lru_om", c1 + 21, [P, CT, T])
        lru_r = at("lru_r", 156, [P, CT, T])
        lru_g = at("lru_g", 160, [P, CT, T])
        lru_z = at("lru_z", 164, [P, CT, T])
        lru_p = at("lru_p", 168, [P, CT, T])
        wr_sb = at("wr_sb", c1 + 25, [P, CT, P])
        wi_sb = at("wi_sb", c1 + 27, [P, CT, P])
        pw_sb = at("pw_sb", c1 + 29, [P, CT, P])
        gc_sb = at("gc_sb", 148, [P, MT, NW])
        v_sb = at("v_sb", 152, [P, MT, NW])
        q_aug = at("q_aug", c1 + 31, [P, MT * HEADS, AUG])
        k_aug = at("k_aug", c1 + 35.25, [P, MT * HEADS, AUG])
        c2 = c1 + 39.5
        assert c2 <= room, (c2, room)
        qT = at("qT", c1, [P, HEADS, T])
        kT = at("kT", c1 + 8, [P, HEADS, T])
        scores = at("scores", c1 + 16, [P, NW])
        probs = at("probs", c1 + 18, [P, 2, NW])
        probsT = at("probsT", c1 + 22, [P, NW])

        acc = ctx.enter_context(nc.psum_tensor("acc", [P, 2, MT, NW], F32))
        tp = ctx.enter_context(nc.psum_tensor("tp", [P, 2, NW], F32))
        sd = ctx.enter_context(nc.psum_tensor("sd", [P, 2, NW], F32))

        u_sb = at("u_sb", 156, [P, MT, W])
        sig_sb = at("sig_sb", 160, [P, MT, W])
        tap_tmp = at("tap_tmp", 156, [P, 2, T])
        hT = at("hT", c1, [P, CT, CP + T])
        yT = at("yT", c1 + 4.5, [P, CT, T])
        y_tok = at("y_tok", c1 + 8.5, [P, MT, W])
        silT = at("silT", c1, [P, CT, T])
        q_tok = at("q_tok", c1 + 12.5, [P, 2, MT, W])
        q2T = at("q2T", c1 + 20.5, [P, 2, CT, T])
        kv_tok = at("kv_tok", c1 + 28.5, [P, MT, 2 * P])
        k_dup = at("k_dup", c1 + 30.5, [P, MT, 2, 2, HD])
        kwT = at("kwT", c1 + 32.5, [P, 2, T])
        win_mask = at("win_mask", c1 + 34.5, [P, T])
        dil_mask = at("dil_mask", c1 + 35.5, [P, T])
        mult4 = at("mult4", c1 + 36.5, [P, P])
        mult16 = at("mult16", c1 + 37, [P, P])
        dist = at("dist", c1 + 37.5, [P, 2, P], I32)
        smalls2 = at("smalls2", c1 + 38.5, [P, 256])
        near = at("near", c1 + 39.5, [P, P])
        far = at("far", c1 + 40, [P, P])
        assert c1 + 40.5 <= room, (c1, room)
        k_tok = at("k_tok", 156, [P, MT, W])
        kdT = at("kdT", 160, [P, CT, T])
        vd_sb = at("vd_sb", 164, [P, MT, W])
        squares2 = at("squares2", 168, [P, MT, W])
        scores2 = at("scores2", 148, [P, NW])
        probs2 = at("probs2", 150, [P, 2, NW])
        probsT2 = at("probsT2", 154, [P, NW])
        gain2 = at("gain2", c1, [P, D])
        silu_gate = at("silu_gate", 156, [P, MT, NW])
        stat2 = lambda k: smalls2[:, k * 48:(k + 1) * 48].rearrange("p (s c) -> p s c", s=3)
        negmax2, rowsum2, rinv2, sink_e = [stat2(k) for k in range(4)]
        nsink = smalls2[:, 192:208]
        bn6 = smalls2[:, 208:220].rearrange("p (m c) -> p m c", m=MT)
        bn2 = smalls2[:, 220:224].rearrange("p (m c) -> p m c", m=MT)
        bn_var, bn_root, bn_inv = [smalls2[:, 224 + 2 * k:226 + 2 * k] for k in range(3)]

        landed = [sem(f"landed{s}") for s in range(RAW)]
        hi_split = sem("hi_split")
        lo_split = sem("lo_split")
        units_used = sem("units_used")
        read_act = sem("read_act")
        read_dve = sem("read_dve")
        turned = sem("turned")
        op_hi = sem("op_hi")
        op_lo = sem("op_lo")
        staged = sem("staged")
        x_in = [sem(f"x_in{j}") for j in range(UN)]
        x_back = [sem(f"x_back{j}") for j in range(UN)]
        gain_in = [sem(f"gain_in{n}") for n in range(4)]
        sq_done = sem("sq_done")
        xg_done = sem("xg_done")
        msq_done, rms_done, rstd_done = sem("msq_done"), sem("rms_done"), sem("rstd_done")
        dv, pc, ac = sem("dv"), sem("pc"), sem("ac")
        consts, pads = sem("consts"), sem("pads")
        rc_ready = sem("rc_ready")
        rows_in, bc_in, f_in, sw_in = sem("rows_in"), sem("bc_in"), sem("f_in"), sem("sw_in")
        par_turned, par_ready = sem("par_turned"), sem("par_ready")
        stored = sem("stored")
        side_turned = sem("side_turned")
        side_read = sem("side_read")
        u_ready, lru_mm, r_ready, g_ready, a_ready = (
            sem("u_ready"), sem("lru_mm"), sem("r_ready"), sem("g_ready"), sem("a_ready"))
        lam_abs, lam_exp = sem("lam_abs"), sem("lam_exp")
        c_ready, z_ready = sem("c_ready"), sem("z_ready")
        om_ready, root_ready, h_ready = sem("om_ready"), sem("root_ready"), sem("h_ready")
        gu_ready, asq_ready = sem("gu_ready"), sem("asq_ready")
        pooled, pool_mm, sc_ready, sc_gated = sem("pooled"), sem("pool_mm"), sem("sc_ready"), sem("sc_gated")
        y_hi, y_lo = sem("y_hi"), sem("y_lo")
        f_split, f_mm, f_tok, f_abs, f_exp, f_log, f_cum, cum_mm = [
            sem("f_" + n) for n in ("split", "mm", "tok", "abs", "exp", "log", "cum", "cumm")]
        head_sq, head_sum, head_root, head_scaled, aug_done = [
            sem("head_" + n) for n in ("sq", "sum", "root", "scaled", "aug")]
        qk_done, s_ready, max_ready, p_ready, p_turned, pT_ready, pv_done = [
            sem("at_" + n) for n in ("qk", "s", "max", "p", "turn", "pT", "pv")]
        o_ready = sem("o_ready")
        tp_full = [sem(f"tp_full{b}") for b in range(2)]
        tp_free = [sem(f"tp_free{b}") for b in range(2)]
        h2_sq, h2_sum, h2_root, h2_scaled, h2_gained = [
            sem("h2_" + n) for n in ("sq", "sum", "root", "scaled", "gained")]
        glu_ready, conv_dve, conv_pool = sem("glu_ready"), sem("conv_dve"), sem("conv_pool")
        ln_var, ln_root, ln_done = sem("ln_var"), sem("ln_root"), sem("ln_done")
        mix_hi, conf_hi, conf_lo = sem("mix_hi"), sem("conf_hi"), sem("conf_lo")
        masks_raw, mults_ready, masks_ready = sem("masks_raw"), sem("mults_ready"), sem("masks_ready")
        sink_arg, sink_exp = sem("sink_arg"), sem("sink_exp")
        pads2, silu_done = sem("pads2"), sem("silu_done")
        merged_ready = sem("merged_ready")

        class Chain:

            def __init__(self, eng, s):
                self.eng, self.s, self.n = eng, s, 0

            def mark(self, ins):
                ins.then_inc(self.s, 1)
                self.n += 1
                return self.n

            def need(self, n):
                self.eng.wait_ge(self.s, n)

            def done(self, ins):
                self.need(self.mark(ins))

        block = ctx.enter_context(nc.Block())

        def rows_of(w):
            return w.rearrange("(k p) n -> p k n", p=P)

        w_in = rows_of(t["w_in"][0])
        w_br = rows_of(t["w_branch"][0].rearrange("b w n -> (b w) n"))
        w_out = rows_of(t["w_out"][0])
        w_up = rows_of(t["w_mlp_up"][0])
        w_dn = rows_of(t["w_mlp_down"][0])
        w_in2, w_out2, w_gate2, w_up2, w_dn2 = [
            rows_of(t[n][0]) for n in ("w_in_2", "w_out_2", "w_gate_2", "w_up_2", "w_down_2")]

        def load_unit(eng, group, j, w, kt, col, cols=NW):
            if not (isinstance(group, int) and group == 0):
                eng.wait_ge(lo_split, group * UN + j - RAW + 1)
            src = w[:, kt:kt + UK, col:col + cols] if isinstance(col, int) else w[:, kt:kt + UK, bass.ds(col, cols)]
            eng.dma_start(raw[:, j, :, 0:cols], src).then_inc(landed[j], 16)

        def hi_unit(eng, group, j, cols=NW):
            eng.wait_ge(landed[j], group * 16 + 16)
            if not (isinstance(group, int) and group == 0 and j < SPL):
                eng.wait_ge(units_used, group * UN + j - SPL + 1)
            eng.activation(whi[:, j % SPL, :, 0:cols], raw[:, j, :, 0:cols], ACT.Copy).then_inc(hi_split, 1)

        def lo_unit(eng, group, j, cols=NW):
            eng.wait_ge(hi_split, group * UN + j + 1)
            eng.tensor_tensor(wlo[:, j % SPL, :, 0:cols], raw[:, j, :, 0:cols],
                              whi[:, j % SPL, :, 0:cols].bitcast(F32), ALU.subtract).then_inc(lo_split, 1)

        def unit_products(eng, group, j, pair, hi, lo, kt, first, last, cols=NW):
            eng.wait_ge(lo_split, group * UN + j + 1)
            s = j % SPL
            for i in range(UK):
                for m in range(MT):
                    o = acc[:, pair, m, 0:cols]
                    a_hi = hi[:, kt + i, m * P:(m + 1) * P]
                    a_lo = lo[:, kt + i, m * P:(m + 1) * P]
                    eng.matmul(o, a_hi, whi[:, s, i, 0:cols], start=first and i == 0, stop=False)
                    eng.matmul(o, a_hi, wlo[:, s, i, 0:cols], start=False, stop=False)
                    mm = eng.matmul(o, a_lo, whi[:, s, i, 0:cols], start=False, stop=last and i == UK - 1)
            mm.then_inc(units_used, 1)

        def pair_free(eng, run, i=0, runs_a=0, runs_d=0):
            if run < 2:
                return
            who = READERS[run - 2]
            count = readers_before(run - 1, who)
            step = runs_a if who == "A" else runs_d
            eng.wait_ge(read_act if who == "A" else read_dve, count * MT + (i * (step * MT) if step else 0))

        def turn(eng, src, before):
            for m in range(MT):
                if not (isinstance(before, int) and before == 0):
                    eng.wait_ge(op_lo, before + m - 1)
                for c in range(CT):
                    tr = eng.transpose(tp[:, m, c * P:(c + 1) * P], src(m, c), ident[:, :])
                tr.then_inc(turned, 1)

        def turned_hi(eng, before, hi, kt):
            for m in range(MT):
                eng.wait_ge(turned, before + m + 1)
                eng.activation(hi[:, kt:kt + CT, m * P:(m + 1) * P],
                               tp[:, m].rearrange("p (c t) -> p c t", c=CT), ACT.Copy).then_inc(op_hi, 1)

        def turned_lo(eng, before, hi, lo, kt):
            for m in range(MT):
                eng.wait_ge(op_hi, before + m + 1)
                eng.tensor_tensor(lo[:, kt:kt + CT, m * P:(m + 1) * P],
                                  tp[:, m].rearrange("p (c t) -> p c t", c=CT),
                                  hi[:, kt:kt + CT, m * P:(m + 1) * P].bitcast(F32),
                                  ALU.subtract).then_inc(op_lo, 1)

        G_GATE0, G_LOOP, G_OUT, G_UP0, G_DLOOP, G_DLAST = 8, 13, 28, 32, 36, 60
        R_GATE0, R_LOOP, R_OUT, R_UP0, R_DLOOP, R_DLAST = 8, 16, 40, 44, 48, 72
        T_XN, T_YD, T_MERGED, T_XN2, T_HID, T_XN3 = 0, 8, 10, 18, 26, 58
        G_HEAD2, G_OUT2, G_PAIR0, G_LOOP2 = 64, 72, 76, 85
        R_HEAD2, R_OUT2, R_PAIR0, R_DOWN0, R_LOOP2 = 76, 84, 96, 102, 106
        T_XN4, T_HID2 = 66, 74
        LOOP2_RUNS, LOOP2_UNITS = 12, 12 * UN
        OUT2 = ([(k, n, k == K_CONV, k == K_WIN0) for n in range(UN) for k in (K_CONV, K_WIN0)]
                + [(k, n, True, True) for k in (K_WIN1, K_DIL) for n in range(UN)])

        TP0 = ["h0", "y0"] + [f"o{a}{m}" for a in (1, 2, 3) for m in range(MT)]
        TP1 = ["h1", "q10", "q11", "k1", "y1", "q20", "q21", "n0", "n1", "mix10", "q30", "mix11", "q31",
               "k30", "k31", "mix20", "mix21", "mix30", "mix31"]

        def tp_use(name):
            b = int(name in TP1)
            return b, (TP0, TP1)[b].index(name)

        A0 = [35, 20, 26, 34]

        class Attention:

            def __init__(self, set_, q, k, v, out, bufs, stats, masks, sinks=None):
                self.set, self.q, self.k, self.v, self.out = set_, q, k, v, out
                self.scores, self.probs, self.probsT = bufs
                self.negmax, self.rowsum, self.rinv = stats
                self.mask, self.sinks = masks, sinks
                self.first = set_ * len(GROUPS)
                self.cols = set_ * MT * HEADS

        def pair_of(x, h):
            return x[(h % 2) * HD:(h % 2 + 1) * HD, h // 2, :]

        attentions = [Attention(
            0, lambda h: qT[0:AUG, h, :], lambda h: kT[0:AUG, h, :], lambda h, kt: v_sb[:, kt, h * HD:(h + 1) * HD],
            lambda tile: tp[:, tile], (scores, probs, probsT), (negmax, rowsum, rinv), mask)]

        def windowed(a):
            return Attention(
                a, lambda h: pair_of(q2T[:, a - 1], h), lambda h: kwT[(h % 2) * HD:(h % 2 + 1) * HD, a - 1, :],
                lambda h, kt: kv_tok[:, kt, P + (a - 1) * HD:P + a * HD], lambda tile: tp[:, 0],
                (scores2, probs2, probsT2), [x[:, a - 1] for x in (negmax2, rowsum2, rinv2)], win_mask,
                (nsink[:, (a - 1) * HEADS:a * HEADS], sink_e[:, a - 1]))

        attentions += [windowed(1), windowed(2), Attention(
            3, lambda h: pair_of(q2T[:, 0], h), lambda h: pair_of(kdT, h),
            lambda h, kt: vd_sb[:, kt, h * HD:(h + 1) * HD], lambda tile: tp[:, 0],
            (scores2, probs2, probsT2), [x[:, 2] for x in (negmax2, rowsum2, rinv2)], dil_mask)]
        SINK_SETS = (1, 2)

        def same(x, width):
            return lambda m: [x[:, m, 0:width].rearrange("p (h d) -> p h d", d=HD)]

        NORMS2 = [(run, src, gain, same(src, W), W) for run, src, gain in (
            (HEAD2.index(I2_CQ0), q_tok[:, 0], B_CQG), (HEAD2.index(I2_CQ1), q_tok[:, 1], B_CQG),
            (HEAD2.index(I2_AQ), q_tok[:, 0], B_AQG), (HEAD2.index(I2_AK), k_tok[:, :, :], B_AKG))]
        NORMS2.insert(1, (HEAD2.index(I2_CKV), kv_tok[:, :, 0:P], B_CKG,
                          lambda m: [k_dup[:, m, :, d, :] for d in range(2)], P))
        GAINED2 = [MT, 3 * MT, 4 * MT, 5 * MT, 6 * MT]
        TURNS2 = {15: ("q10", 0, q_tok[:, 0], 0), 16: ("q11", 0, q_tok[:, 0], 1),
                  23: ("q20", 2, q_tok[:, 1], 0), 24: ("q21", 2, q_tok[:, 1], 1),
                  30: ("q30", 3, q_tok[:, 0], 0), 32: ("q31", 3, q_tok[:, 0], 1),
                  33: ("k30", 4, k_tok, 0), 34: ("k31", 4, k_tok, 1)}
        TURNED2 = {15: q2T[:, 0], 16: q2T[:, 0], 23: q2T[:, 1], 24: q2T[:, 1], 30: q2T[:, 0], 32: q2T[:, 0],
                   33: kdT, 34: kdT}
        MIX2 = {29: ("mix10", 1, 0), 31: ("mix11", 1, 1), 35: ("mix20", 2, 0), 37: ("mix21", 2, 1)}
        MIX_KT = {1: K_WIN0, 2: K_WIN1, 3: K_DIL}

        def sink_step(a, tile):
            return (a - 1) * MT + tile + 1

        def first_column(g):
            return sum(len(heads) for _, heads in GROUPS[:g])

        def head2_cols(col):
            return 2 * P if col == I2_CKV else NW

        def chunk(n, width=NW):
            return slice(n * width, (n + 1) * width) if isinstance(n, int) else bass.ds(n * width, width)

        def head_view(x):
            return x.rearrange("p (a b d) -> p b a d", b=2, d=HD)

        @block.sync
        def _(sp):
            for j in range(UN):
                sp.dma_start(xres[:, :, chunk(j)],
                             t["x"][0].rearrange("(m p) d -> p m d", p=P)[:, :, chunk(j)]).then_inc(x_in[j], 16)
            for r, col in enumerate(HEAD1):
                for j in range(UN):
                    load_unit(sp, r, j, w_in, UK * j, col)
            for k in range(NB):
                for j in range(UN):
                    load_unit(sp, G_GATE0 + k, j, w_in, UK * j, IN_GATE + k * D)
            for k in range(NB):
                load_unit(sp, G_GATE0 + NB, k, w_br, CT * k, 0)
            with sp.Fori(0, 3) as i:
                for k in range(NB):
                    for j in range(UN):
                        load_unit(sp, G_LOOP + k + i * 5, j, w_in, UK * j, i * NW + (IN_GATE + k * D + NW))
                for k in range(NB):
                    load_unit(sp, G_LOOP + NB + i * 5, k, w_br, CT * k, i * NW + NW)
            for n in range(UN):
                for j in range(UN):
                    load_unit(sp, G_OUT + n, j, w_out, UK * j, n * NW)
            for c in range(UN):
                for j in range(UN):
                    load_unit(sp, G_UP0 + c, j, w_up, UK * j, c * NW)

            def down_loads(g, q):
                for n in range(UN):
                    for j in range(UN):
                        load_unit(sp, g + n, j, w_dn[:, q * KT:(q + 1) * KT] if isinstance(q, int) else
                                  w_dn[:, bass.ds(q * KT, KT)], UK * j, n * NW)

            with sp.Fori(0, 3) as i:
                down_loads(G_DLOOP + i * 8, i)
                for c in range(UN):
                    for j in range(UN):
                        load_unit(sp, G_DLOOP + UN + c + i * 8, j, w_up, UK * j, i * D + (D + c * NW))
            down_loads(G_DLAST, 3)

            for r, col in enumerate(HEAD2):
                for j in range(UN):
                    load_unit(sp, G_HEAD2 + r, j, w_in2, UK * j, col, head2_cols(col))
            for u, (kt, n, _, _) in enumerate(OUT2):
                load_unit(sp, G_OUT2 + u // UN, u % UN, w_out2, kt, n * NW)

            def pair_loads(g, col):
                for w in (w_gate2, w_up2):
                    for j in range(UN):
                        load_unit(sp, g, j, w, UK * j, col)
                    g = g + 1

            for c in range(CH2_FIRST):
                pair_loads(G_PAIR0 + 2 * c, c * NW)
            for n in range(UN):
                for k in range(CH2_FIRST):
                    u = n * CH2_FIRST + k
                    load_unit(sp, G_PAIR0 + 2 * CH2_FIRST + u // UN, u % UN, w_dn2, UK * k, n * NW)
            with sp.Fori(0, 2) as i:
                for c in range(CH2_LOOP):
                    pair_loads(i * LOOP2_RUNS + (G_LOOP2 + 2 * c), i * (CH2_LOOP * NW) + (CH2_FIRST + c) * NW)
                for n in range(UN):
                    for j in range(UN):
                        rows = w_dn2[:, bass.ds(i * (CH2_LOOP * CT) + CH2_FIRST * CT, CH2_LOOP * CT)]
                        load_unit(sp, i * LOOP2_RUNS + (G_LOOP2 + 2 * CH2_LOOP + n), j, rows, UK * j, n * NW)

            sp.wait_ge(read_dve, READERS.count("D") * MT)
            sp.dma_start(out[0].rearrange("(m p) d -> p m d", p=P), xres[:, :, :]).then_inc(stored, 16)
            sp.wait_ge(stored, 16)

        @block.gpsimd
        def _(pool):
            own = Chain(pool, pc)
            n0 = own.mark(pool.memset(ident[:, :], 0.0))
            pool.memset(ones[:, :], 1.0).then_inc(consts, 1)
            n1 = own.mark(pool.memset(tri[:, :], 1.0))
            n2 = own.mark(pool.memset(mask[:, :], 0.0))
            own.need(n0)
            pool.affine_select(out=ident[:, :], in_=ident[:, :], compare_op=ALU.not_equal, fill=1.0, base=0,
                               pattern=[[-1, P]], channel_multiplier=1).then_inc(consts, 1)
            own.need(n1)
            pool.affine_select(out=tri[:, :], in_=tri[:, :], compare_op=ALU.is_ge, fill=0.0, base=0,
                               pattern=[[1, P]], channel_multiplier=-1).then_inc(consts, 1)
            own.need(n2)
            pool.affine_select(out=mask[:, P:T], in_=mask[:, P:T], compare_op=ALU.is_ge, fill=NEG, base=0,
                               pattern=[[-1, P]], channel_multiplier=1).then_inc(consts, 1)
            pool.memset(wr_sb[:, :, :], 0.0).then_inc(pads, 1)
            pool.memset(wi_sb[:, :, :], 0.0).then_inc(pads, 1)
            pool.memset(xaT[:, :, 0:LP], 0.0).then_inc(pads, 1)
            pool.memset(xpT[:, :, 0:PP], 0.0).then_inc(pads, 1)
            pool.memset(zT[:, :, 0:SP_], 0.0).then_inc(pads, 1)
            pool.memset(q_aug[:, :, HD + 1:AUG], 1.0).then_inc(pads, 1)
            pool.memset(k_aug[:, :, HD:HD + 1], 1.0).then_inc(pads, 1)
            pool.iota(steps[:, :], pattern=[[1, 16]], base=1, channel_multiplier=0).then_inc(pads, 1)

            pool.wait_ge(side_read, 4)
            pool.wait_ge(u_ready, CT)
            pool.wait_ge(rc_ready, 1)
            for g in range(CT):
                src, dst, width = xpT[:, g, :], pool_a, 1
                while width < 2 << g:
                    lo = 2 * width - 1
                    own.done(pool.tensor_tensor(dst[:, lo:], src[:, lo:], src[:, lo - width:PP + T - width], ALU.add))
                    src, dst, width = dst[:, :], (pool_b if dst is pool_a else pool_a), 2 * width
                head = own.mark(pool.tensor_tensor(dst[:, PP:PP + 16], src[:, PP:PP + 16], recip_count[:, g, :], ALU.mult))
                own.need(head)
                own.done(pool.tensor_scalar(dst[:, PP + 16:], src[:, PP + 16:], 1.0 / (2 << g), 1.0, ALU.mult, ALU.mult))
                pool.tensor_tensor(xpT[:, g, PP:], dst[:, PP:], xpT[:, g, PP:], ALU.subtract).then_inc(pooled, 1)
                pool.wait_ge(pooled, g + 1)

            pool.wait_ge(a_ready, CT)
            own.done(pool.tensor_tensor(lru_om[:, :, :], lru_r[:, :, :], lru_r[:, :, :], ALU.mult))
            pool.tensor_scalar(lru_om[:, :, :], lru_om[:, :, :], -1.0, 1.0, ALU.mult, ALU.add).then_inc(asq_ready, 1)
            pool.wait_ge(g_ready, CT)
            pool.tensor_tensor(lru_g[:, :, :], lru_g[:, :, :], lru_u[:, :, :], ALU.mult).then_inc(gu_ready, 1)

            def head_squares(before):
                pool.wait_ge(read_act, readers_before(HEAD1.index(IN_Q) + before + 1, "A") * MT)
                pool.tensor_tensor(lru_om[:, :, :].rearrange("p c t -> p (c t)"),
                                   stage[:, :, :].rearrange("p m n -> p (m n)"),
                                   stage[:, :, :].rearrange("p m n -> p (m n)"), ALU.mult).then_inc(head_sq, 1)

            pool.wait_ge(h_ready, CT)
            head_squares(0)
            pool.wait_ge(sc_ready, CT)
            pool.wait_ge(side_read, 8)
            pool.tensor_tensor(lru_z[:, :, :], lru_z[:, :, :], gbT[:, :, :], ALU.mult).then_inc(sc_gated, 1)
            pool.wait_ge(head_sum, 1)
            head_squares(1)

            def merge(n):
                for k in range(1, NB):
                    run = R_GATE0 + n * 2 * NB + NB + k
                    pool.wait_ge(read_dve, readers_before(run + 1, "D") * MT)
                    if k > 1:
                        pool.wait_ge(merged_ready, n * (NB - 1) + k - 1)
                    pool.tensor_tensor(xres[:, :, chunk(n)], xres[:, :, chunk(n)], stage[:, :, :],
                                       ALU.add).then_inc(merged_ready, 1)

            for n in range(UN):
                merge(n)

            def gained(run, n, gain=gainB):
                pool.wait_ge(read_dve, readers_before(run + 1, "D") * MT)
                for m in range(MT):
                    pool.tensor_tensor(stage[:, m, :], xres[:, m, chunk(n)], gain[:, chunk(n)],
                                       ALU.mult).then_inc(staged, 1)

            def squares(run, i=0):
                for m in range(MT):
                    pool.wait_ge(read_act, i * (UN * MT) + readers_before(run, "A") * MT + m + 1)
                    pool.tensor_tensor(stage[:, m, :], stage[:, m, :], stage[:, m, :], ALU.mult).then_inc(staged, 1)

            pool.wait_ge(gain_in[1], 16)
            for n in range(UN):
                gained(R_OUT + n, n)
            for c in range(UN):
                squares(R_UP0 + c)
            with pool.Fori(0, 3) as i:
                for c in range(UN):
                    squares(R_DLOOP + UN + c, i)

            pool.wait_ge(gain_in[2], 16)
            for n in range(UN):
                gained(R_DLAST + n, n)

            pool.memset(hT[:, :, 0:CP], 0.0).then_inc(pads2, 1)
            n0 = own.mark(pool.memset(win_mask[:, :], 0.0))
            pool.iota(dist[:, 0, :], pattern=[[-1, P]], base=NW, channel_multiplier=1).then_inc(masks_raw, 1)
            pool.iota(dist[:, 1, :], pattern=[[-1, P]], base=NW, channel_multiplier=1).then_inc(masks_raw, 1)
            own.need(n0)
            pool.affine_select(out=win_mask[:, 0:P], in_=win_mask[:, 0:P], compare_op=ALU.is_ge, fill=NEG, base=-1,
                               pattern=[[1, P]], channel_multiplier=-1).then_inc(masks_ready, 1)
            pool.affine_select(out=win_mask[:, P:T], in_=win_mask[:, P:T], compare_op=ALU.is_ge, fill=NEG, base=0,
                               pattern=[[-1, P]], channel_multiplier=1).then_inc(masks_ready, 1)
            pool.wait_ge(mults_ready, 2)
            pool.affine_select(out=dil_mask[:, P:T], in_=near[:, :], compare_op=ALU.is_ge, fill=NEG, base=0,
                               pattern=[[-1, P]], channel_multiplier=1).then_inc(masks_ready, 1)
            pool.wait_ge(masks_ready, 3)
            pool.affine_select(out=near[:, :], in_=near[:, :], compare_op=ALU.is_ge, fill=0.0, base=0,
                               pattern=[[1, P]], channel_multiplier=-1).then_inc(masks_ready, 1)
            pool.affine_select(out=far[:, :], in_=far[:, :], compare_op=ALU.is_ge, fill=0.0, base=-1,
                               pattern=[[-1, P]], channel_multiplier=1).then_inc(masks_ready, 1)
            pool.wait_ge(masks_ready, 5)
            pool.tensor_tensor(dil_mask[:, 0:P], near[:, :], far[:, :], ALU.add).then_inc(masks_ready, 1)

            def head2_squares(n):
                run, src, _, _, width = NORMS2[n]
                pool.wait_ge(read_act, readers_before(R_HEAD2 + run + 1, "A") * MT)
                if n:
                    pool.wait_ge(h2_sum, n)
                pool.tensor_tensor(squares2[:, :, 0:width], src, src, ALU.mult).then_inc(h2_sq, 1)

            def head2_gain(n):
                _, src, gain, dst, width = NORMS2[n]
                pool.wait_ge(h2_scaled, n + 1)
                g = bcast[:, gain:gain + HD].unsqueeze(1).to_broadcast([P, width // HD, HD])
                for m in range(MT):
                    x = src[:, m, :].rearrange("p (h d) -> p h d", d=HD)
                    for o in dst(m):
                        pool.tensor_tensor(o, x, g, ALU.mult).then_inc(h2_gained, 1)

            pool.wait_ge(read_act, readers_before(R_HEAD2 + 2, "A") * MT)
            pool.tensor_tensor(stage[:, :, :], u_sb[:, :, :], sig_sb[:, :, :], ALU.mult).then_inc(glu_ready, 1)
            pool.wait_ge(tp_free[0], 1)
            pool.wait_ge(tp_free[1], 1)
            pool.wait_ge(pads2, 1)
            marks, tmp_marks = {}, {}

            def pool_taps(k0, k1):
                for k in range(k0, k1):
                    for c in (2, 3):
                        if k == 0:
                            marks[c] = own.mark(pool.tensor_scalar(
                                yT[:, c, :], hT[:, c, 0:T], par[:, c, R_CONV2:R_CONV2 + 1],
                                par[:, c, R_CONV2B:R_CONV2B + 1], ALU.mult, ALU.add))
                        else:
                            tmp_marks[c] = own.mark(pool.tensor_scalar(
                                tap_tmp[:, c - 2, :], hT[:, c, k:k + T], par[:, c, R_CONV2 + k:R_CONV2 + k + 1], 1.0,
                                ALU.mult, ALU.mult))
                    if k:
                        for c in (2, 3):
                            own.need(tmp_marks[c])
                            own.need(marks[c])
                            add = pool.tensor_tensor(yT[:, c, :], yT[:, c, :], tap_tmp[:, c - 2, :], ALU.add)
                            if k == CONV_TAPS - 1:
                                add.then_inc(conv_pool, 1)
                            else:
                                marks[c] = own.mark(add)
                                own.need(marks[c])

            pool_taps(0, 6)
            head2_squares(0)
            pool_taps(6, 14)
            head2_gain(0)
            head2_squares(1)
            pool_taps(14, 22)
            head2_gain(1)
            head2_squares(2)
            pool_taps(22, CONV_TAPS)
            head2_gain(2)
            head2_squares(3)
            head2_gain(3)
            head2_squares(4)
            head2_gain(4)

            pool.wait_ge(gain_in[3], 16)
            for n in range(UN):
                if n:
                    pool.wait_ge(turned, T_XN4 + n * MT)
                gained(R_OUT2 + 2 * UN + n, n, gain2)

        @block.scalar
        def _(act):
            own = Chain(act, ac)

            def evac(run, out, func=ACT.Copy, done=None, cols=NW):
                act.wait_ge(units_used, UN * (run + 1) if done is None else done)
                for m in range(MT):
                    act.activation(out(m), acc[:, run % 2, m, 0:cols], func, scale=rstd[:, m:m + 1]).then_inc(read_act, 1)

            def relu_evac(run, done):
                evac(run, lambda m: stage[:, m, :], ACT.Relu, done)

            def side_copy(n, out):
                act.wait_ge(side_turned, n + 1)
                rows = out.shape[0]
                act.activation(out, tp[0:rows, n % 2].rearrange("p (c t) -> p c t", c=CT), ACT.Copy).then_inc(side_read, 1)

            def channel_copy(n, dst, pad):
                for m in range(MT):
                    side_copy(n + m, dst[:, :, pad + m * P:pad + (m + 1) * P])

            def norm_squares(norm, n):
                if norm or n:
                    act.wait_ge(sq_done, (norm * UN + n) * MT)
                for m in range(MT):
                    act.activation(junk[:, m, :], xres[:, m, chunk(n)], ACT.Square,
                                   accum_out=sumsq[:, m, n:n + 1]).then_inc(sq_done, 1)

            def norm_root(norm):
                act.wait_ge(msq_done, norm + 1)
                act.activation(rms[:, :], msq[:, :], ACT.Sqrt).then_inc(rms_done, 1)

            def head_root_of(n):
                act.wait_ge(head_sum, n + 1)
                act.activation(hroot[:, :], hsum[:, :], ACT.Sqrt).then_inc(head_root, 1)

            def exps(a, g):
                tile, heads = GROUPS[g]
                width = (tile + 1) * P
                act.wait_ge(max_ready, a.first + g + 1)
                if a.first + g >= 2:
                    act.wait_ge(p_turned, a.first + g - 1)
                for i, h in enumerate(heads):
                    c = first_column(g) + i
                    act.activation(a.probs[:, g % 2, i * width:(i + 1) * width], a.scores[:, i * width:(i + 1) * width],
                                   ACT.Exp, bias=a.negmax[:, c:c + 1], accum_out=a.rowsum[:, c:c + 1]).then_inc(p_ready, 1)

            def copy_probsT(a, g):
                act.wait_ge(p_turned, a.first + g + 1)
                if a.first + g:
                    act.wait_ge(pv_done, a.first + g)
                act.activation(a.probsT[:, :], sd[:, 1, :], ACT.Copy).then_inc(pT_ready, 1)

            def attention_side(a, s):
                s = s - A0[a.set]
                if 2 <= s < 2 + len(GROUPS):
                    exps(a, s - 2)
                if 4 <= s < 4 + len(GROUPS):
                    copy_probsT(a, s - 4)
                if a.sinks and s in (5, 9):
                    tile = int(s == 9)
                    act.wait_ge(sink_arg, sink_step(a.set, tile))
                    e = a.sinks[1][:, tile * HEADS:(tile + 1) * HEADS]
                    act.activation(e, e, ACT.Exp).then_inc(sink_exp, 1)

            act.dma_start(gainB[:, :], t["norm_mix_g"][0].partition_broadcast(P)).then_inc(gain_in[0], 16)
            for j in range(UN):
                act.wait_ge(x_in[j], 16)
                norm_squares(0, j)
            for j in range(UN):
                if j == 0:
                    act.dma_start(rows_par[R_CONV:R_CONVB, :], t["lru_conv_w"][0]).then_inc(rows_in, 16)
                    for r, name in ((R_CONVB, "lru_conv_b"), (R_BR, "lru_br"), (R_BI, "lru_bi"),
                                    (R_LAM, "lru_lambda"), (R_PSCALE, "pool_scale")):
                        act.dma_start(rows_par[r:r + 1, :], t[name]).then_inc(rows_in, 16)
                    act.dma_start(rows_par[R_SC:R_CONV2, :], t["sconv_w"][0]).then_inc(rows_in, 16)
                    act.dma_start(rows_par[R_CONV2:R_CONV2B, :], t["conv_w_2"][0]).then_inc(rows_in, 16)
                    for r, name in ((R_CONV2B, "conv_b_2"), (R_LNG, "conv_ln_g_2"), (R_LNB, "conv_ln_b_2")):
                        act.dma_start(rows_par[r:r + 1, :], t[name]).then_inc(rows_in, 16)
                if j == 1:
                    act.dma_start(f_raw[:, :, :], w_in[:, :, IN_F:IN_GATE]).then_inc(f_in, 16)
                    for c, name in ((B_QG, "q_norm_g"), (B_KG, "k_norm_g"), (B_AQG, "a_q_g_2"), (B_AKG, "a_k_g_2"),
                                    (B_CQG, "c_q_g_2"), (B_CKG, "c_k_g_2"), (B_FB, "forget_b"), (B_SINK, "c_sinks_2")):
                        n = t[name].shape[1]
                        act.dma_start(bcast[:, c:c + n], t[name][0].partition_broadcast(P)).then_inc(bc_in, 16)
                if j == 2:
                    act.wait_ge(pads, 2)
                    for dst, name in ((wr_sb, "lru_wr"), (wi_sb, "lru_wi")):
                        for b in range(2):
                            act.dma_start(dst[b * HD:(b + 1) * HD, :, b * HD:(b + 1) * HD],
                                          t[name][0, b::2].rearrange("h i j -> i h j")).then_inc(sw_in, 16)
                    act.dma_start(pw_sb[:, :, :], t["pool_w"][0].rearrange("g i j -> i g j")).then_inc(sw_in, 16)
                if j == 3:
                    norm_root(0)
                turned_hi_bank = T_XN + j * MT
                turned_hi(act, turned_hi_bank, opA_hi, j * CT)
                hi_unit(act, 0, j) if j < SPL else None
            for j in range(SPL, UN):
                hi_unit(act, 0, j)

            def side(s):
                if s == 3:
                    act.wait_ge(f_in, 16)
                    act.activation(f_hi[:, :, :], f_raw[:, :, :], ACT.Copy).then_inc(f_split, 1)
                if s == 4:
                    act.wait_ge(rstd_done, 1)
                    evac(0, lambda m: stage[:, m, :])
                    act.wait_ge(par_turned, 1)
                    act.activation(par[:, :, :], sd[:, 0, 0:CT * NPAR].rearrange("p (c r) -> p c r", c=CT),
                                   ACT.Copy).then_inc(par_ready, 1)
                if s == 6:
                    act.wait_ge(f_mm, 1)
                    for m in range(MT):
                        act.activation(ftok[:, m * HEADS:(m + 1) * HEADS], sd[:, 1, m * HEADS:(m + 1) * HEADS],
                                       ACT.Copy, scale=rstd[:, m:m + 1]).then_inc(f_tok, 1)
                    channel_copy(0, xaT, LP)
                if s == 8:
                    evac(1, lambda m: stage[:, m, :])
                    act.wait_ge(f_abs, 1)
                    act.activation(sp_e[:, :], sp_abs[:, :], ACT.Exp, scale=-1.0).then_inc(f_exp, 1)
                    act.wait_ge(lam_abs, 1)
                    act.activation(l_e[:, :], l_abs[:, :], ACT.Exp, scale=-1.0).then_inc(lam_exp, 1)
                if s == 10:
                    channel_copy(2, xpT, PP)
                if s == 12:
                    evac(2, lambda m: gc_sb[:, m, :])
                if s == 13:
                    act.wait_ge(lru_mm, 1)
                    for c in range(CT):
                        act.activation(lru_r[:, c, :], sd[:, c // 2, (c % 2) * T:(c % 2 + 1) * T], ACT.Sigmoid,
                                       bias=par[:, c, R_BR:R_BR + 1]).then_inc(r_ready, 1)
                if s == 16:
                    act.wait_ge(lru_mm, 2)
                    for c in range(CT):
                        act.activation(lru_g[:, c, :], sd[:, c // 2, (c % 2) * T:(c % 2 + 1) * T], ACT.Sigmoid,
                                       bias=par[:, c, R_BI:R_BI + 1]).then_inc(g_ready, 1)
                if s == 17:
                    act.wait_ge(z_ready, CT)
                    for c in range(CT):
                        act.activation(lru_r[:, c, :], lru_r[:, c, :], ACT.Exp, scale=l_c[:, c:c + 1]).then_inc(a_ready, 1)
                if s == 18:
                    channel_copy(4, zT, SP_)
                if s == 20:
                    evac(4, lambda m: stage[:, m, :])
                if s == 22:
                    act.wait_ge(om_ready, 1)
                    act.activation(lru_om[:, :, :], lru_om[:, :, :], ACT.Sqrt).then_inc(root_ready, 1)
                    channel_copy(6, gbT, 0)
                if s == 24:
                    evac(5, lambda m: stage[:, m, :])
                if s == 25:
                    act.wait_ge(h_ready, CT)
                    act.activation(opB_hi[:, 0:CT, :], lru_u[:, :, :], ACT.Copy).then_inc(y_hi, 1)
                if s == 26:
                    head_root_of(0)
                    act.wait_ge(pool_mm, 1)
                    for c in range(CT):
                        act.activation(opB_hi[:, CT + c, :], sd[:, c // 2, (c % 2) * T:(c % 2 + 1) * T], ACT.Copy,
                                       scale=par[:, c, R_PSCALE:R_PSCALE + 1]).then_inc(y_hi, 1)
                if s == 28:
                    act.wait_ge(head_scaled, 1)
                    evac(6, lambda m: stage[:, m, :])
                if s == 30:
                    head_root_of(1)
                if s == 31:
                    act.wait_ge(sc_gated, 1)
                    act.activation(opB_hi[:, 2 * CT:3 * CT, :], lru_z[:, :, :], ACT.Copy).then_inc(y_hi, 1)
                if s == 32:
                    evac(7, lambda m: v_sb[:, m, :])
                if s in (33, 34):
                    if s == 33:
                        act.wait_ge(y_lo, 6)
                    m = s - 33
                    for half in range(2):
                        side_copy(8 + 2 * m + half, qT[0:AUG, half * CT:(half + 1) * CT, m * P:(m + 1) * P])
                if s in (35, 36):
                    m = s - 35
                    for half in range(2):
                        side_copy(12 + 2 * m + half, kT[0:AUG, half * CT:(half + 1) * CT, m * P:(m + 1) * P])
                if s == 36:
                    evac(8, lambda m: gates[:, 0, m, :], ACT.Sigmoid)
                if s in (40, 44):
                    k = (s - 36) // 4
                    evac(R_GATE0 + k, lambda m: gates[:, k, m, :], ACT.Sigmoid)
                attention_side(attentions[0], s)
                if s == 48:
                    evac(R_GATE0 + 3, lambda m: gates[:, 3, m, :], ACT.Sigmoid)
                    turned_hi(act, T_YD, opB_hi, 3 * CT)

            side(3)
            for g in range(1, G_LOOP):
                for j in range(UN):
                    hi_unit(act, g, j)
                    side(g * UN + j)
            with act.Fori(0, 3) as i:
                for k in range(NB + 1):
                    for j in range(UN):
                        hi_unit(act, G_LOOP + k + i * 5, j)
                        if k and j == 0:
                            evac(R_LOOP + k - 1, lambda m: gates[:, k - 1, m, :], ACT.Sigmoid,
                                 done=i * (5 * UN) + (G_LOOP + k) * UN)
            for n in range(UN):
                for j in range(UN):
                    if n == 0:
                        turned_hi(act, T_MERGED + j * MT, opA_hi, j * CT)
                        act.dma_start(xres[:, :, chunk(j)],
                                      t["x"][0].rearrange("(m p) d -> p m d", p=P)[:, :, chunk(j)]).then_inc(x_back[j], 16)
                        if j == 0:
                            act.dma_start(gainB[:, :], t["norm_mlp_g"][0].partition_broadcast(P)).then_inc(gain_in[1], 16)
                    hi_unit(act, G_OUT + n, j)
                    if n and j == 0:
                        act.wait_ge(read_dve, readers_before(R_OUT + n, "D") * MT)
                        norm_squares(1, n - 1)
                    if n and j == 2:
                        turned_hi(act, T_XN2 + (n - 1) * MT, opB_hi, (n - 1) * CT)

            for c in range(UN):
                for j in range(UN):
                    hi_unit(act, G_UP0 + c, j)
                    if j == 0 and c == 0:
                        act.wait_ge(read_dve, readers_before(R_UP0, "D") * MT)
                        norm_squares(1, 3)
                        norm_root(1)
                    if j == 0 and c == 1:
                        act.wait_ge(rstd_done, 2)
                    if j == 0 and c:
                        relu_evac(R_UP0 + c - 1, (G_UP0 + c) * UN)
                    if j == 3 and c == 1:
                        act.wait_ge(staged, 4 * MT)
                        act.dma_start(gainB[:, :], t["norm1_g_2"][0].partition_broadcast(P)).then_inc(gain_in[2], 16)
                    if j == 2 and c == 0:
                        turned_hi(act, T_XN2 + 3 * MT, opB_hi, 3 * CT)
                    if j == 2 and c:
                        turned_hi(act, T_HID + (c - 1) * MT, opA_hi, (c - 1) * CT)
            with act.Fori(0, 3) as i:
                for r in range(2 * UN):
                    g = i * 8 + (G_DLOOP + r)
                    for j in range(UN):
                        hi_unit(act, g, j)
                        up = UN - 1 if r == 0 else r - UN - 1
                        if up >= 0 and j == 0:
                            relu_evac(R_DLOOP + r - 1, i * (8 * UN) + (G_DLOOP + r) * UN)
                        if up >= 0 and j == 2:
                            before = T_HID + (up if r == 0 else UN + up) * MT
                            turned_hi(act, i * (UN * MT) + before, opA_hi, up * CT)
            for n in range(UN):
                for j in range(UN):
                    hi_unit(act, G_DLAST + n, j)
                    if n == 0 and j == 0:
                        relu_evac(R_DLAST - 1, G_DLAST * UN)
                    if n == 0 and j == 2:
                        turned_hi(act, T_HID + (4 * UN - 1) * MT, opA_hi, 3 * CT)
                    if n and j == 0:
                        act.wait_ge(read_dve, readers_before(R_DLAST + n, "D") * MT)
                        norm_squares(2, n - 1)
                    if n and j == 2:
                        turned_hi(act, T_XN3 + (n - 1) * MT, opB_hi, (n - 1) * CT)

            def evac2(r, out, func=ACT.Copy):
                evac(R_HEAD2 + r, out, func, (G_HEAD2 + r + 1) * UN, head2_cols(HEAD2[r]))

            def tp_copy(name, out, func=ACT.Copy):
                b, n = tp_use(name)
                act.wait_ge(tp_full[b], n + 1)
                act.activation(out, tp[:, b].rearrange("p (c t) -> p c t", c=CT), func).then_inc(tp_free[b], 1)

            def mix_turned_hi(name, a, m):
                b, n = tp_use(name)
                act.wait_ge(tp_full[b], n + 1)
                kt = MIX_KT[a]
                act.activation(opA_hi[:, kt:kt + CT, m * P:(m + 1) * P], tp[:, b].rearrange("p (c t) -> p c t", c=CT),
                               ACT.Copy).then_inc(mix_hi, 1)

            EVAC2 = [lambda m: u_sb[:, m, :], lambda m: sig_sb[:, m, :], lambda m: q_tok[:, 0, m, :],
                     lambda m: kv_tok[:, m, :], lambda m: q_tok[:, 1, m, :], lambda m: q_tok[:, 0, m, :],
                     lambda m: k_tok[:, m, :], lambda m: vd_sb[:, m, :]]

            def side2(s):
                if s == 0:
                    act.wait_ge(read_dve, readers_before(R_HEAD2, "D") * MT)
                    norm_squares(2, 3)
                    norm_root(2)
                if s == 2:
                    turned_hi(act, T_XN3 + 3 * MT, opB_hi, 3 * CT)
                if s % UN == 0 and 0 < s <= 8 * UN:
                    r = s // UN - 1
                    if r == 0:
                        act.wait_ge(rstd_done, 3)
                    if r == 1:
                        act.wait_ge(sq_done, 3 * UN * MT)
                    evac2(r, EVAC2[r], ACT.Sigmoid if r == 1 else ACT.Copy)
                if s == 10:
                    tp_copy("h0", hT[:, :, CP:CP + P])
                    tp_copy("h1", hT[:, :, CP + P:CP + T])
                if s in (14, 18, 22, 26, 30):
                    n = (s - 14) // 4
                    act.wait_ge(h2_sum, n + 1)
                    act.activation(hroot[:, :], hsum[:, :], ACT.Sqrt).then_inc(h2_root, 1)
                if s - 2 in TURNS2:
                    name, _, _, m = TURNS2[s - 2]
                    tp_copy(name, TURNED2[s - 2][:, :, m * P:(m + 1) * P])
                if s == 21:
                    tp_copy("k1", kwT[:, :, :].rearrange("p v (m t) -> p v m t", m=MT).rearrange("p v m t -> p (v m) t"))
                if s == 23:
                    tp_copy("y0", y_tok[:, 0, :].rearrange("p (c t) -> p c t", c=CT))
                    tp_copy("y1", y_tok[:, 1, :].rearrange("p (c t) -> p c t", c=CT))
                if s == 25:
                    act.wait_ge(ln_var, 1)
                    act.activation(bn_root[:, :], bn_var[:, :], ACT.Sqrt).then_inc(ln_root, 1)
                if s in (29, 30):
                    tp_copy(f"n{s - 29}", silT[:, :, (s - 29) * P:(s - 28) * P])
                if s == 30:
                    b, n = tp_use("n1")
                    act.wait_ge(tp_free[b], n + 1)
                    for c in range(CT):
                        act.activation(silT[:, c, :], silT[:, c, :], ACT.Silu, bias=par[:, c, R_LNB:R_LNB + 1],
                                       scale=par[:, c, R_LNG:R_LNG + 1]).then_inc(silu_done, 1)
                    act.wait_ge(silu_done, CT)
                if s == 31:
                    act.activation(opA_hi[:, K_CONV:K_CONV + CT, :], silT[:, :, :], ACT.Copy).then_inc(conf_hi, 1)
                if s == 34:
                    act.wait_ge(conf_lo, 1)
                    act.dma_start(gain2[:, :], t["norm2_g_2"][0].partition_broadcast(P)).then_inc(gain_in[3], 16)
                if s - 2 in MIX2:
                    mix_turned_hi(*MIX2[s - 2])
                for a in attentions[1:]:
                    attention_side(a, s)
                if s == 45:
                    for m in range(MT):
                        mix_turned_hi(f"mix3{m}", 3, m)
                if 46 <= s <= 49:
                    n = s - 46
                    act.wait_ge(read_dve, readers_before(R_OUT2 + 2 * UN + n + 1, "D") * MT)
                    norm_squares(3, n)
                if 47 <= s <= 50:
                    turned_hi(act, T_XN4 + (s - 47) * MT, opB_hi, (s - 47) * CT)
                if s == 50:
                    norm_root(3)

            for u in range(12 * UN):
                hi_unit(act, G_HEAD2 + u // UN, u % UN, head2_cols(HEAD2[u // UN]) if u < 8 * UN else NW)
                side2(u)

            def gate_evac(run, done, i=0):
                act.wait_ge(read_dve, i * (2 * CH2_LOOP * MT) + readers_before(run, "D") * MT)
                evac(run, lambda m: silu_gate[:, m, :], ACT.Silu, done)

            for r in range(2 * CH2_FIRST):
                for j in range(UN):
                    hi_unit(act, G_PAIR0 + r, j)
                    if r == 0:
                        side2(12 * UN + j)
                    if r == 1 and j == 0:
                        act.wait_ge(rstd_done, 4)
                    if r % 2 and j == 0:
                        gate_evac(R_PAIR0 + r - 1, (G_PAIR0 + r) * UN)
                    if r and r % 2 == 0 and j == 2:
                        turned_hi(act, T_HID2 + (r // 2 - 1) * MT, opA_hi, (r // 2 - 1) * CT)
            for u in range(CH2_FIRST * UN):
                hi_unit(act, G_PAIR0 + 2 * CH2_FIRST + u // UN, u % UN)
                if u == 2:
                    turned_hi(act, T_HID2 + (CH2_FIRST - 1) * MT, opA_hi, (CH2_FIRST - 1) * CT)
            with act.Fori(0, 2) as i:
                for r in range(LOOP2_RUNS):
                    for j in range(UN):
                        hi_unit(act, i * LOOP2_RUNS + (G_LOOP2 + r), j)
                        c = r // 2
                        if r % 2 and c < CH2_LOOP and j == 0:
                            gate_evac(R_LOOP2 + r - 1, i * LOOP2_UNITS + (G_LOOP2 + r) * UN, i)
                        if r % 2 == 0 and 1 <= c <= CH2_LOOP and j == 2:
                            before = T_HID2 + (CH2_FIRST + c - 1) * MT
                            turned_hi(act, i * (CH2_LOOP * MT) + before, opA_hi, (c - 1) * CT)

        @block.tensor
        def _(pe):
            def products(group, run, j, hi, lo, kt, pair_wait=None, first=None, last=None, free=None):
                first = j == 0 if first is None else first
                last = j == UN - 1 if last is None else last
                if first:
                    free() if free else pair_free(pe, run)
                unit_products(pe, group, j, run % 2, hi, lo, kt, first, last)

            def stage_operand(c, before, staged_by):
                pe.wait_ge(staged, staged_by)
                turn(pe, lambda m, b: stage[:, m, b * P:(b + 1) * P], before)

            def side_turn(n, blocks):
                if n < 2:
                    pe.wait_ge(op_lo, T_YD)
                else:
                    pe.wait_ge(side_read, n - 1)
                for c, b in enumerate(blocks):
                    w = b.shape[1]
                    tr = pe.transpose(tp[0:w, n % 2, c * P:(c + 1) * P], b, ident[:, :])
                tr.then_inc(side_turned, 1)

            def stage_turn(n):
                for m in range(MT):
                    side_turn(n + m, [stage[:, m, c * P:(c + 1) * P] for c in range(CT)])

            def aug_turn(n, aug, m):
                for half in range(2):
                    side_turn(n + half, [aug[:, m * HEADS + half * CT + c, :] for c in range(CT)])

            def lru_products(w):
                for c in range(CT):
                    mm = pe.matmul(sd[:, c // 2, (c % 2) * T:(c % 2 + 1) * T], w[:, c, :], lru_u[:, c, :],
                                   start=True, stop=True)
                mm.then_inc(lru_mm, 1)

            def qk(a, g):
                tile, heads = GROUPS[g]
                width = (tile + 1) * P
                if a.first + g:
                    pe.wait_ge(s_ready, a.first + g)
                for i, h in enumerate(heads):
                    mm = pe.matmul(sd[:, 0, i * width:(i + 1) * width], a.q(h)[:, tile * P:(tile + 1) * P],
                                   a.k(h)[:, 0:width], start=True, stop=True)
                mm.then_inc(qk_done, 1)

            def turn_probs(a, g):
                pe.wait_ge(p_ready, a.cols + first_column(g) + len(GROUPS[g][1]))
                if a.first + g:
                    pe.wait_ge(pT_ready, a.first + g)
                for b in range(CT):
                    tr = pe.transpose(sd[:, 1, b * P:(b + 1) * P], a.probs[:, g % 2, b * P:(b + 1) * P], ident[:, :])
                tr.then_inc(p_turned, 1)

            def pv(a, g):
                tile = GROUPS[g][0]
                pe.wait_ge(pT_ready, a.first + g + 1)
                for b, (h, kt) in enumerate(blocks_of(GROUPS[g])):
                    mm = pe.matmul(a.out(tile)[:, h * HD:(h + 1) * HD], a.probsT[:, b * P:(b + 1) * P],
                                   a.v(h, kt), start=kt == 0, stop=kt == tile)
                mm.then_inc(pv_done, 1)

            def attention_side(a, s, qk_wait, pv_wait):
                s = s - A0[a.set]
                if 0 <= s < len(GROUPS):
                    qk_wait(GROUPS[s][0])
                    qk(a, s)
                if 4 <= s < 4 + len(GROUPS):
                    pv_wait(s - 4)
                    pv(a, s - 4)
                if 2 <= s < 2 + len(GROUPS):
                    turn_probs(a, s - 2)

            def side(s):
                if s == 2:
                    pe.wait_ge(rows_in, 11 * 16)
                    for c in range(CT):
                        tr = pe.transpose(sd[:, 0, c * NPAR:(c + 1) * NPAR], rows_par[0:NPAR, c * P:(c + 1) * P],
                                          ident[0:NPAR, 0:NPAR])
                    tr.then_inc(par_turned, 1)
                if s == 4:
                    pe.wait_ge(f_split, 2)
                    for m in range(MT):
                        o = sd[:, 1, m * HEADS:(m + 1) * HEADS]
                        for kt in range(KT):
                            a_hi, a_lo = opA_hi[:, kt, m * P:(m + 1) * P], opA_lo[:, kt, m * P:(m + 1) * P]
                            pe.matmul(o, a_hi, f_hi[:, kt, :], start=kt == 0, stop=False)
                            pe.matmul(o, a_hi, f_lo[:, kt, :], start=False, stop=False)
                            mm = pe.matmul(o, a_lo, f_hi[:, kt, :], start=False, stop=kt == KT - 1)
                    mm.then_inc(f_mm, 1)
                    pe.wait_ge(read_act, 2)
                    stage_turn(0)
                if s == 8:
                    pe.wait_ge(read_act, 4)
                    stage_turn(2)
                if s == 9:
                    pe.wait_ge(f_log, 1)
                    pe.matmul(sd[:, 1, 0:HEADS], tri[:, :], logf[:, 0:HEADS], start=True, stop=True)
                    pe.matmul(sd[:, 1, HEADS:2 * HEADS], tri[:, :], logf[:, HEADS:2 * HEADS], start=True, stop=False)
                    pe.matmul(sd[:, 1, HEADS:2 * HEADS], ones[:, :], logf[:, 0:HEADS],
                              start=False, stop=True).then_inc(cum_mm, 1)
                if s == 11:
                    pe.wait_ge(u_ready, CT)
                    pe.wait_ge(sw_in, 5 * 16)
                    pe.wait_ge(f_cum, 4)
                    lru_products(wr_sb)
                if s == 14:
                    pe.wait_ge(r_ready, CT)
                    lru_products(wi_sb)
                if s == 16:
                    pe.wait_ge(read_dve, 2)
                    stage_turn(4)
                if s == 20:
                    pe.wait_ge(read_act, 8)
                    stage_turn(6)
                if s == 24:
                    pe.wait_ge(pooled, CT)
                    pe.wait_ge(g_ready, CT)
                    for c in range(CT):
                        mm = pe.matmul(sd[:, c // 2, (c % 2) * T:(c % 2 + 1) * T], pw_sb[:, c, :],
                                       xpT[:, c, PP:], start=True, stop=True)
                    mm.then_inc(pool_mm, 1)
                if s in (31, 32):
                    pe.wait_ge(aug_done, 1)
                    aug_turn(8 + 2 * (s - 31), q_aug, s - 31)
                if s in (33, 34):
                    pe.wait_ge(aug_done, 2)
                    aug_turn(12 + 2 * (s - 33), k_aug, s - 33)
                attention_side(attentions[0], s,
                               lambda tile: pe.wait_ge(side_read, 14 + 2 * tile),
                               lambda g: pe.wait_ge(side_read, 16))
                if s == 47:
                    pe.wait_ge(o_ready, MT)
                    turn(pe, lambda m, c: stage[:, m, c * P:(c + 1) * P], T_YD)

            pe.wait_ge(consts, 4)

            def xn_turn(j):
                pe.wait_ge(xg_done, j + 1)
                turn(pe, lambda m, c: xres[:, m, j * NW + c * P:j * NW + (c + 1) * P], T_XN + j * MT)

            def xn_ready(j, before=T_XN):
                pe.wait_ge(op_lo, before + (j + 1) * MT)

            xn_turn(0)
            for r in range(12):
                for j in range(UN):
                    if r == 0:
                        if j < UN - 1:
                            xn_turn(j + 1)
                        xn_ready(j)
                    products(r, r, j, opA_hi, opA_lo, UK * j)
                    side(r * UN + j)

            def branch_products(group, run, k, free=None):
                unit_wait = free() if free else pair_free(pe, run)
                unit_products(pe, group, k, run % 2, opB_hi, opB_lo, CT * k, True, True)

            for k in range(NB):
                if k == 0:
                    pe.wait_ge(y_lo, 6)
                if k == NB - 1:
                    pe.wait_ge(op_lo, T_MERGED)
                branch_products(G_GATE0 + NB, R_GATE0 + NB + k, k)
            with pe.Fori(0, 3) as i:
                for k in range(NB):
                    for j in range(UN):
                        if j == 0:
                            pair_free(pe, R_LOOP + k, i, NB, NB)
                        unit_products(pe, G_LOOP + k + i * 5, j, k % 2, opA_hi, opA_lo, UK * j, j == 0, j == UN - 1)
                for k in range(NB):
                    pair_free(pe, R_LOOP + NB + k, i, NB, NB)
                    unit_products(pe, G_LOOP + NB + i * 5, k, k % 2, opB_hi, opB_lo, CT * k, True, True)
            for n in range(UN):
                for j in range(UN):
                    if n == 0:
                        pe.wait_ge(merged_ready, (NB - 1) * (j + 1))
                        turn(pe, lambda m, c: xres[:, m, j * NW + c * P:j * NW + (c + 1) * P], T_MERGED + j * MT)
                        xn_ready(j, T_MERGED)
                    products(G_OUT + n, R_OUT + n, j, opA_hi, opA_lo, UK * j)
                    if n and j == 0:
                        stage_operand(n - 1, T_XN2 + (n - 1) * MT, n * MT)
            for c in range(UN):
                for j in range(UN):
                    if c == 0:
                        xn_ready(j, T_XN2)
                    products(G_UP0 + c, R_UP0 + c, j, opB_hi, opB_lo, UK * j)
                    if j == 0:
                        if c == 0:
                            stage_operand(3, T_XN2 + 3 * MT, 4 * MT)
                        else:
                            stage_operand(c - 1, T_HID + (c - 1) * MT, (4 + c) * MT)
            with pe.Fori(0, 3) as i:
                for r in range(2 * UN):
                    down = r < UN
                    for j in range(UN):
                        if j == 0:
                            pair_free(pe, R_DLOOP + r, i, UN, UN)
                        if r == 0:
                            pe.wait_ge(op_lo, i * (UN * MT) + T_HID + (j + 1) * MT)
                        unit_products(pe, i * (2 * UN) + G_DLOOP + r, j, r % 2, opA_hi if down else opB_hi,
                                      opA_lo if down else opB_lo, UK * j, j == 0, j == UN - 1)
                        if j == 0 and r == 0:
                            stage_operand(3, i * (UN * MT) + (T_HID + 3 * MT), i * (UN * MT) + 8 * MT)
                        if j == 0 and r > UN:
                            c = r - UN - 1
                            stage_operand(c, i * (UN * MT) + (T_HID + (4 + c) * MT), i * (UN * MT) + (9 + c) * MT)
            for n in range(UN):
                for j in range(UN):
                    if n == 0:
                        xn_ready(j, T_HID + 12 * MT)
                    products(G_DLAST + n, R_DLAST + n, j, opA_hi, opA_lo, UK * j)
                    if n == 0 and j == 0:
                        stage_operand(3, T_HID + 15 * MT, 20 * MT)
                    if n and j == 0:
                        stage_operand(n - 1, T_XN3 + (n - 1) * MT, (20 + n) * MT)

            def tp_turn(name, blocks):
                b, n = tp_use(name)
                if n:
                    pe.wait_ge(tp_free[b], n)
                for c, x in enumerate(blocks):
                    tr = pe.transpose(tp[:, b, c * P:(c + 1) * P], x, ident[:, :])
                tr.then_inc(tp_full[b], 1)

            def tp_read(name):
                b, n = tp_use(name)
                pe.wait_ge(tp_free[b], n + 1)

            def quarters(x):
                return [x[:, c * P:(c + 1) * P] for c in range(CT)]

            def mix_turn(name, a, m):
                tp_read(f"o{a}{m}")
                tp_turn(name, quarters(stage[:, m, :]))

            def qk_wait(a):
                names = {1: ("k1", "k1"), 2: ("q20", "q21"), 3: ("k30", "k31")}[a.set]
                return lambda tile: tp_read(names[tile])

            def pv_wait(a):
                def wait(g):
                    tile = GROUPS[g][0]
                    pe.wait_ge(tp_free[0], tp_use(f"o{a.set}{tile}")[1])
                    if a.set == 3:
                        pe.wait_ge(read_act, readers_before(R_HEAD2 + len(HEAD2), "A") * MT)
                return wait

            def side2(s):
                if s == 0:
                    stage_operand(3, T_XN3 + 3 * MT, 24 * MT)
                if s == 8:
                    pe.wait_ge(glu_ready, 1)
                    for m in range(MT):
                        tp_turn(f"h{m}", quarters(stage[:, m, :]))
                if s in TURNS2:
                    name, norm, src, m = TURNS2[s]
                    pe.wait_ge(h2_gained, GAINED2[norm])
                    tp_turn(name, quarters(src[:, m, :]))
                if s == 19:
                    pe.wait_ge(h2_gained, GAINED2[1])
                    tp_turn("k1", [k_dup[:, m, v].rearrange("p d e -> p (d e)") for v in range(2) for m in range(MT)])
                if s == 21:
                    pe.wait_ge(conv_dve, 2)
                    pe.wait_ge(conv_pool, 2)
                    for m in range(MT):
                        tp_turn(f"y{m}", [yT[:, c, m * P:(m + 1) * P] for c in range(CT)])
                if s in (27, 28):
                    pe.wait_ge(ln_done, s - 26)
                    tp_turn(f"n{s - 27}", quarters(y_tok[:, s - 27, :]))
                if s in MIX2:
                    mix_turn(*MIX2[s])
                for a in attentions[1:]:
                    attention_side(a, s, qk_wait(a), pv_wait(a))
                if s == 43:
                    for m in range(MT):
                        mix_turn(f"mix3{m}", 3, m)
                if 45 <= s < 49:
                    stage_operand(s - 45, T_XN4 + (s - 45) * MT, (25 + s - 45) * MT)

            for r, col in enumerate(HEAD2):
                for j in range(UN):
                    if r == 0:
                        xn_ready(j, T_XN3)
                    if j == 0:
                        pair_free(pe, R_HEAD2 + r)
                    unit_products(pe, G_HEAD2 + r, j, r % 2, opB_hi, opB_lo, UK * j, j == 0, j == UN - 1, head2_cols(col))
                    side2(r * UN + j)
            run = R_OUT2 - 1
            for u, (kt, n, first, last) in enumerate(OUT2):
                if first:
                    run += 1
                    pair_free(pe, run)
                if kt == K_CONV:
                    pe.wait_ge(conf_lo, 1)
                else:
                    tp_read({K_WIN0: "mix11", K_WIN1: "mix21", K_DIL: "mix31"}[kt])
                unit_products(pe, G_OUT2 + u // UN, u % UN, run % 2, opA_hi, opA_lo, kt, first, last)
                side2(8 * UN + u)

            def hidden_turn(before, run, i=0):
                pe.wait_ge(read_dve, i * (2 * CH2_LOOP * MT) + readers_before(run + 1, "D") * MT)
                turn(pe, lambda m, b: stage[:, m, b * P:(b + 1) * P], before)

            for r in range(2 * CH2_FIRST):
                for j in range(UN):
                    if r == 0:
                        xn_ready(j, T_XN4)
                    products(G_PAIR0 + r, R_PAIR0 + r, j, opB_hi, opB_lo, UK * j)
                    if r == 0:
                        side2(12 * UN + j)
                    if r and r % 2 == 0 and j == 0:
                        hidden_turn(T_HID2 + (r // 2 - 1) * MT, R_PAIR0 + r - 1)
            for n in range(UN):
                for k in range(CH2_FIRST):
                    u = n * CH2_FIRST + k
                    if n == 0:
                        xn_ready(k, T_HID2)
                    if k == 0:
                        pair_free(pe, R_DOWN0 + n)
                    unit_products(pe, G_PAIR0 + 2 * CH2_FIRST + u // UN, u % UN, n % 2, opA_hi, opA_lo, UK * k,
                                  k == 0, k == CH2_FIRST - 1)
                    if u == 0:
                        hidden_turn(T_HID2 + (CH2_FIRST - 1) * MT, R_DOWN0 - 1)
            with pe.Fori(0, 2) as i:
                for r in range(LOOP2_RUNS):
                    pairs = r < 2 * CH2_LOOP
                    c = r // 2
                    before = T_HID2 + CH2_FIRST * MT
                    for j in range(UN):
                        if j == 0:
                            pair_free(pe, R_LOOP2 + r, i, CH2_LOOP, 2 * CH2_LOOP)
                        if r == 2 * CH2_LOOP:
                            pe.wait_ge(op_lo, i * (CH2_LOOP * MT) + before + (j + 1) * MT)
                        unit_products(pe, i * LOOP2_RUNS + (G_LOOP2 + r), j, r % 2, opB_hi if pairs else opA_hi,
                                      opB_lo if pairs else opA_lo, UK * j, j == 0, j == UN - 1)
                        if r % 2 == 0 and 1 <= c <= CH2_LOOP and j == 0:
                            hidden_turn(i * (CH2_LOOP * MT) + before + (c - 1) * MT, R_LOOP2 + r - 1, i)

        @block.vector
        def _(dve):
            own = Chain(dve, dv)

            def gained_in_place(j):
                dve.wait_ge(sq_done, (j + 1) * MT)
                dve.tensor_tensor(xres[:, :, chunk(j)], xres[:, :, chunk(j)],
                                  gainB[:, chunk(j)].unsqueeze(1).to_broadcast([P, MT, NW]), ALU.mult).then_inc(xg_done, 1)

            def mean_square(norm):
                dve.wait_ge(sq_done, (norm + 1) * UN * MT)
                own.done(dve.tensor_reduce(msq[:, :], sumsq[:, :, :], AX.X, ALU.add))
                dve.tensor_scalar(msq[:, :], msq[:, :], 1.0 / D, EPS, ALU.mult, ALU.add).then_inc(msq_done, 1)

            def inverse_rms(norm):
                dve.wait_ge(rms_done, norm + 1)
                dve.reciprocal(rstd[:, :], rms[:, :]).then_inc(rstd_done, 1)

            def soft(z, neg, mag, done):
                own.done(dve.tensor_scalar(neg, z, -1.0, None, ALU.mult))
                dve.tensor_tensor(mag, z, neg, ALU.max).then_inc(done, 1)

            def softplus(out, neg, e, t_, r_, s_, s2, p_, times, done):
                own.done(dve.tensor_scalar(t_, e, 2.0, None, ALU.add))
                own.done(dve.reciprocal(r_, t_))
                own.done(dve.tensor_tensor(s_, e, r_, ALU.mult))
                own.done(dve.tensor_tensor(s2, s_, s_, ALU.mult))
                own.done(dve.tensor_scalar(p_, s2, 1.0 / 15, None, ALU.mult))
                for d in (13, 11, 9, 7, 5, 3):
                    own.done(dve.scalar_tensor_tensor(p_, p_, 1.0 / d, s2, ALU.add, ALU.mult))
                own.done(dve.scalar_tensor_tensor(p_, p_, 1.0, s_, ALU.add, ALU.mult))
                own.done(dve.tensor_scalar(neg, neg, 0.0, 0.5, ALU.max, ALU.mult))
                own.done(dve.tensor_tensor(p_, p_, neg, ALU.add))
                dve.tensor_scalar(out, p_, 2.0 * times, None, ALU.mult).then_inc(done, 1)

            def taps(out, src, row, k0, k1, taps_n, ready=None):
                for k in range(k0, k1):
                    for c in range(CT):
                        w = par[:, c, row + k:row + k + 1]
                        x = src[:, c, k:k + T]
                        if k == 0:
                            b = par[:, c, R_CONVB:R_CONVB + 1] if row == R_CONV else 0.0
                            ins = dve.tensor_scalar(out[:, c, :], x, w, b, ALU.mult, ALU.add)
                        else:
                            own.need(tap_marks[c])
                            ins = dve.scalar_tensor_tensor(out[:, c, :], x, w, out[:, c, :], ALU.mult, ALU.add)
                        if k == taps_n - 1:
                            ins.then_inc(ready, 1)
                        else:
                            tap_marks[c] = own.mark(ins)

            tap_marks = [0] * CT

            def head_sums(n):
                dve.wait_ge(head_sq, n + 1)
                own.done(dve.tensor_reduce(hsum[:, :], lru_om[:, :, :].rearrange("p c (b d) -> p (c b) d", d=HD),
                                           AX.X, ALU.add))
                dve.tensor_scalar(hsum[:, :], hsum[:, :], 1.0 / HD, EPS, ALU.mult, ALU.add).then_inc(head_sum, 1)

            def head_scale(n, aug, gain):
                dve.wait_ge(head_root, n + 1)
                own.done(dve.reciprocal(hinv[:, :], hroot[:, :]))
                dve.tensor_tensor(aug[:, :, 0:HD], stage[:, :, :].rearrange("p m (h d) -> p (m h) d", d=HD),
                                  hinv[:, :].unsqueeze(2).to_broadcast([P, MT * HEADS, HD]), ALU.mult).then_inc(head_scaled, 1)
                dve.wait_ge(head_scaled, n + 1)
                dve.tensor_tensor(aug[:, :, 0:HD], aug[:, :, 0:HD],
                                  bcast[:, gain:gain + HD].unsqueeze(1).to_broadcast([P, MT * HEADS, HD]),
                                  ALU.mult).then_inc(aug_done, 1)

            def score_step(a, g):
                tile, heads = GROUPS[g]
                width, n, c = (tile + 1) * P, len(heads), first_column(g)
                dve.wait_ge(qk_done, a.first + g + 1)
                if a.first + g:
                    dve.wait_ge(p_ready, a.cols + c)
                s_view = a.scores[:, :].rearrange("p (h k) -> p h k", k=width)
                dve.tensor_tensor(s_view, sd[:, 0, :].rearrange("p (h k) -> p h k", k=width),
                                  a.mask[:, T - width:T].unsqueeze(1).to_broadcast([P, n, width]), ALU.add).then_inc(s_ready, 1)
                dve.wait_ge(s_ready, a.first + g + 1)
                top = dve.tensor_reduce(a.negmax[:, c:c + n], s_view, AX.X, ALU.max, negate=True)
                if a.sinks:
                    own.done(top)
                    h = c % HEADS
                    top = dve.tensor_tensor(a.negmax[:, c:c + n], a.negmax[:, c:c + n], a.sinks[0][:, h:h + n], ALU.min)
                top.then_inc(max_ready, 1)

            def normalise(a, tile):
                cols = slice(tile * HEADS, (tile + 1) * HEADS)
                dve.wait_ge(pv_done, a.first + (2 if tile == 0 else len(GROUPS)))
                if a.sinks:
                    dve.wait_ge(sink_exp, sink_step(a.set, tile))
                    own.done(dve.tensor_tensor(a.rowsum[:, cols], a.rowsum[:, cols], a.sinks[1][:, cols], ALU.add))
                own.done(dve.reciprocal(a.rinv[:, cols], a.rowsum[:, cols]))
                r = a.rinv[:, cols].rearrange("p (b a) -> p b a", b=2).unsqueeze(3).to_broadcast([P, 2, HEADS // 2, HD])
                dve.tensor_tensor(head_view(stage[:, tile, :]), head_view(a.out(tile)), r, ALU.mult).then_inc(
                    tp_free[0] if a.set else o_ready, 1)

            def attention_side(a, s):
                s = s - A0[a.set]
                if 2 <= s < 2 + len(GROUPS):
                    score_step(a, s - 2)
                if a.sinks and s in (4, 8):
                    tile = int(s == 8)
                    cols = slice(tile * HEADS, (tile + 1) * HEADS)
                    dve.wait_ge(max_ready, a.first + (len(GROUPS) if tile else 2))
                    dve.tensor_tensor(a.sinks[1][:, cols], a.negmax[:, cols], a.sinks[0], ALU.subtract).then_inc(sink_arg, 1)
                if s == 7:
                    normalise(a, 0)
                if s == 11:
                    normalise(a, 1)

            def side(s):
                if s == 3:
                    dve.wait_ge(f_split, 1)
                    dve.tensor_tensor(f_lo[:, :, :], f_raw[:, :, :], f_hi[:, :, :].bitcast(F32), ALU.subtract).then_inc(f_split, 1)
                    dve.wait_ge(bc_in, 8 * 16)
                    dve.wait_ge(pads, 8)
                    for g in (B_QG, B_AQG, B_CQG):
                        own.done(dve.tensor_scalar(bcast[:, g:g + HD], bcast[:, g:g + HD], HD ** -0.5, None, ALU.mult))
                    marks = [own.mark(dve.tensor_scalar(recip_count[:, g, :], steps[:, :], float(2 << g), None, ALU.min))
                             for g in range(CT)]
                    own.need(marks[-1])
                    dve.reciprocal(recip_count[:, :, :], recip_count[:, :, :]).then_inc(rc_ready, 1)
                if s == 6:
                    dve.wait_ge(f_tok, 2)
                    z = ftok.rearrange("p (m h) -> p m h", m=MT)
                    own.done(dve.tensor_tensor(z, z, bcast[:, B_FB:B_FB + HEADS].unsqueeze(1).to_broadcast([P, MT, HEADS]), ALU.add))
                    soft(ftok[:, :], sp_neg[:, :], sp_abs[:, :], f_abs)
                    dve.wait_ge(par_ready, 1)
                    soft(par[:, :, R_LAM], l_neg[:, :], l_abs[:, :], lam_abs)
                if s == 7:
                    dve.wait_ge(side_read, 2)
                    dve.wait_ge(pads, 8)
                    taps(lru_u, xaT, R_CONV, 0, 2, LRU_TAPS, u_ready)
                if s == 8:
                    dve.wait_ge(f_exp, 1)
                    softplus(logf[:, :], sp_neg[:, :], sp_e[:, :], sp_t[:, :], sp_r[:, :], sp_s[:, :], sp_s2[:, :],
                             sp_p[:, :], -1.0, f_log)
                if s == 9:
                    taps(lru_u, xaT, R_CONV, 2, 4, LRU_TAPS, u_ready)
                if s == 10:
                    dve.wait_ge(lam_exp, 1)
                    softplus(l_c[:, :], l_neg[:, :], l_e[:, :], l_t[:, :], l_r[:, :], l_s[:, :], l_s2[:, :],
                             l_p[:, :], -LRU_C, c_ready)
                    dve.wait_ge(c_ready, 1)
                    dve.tensor_scalar(l_c2[:, :], l_c[:, :], 2.0, None, ALU.mult).then_inc(c_ready, 1)
                    dve.wait_ge(c_ready, 2)
                if s == 11:
                    dve.wait_ge(cum_mm, 1)
                    dve.wait_ge(pads, 8)
                    cum = sd[:, 1, 0:MT * HEADS]
                    dve.tensor_copy(q_aug[:, :, HD:HD + 1], cum.unsqueeze(2)).then_inc(f_cum, 2)
                    dve.tensor_scalar(k_aug[:, :, HD + 1:AUG], cum.unsqueeze(2), -1.0, None, ALU.mult).then_inc(f_cum, 2)
                if s == 13:
                    dve.wait_ge(r_ready, CT)
                    for c in range(CT):
                        dve.tensor_scalar(lru_z[:, c, :], lru_r[:, c, :], l_c2[:, c:c + 1], None, ALU.mult).then_inc(z_ready, 1)
                if s == 14:
                    dve.wait_ge(z_ready, CT)
                    own.done(dve.tensor_scalar(lru_p[:, :, :], lru_z[:, :, :], -1.0 / 720, None, ALU.mult))
                if s in (15, 17, 18, 19, 20):
                    d = {15: 120, 17: 24, 18: 6, 19: 2, 20: 1}[s]
                    own.done(dve.scalar_tensor_tensor(lru_p[:, :, :], lru_p[:, :, :], -1.0 / d, lru_z[:, :, :], ALU.add, ALU.mult))
                if s == 16:
                    dve.wait_ge(units_used, 16)
                    dve.wait_ge(read_act, 6)
                    dve.wait_ge(rstd_done, 1)
                    for m in range(MT):
                        dve.scalar_tensor_tensor(stage[:, m, :], acc[:, 1, m, :], rstd[:, m:m + 1], gc_sb[:, m, :],
                                                 ALU.mult, ALU.mult).then_inc(read_dve, 1)
                if s == 20:
                    own.done(dve.tensor_scalar(lru_z[:, :, :].bitcast(I32), lru_z[:, :, :], -0.25, None, ALU.is_gt))
                    dve.wait_ge(asq_ready, 1)
                    dve.copy_predicated(lru_om[:, :, :], lru_z[:, :, :].bitcast(I32), lru_p[:, :, :]).then_inc(om_ready, 1)
                if s == 23:
                    dve.wait_ge(root_ready, 1)
                    dve.wait_ge(gu_ready, 1)
                    own.done(dve.tensor_tensor(lru_p[:, :, :], lru_om[:, :, :], lru_g[:, :, :], ALU.mult))
                    for c in range(CT):
                        dve.tensor_tensor_scan(lru_u[:, c, :], lru_r[:, c, :], lru_p[:, c, :], 0.0, ALU.mult,
                                               ALU.add).then_inc(h_ready, 1)
                if s == 24:
                    dve.wait_ge(side_read, 6)
                    dve.wait_ge(om_ready, 1)
                    taps(lru_z, zT, R_SC, 0, 1, SC_TAPS, sc_ready)
                if s == 25:
                    taps(lru_z, zT, R_SC, 1, 2, SC_TAPS, sc_ready)
                    head_sums(0)
                if s == 26:
                    taps(lru_z, zT, R_SC, 2, 3, SC_TAPS, sc_ready)
                    dve.wait_ge(y_hi, 1)
                    dve.tensor_tensor(opB_lo[:, 0:CT, :], lru_u[:, :, :], opB_hi[:, 0:CT, :].bitcast(F32),
                                      ALU.subtract).then_inc(y_lo, 1)
                if s == 27:
                    head_scale(0, q_aug, B_QG)
                if s == 28:
                    dve.wait_ge(y_hi, 1 + CT)
                    for c in range(CT):
                        dve.scalar_tensor_tensor(opB_lo[:, CT + c, :], sd[:, c // 2, (c % 2) * T:(c % 2 + 1) * T],
                                                 par[:, c, R_PSCALE:R_PSCALE + 1],
                                                 opB_hi[:, CT + c, :].bitcast(F32), ALU.mult, ALU.subtract).then_inc(y_lo, 1)
                if s == 29:
                    head_sums(1)
                if s == 31:
                    head_scale(1, k_aug, B_KG)
                if s == 32:
                    dve.wait_ge(y_hi, 2 + CT)
                    dve.tensor_tensor(opB_lo[:, 2 * CT:3 * CT, :], lru_z[:, :, :], opB_hi[:, 2 * CT:3 * CT, :].bitcast(F32),
                                      ALU.subtract).then_inc(y_lo, 1)
                attention_side(attentions[0], s)
                if s == 48:
                    turned_lo(dve, T_YD, opB_hi, opB_lo, 3 * CT)

            def branch_part(n, k, run, done, i=0):
                dve.wait_ge(units_used, done)
                gates_before = (readers_before(R_GATE0, "A") + k + 1) * MT
                dve.wait_ge(read_act, i * (NB * MT) + gates_before)
                if k:
                    before = k - 1 if k > 1 else 0
                    if k > 1 or not isinstance(i, int) or i:
                        dve.wait_ge(merged_ready, i * (NB - 1) + before)
                for m in range(MT):
                    dve.tensor_tensor(stage[:, m, :] if k else xres[:, m, chunk(n)], acc[:, run % 2, m, :],
                                      gates[:, k, m, :], ALU.mult).then_inc(read_dve, 1)

            for j in range(UN):
                dve.wait_ge(gain_in[0], 16)
                gained_in_place(j)
            mean_square(0)
            for j in range(UN):
                turned_lo(dve, T_XN + j * MT, opA_hi, opA_lo, j * CT)
                if j < SPL:
                    lo_unit(dve, 0, j)
            inverse_rms(0)
            for j in range(SPL, UN):
                lo_unit(dve, 0, j)
            side(3)
            for g in range(1, G_GATE0 + NB):
                for j in range(UN):
                    lo_unit(dve, g, j)
                    side(g * UN + j)
            dve_g = G_GATE0 + NB
            for j in range(NB):
                lo_unit(dve, dve_g, j)
                side(dve_g * UN + j)
                if j:
                    branch_part(0, j - 1, R_GATE0 + NB + j - 1, dve_g * UN + j)
            with dve.Fori(0, 3) as i:
                for k in range(NB + 1):
                    for j in range(UN):
                        lo_unit(dve, G_LOOP + k + i * 5, j)
                        if k == 0 and j == 0:
                            branch_part(i, NB - 1, R_LOOP - 1, i * (5 * UN) + G_LOOP * UN, i)
                        if k == NB and j:
                            branch_part(i + 1, j - 1, R_LOOP + NB + j - 1, i * (5 * UN) + (G_LOOP + NB) * UN + j, i + 1)

            def add_to_x(run, n, done):
                dve.wait_ge(units_used, done)
                for m in range(MT):
                    dve.tensor_tensor(xres[:, m, chunk(n)], acc[:, run % 2, m, :], xres[:, m, chunk(n)],
                                      ALU.add).then_inc(read_dve, 1)

            for n in range(UN):
                for j in range(UN):
                    if n == 0 and j == 0:
                        branch_part(3, NB - 1, R_OUT - 1, G_OUT * UN, 3)
                    if n == 0:
                        turned_lo(dve, T_MERGED + j * MT, opA_hi, opA_lo, j * CT)
                    lo_unit(dve, G_OUT + n, j)
                    if n and j == 0:
                        dve.wait_ge(x_back[n - 1], 16)
                        add_to_x(R_OUT + n - 1, n - 1, (G_OUT + n) * UN)
                    if n and j == 2:
                        turned_lo(dve, T_XN2 + (n - 1) * MT, opB_hi, opB_lo, (n - 1) * CT)
            for c in range(UN):
                for j in range(UN):
                    lo_unit(dve, G_UP0 + c, j)
                    if j == 0 and c == 0:
                        dve.wait_ge(x_back[3], 16)
                        add_to_x(R_UP0 - 1, 3, G_UP0 * UN)
                        mean_square(1)
                        inverse_rms(1)
                    if j == 2 and c == 0:
                        turned_lo(dve, T_XN2 + 3 * MT, opB_hi, opB_lo, 3 * CT)
                    if j == 2 and c:
                        turned_lo(dve, T_HID + (c - 1) * MT, opA_hi, opA_lo, (c - 1) * CT)
            with dve.Fori(0, 3) as i:
                for r in range(2 * UN):
                    for j in range(UN):
                        lo_unit(dve, i * (2 * UN) + (G_DLOOP + r), j)
                        up = UN - 1 if r == 0 else r - UN - 1
                        if j == 2 and up >= 0:
                            before = T_HID + (up if r == 0 else UN + up) * MT
                            turned_lo(dve, i * (UN * MT) + before, opA_hi, opA_lo, up * CT)
                        if j == 0 and 1 <= r <= UN:
                            add_to_x(R_DLOOP + r - 1, r - 1, i * (8 * UN) + (G_DLOOP + r) * UN)
            for n in range(UN):
                for j in range(UN):
                    lo_unit(dve, G_DLAST + n, j)
                    if n == 0 and j == 2:
                        turned_lo(dve, T_HID + 15 * MT, opA_hi, opA_lo, 3 * CT)
                    if n and j == 0:
                        add_to_x(R_DLAST + n - 1, n - 1, (G_DLAST + n) * UN)
                    if n and j == 2:
                        turned_lo(dve, T_XN3 + (n - 1) * MT, opB_hi, opB_lo, (n - 1) * CT)

            conv_marks = [0] * CT

            def conv_taps(k0, k1):
                for k in range(k0, min(k1, CONV_TAPS)):
                    for c in (0, 1):
                        w, x = par[:, c, R_CONV2 + k:R_CONV2 + k + 1], hT[:, c, k:k + T]
                        if k == 0:
                            ins = dve.tensor_scalar(yT[:, c, :], x, w, par[:, c, R_CONV2B:R_CONV2B + 1], ALU.mult, ALU.add)
                        else:
                            own.need(conv_marks[c])
                            ins = dve.scalar_tensor_tensor(yT[:, c, :], x, w, yT[:, c, :], ALU.mult, ALU.add)
                        if k == CONV_TAPS - 1:
                            ins.then_inc(conv_dve, 1)
                        else:
                            conv_marks[c] = own.mark(ins)

            def head2_heads(n):
                _, src, _, _, width = NORMS2[n]
                heads = width // HD
                stat = lambda x: x[:, 0:MT * heads].rearrange("p (m h) -> p m h", m=MT)
                return src.rearrange("p m (h d) -> p m h d", d=HD), width, heads, stat

            def mix_turned_lo(name, a, m):
                b, n = tp_use(name)
                kt, tokens = MIX_KT[a], slice(m * P, (m + 1) * P)
                dve.wait_ge(mix_hi, [x for x in TP1 if x.startswith("mix")].index(name) + 1)
                dve.tensor_tensor(opA_lo[:, kt:kt + CT, tokens], tp[:, b].rearrange("p (c t) -> p c t", c=CT),
                                  opA_hi[:, kt:kt + CT, tokens].bitcast(F32), ALU.subtract).then_inc(tp_free[b], 1)

            def side2(s):
                if s == 0:
                    add_to_x(R_DLAST + 3, 3, (G_DLAST + 4) * UN)
                    mean_square(2)
                    inverse_rms(2)
                if s == 2:
                    turned_lo(dve, T_XN3 + 3 * MT, opB_hi, opB_lo, 3 * CT)
                if s == 4:
                    dve.wait_ge(masks_raw, 2)
                    own.mark(dve.tensor_scalar(dist[:, 0, :], dist[:, 0, :], 3, None, ALU.bitwise_and))
                    own.done(dve.tensor_scalar(dist[:, 1, :], dist[:, 1, :], 15, None, ALU.bitwise_and))
                    own.mark(dve.tensor_scalar(mult4[:, :], dist[:, 0, :], 0.0, None, ALU.is_equal))
                    own.done(dve.tensor_scalar(mult16[:, :], dist[:, 1, :], 0.0, None, ALU.is_equal))
                    own.mark(dve.tensor_scalar(near[:, :], mult4[:, :], float(np.log(2)), None, ALU.mult))
                    own.done(dve.tensor_scalar(far[:, :], mult4[:, :], -NEG, NEG, ALU.mult, ALU.add))
                    dve.scalar_tensor_tensor(near[:, :], mult16[:, :], float(np.log(1.5)), near[:, :],
                                             ALU.mult, ALU.add).then_inc(mults_ready, 1)
                    dve.scalar_tensor_tensor(far[:, :], mult16[:, :], float(np.log(2)), far[:, :],
                                             ALU.mult, ALU.add).then_inc(mults_ready, 1)
                    for a in range(2):
                        own.done(dve.tensor_scalar(
                            nsink[:, a * HEADS:(a + 1) * HEADS].rearrange("p (b a) -> p b a", b=2),
                            bcast[:, B_SINK + a * HEADS:B_SINK + (a + 1) * HEADS].rearrange("p (a b) -> p b a", b=2),
                            -1.0, None, ALU.mult))
                if s == 10:
                    for b in range(2):
                        dve.wait_ge(tp_free[b], 1)
                    dve.wait_ge(pads2, 1)
                if 10 <= s < 18:
                    conv_taps(4 * (s - 10), 4 * (s - 9))
                if s in (13, 17, 21, 25, 29):
                    n = (s - 13) // 4
                    _, width, heads, stat = head2_heads(n)
                    dve.wait_ge(h2_sq, n + 1)
                    own.done(dve.tensor_reduce(stat(hsum), squares2[:, :, 0:width].rearrange("p m (h d) -> p m h d", d=HD),
                                               AX.X, ALU.add))
                    dve.tensor_scalar(hsum[:, :], hsum[:, :], 1.0 / HD, EPS, ALU.mult, ALU.add).then_inc(h2_sum, 1)
                if s in (15, 19, 23, 27, 31):
                    n = (s - 15) // 4
                    x, width, heads, stat = head2_heads(n)
                    dve.wait_ge(h2_root, n + 1)
                    own.done(dve.reciprocal(hinv[:, :], hroot[:, :]))
                    dve.tensor_tensor(x, x, stat(hinv).unsqueeze(3).to_broadcast([P, MT, heads, HD]),
                                      ALU.mult).then_inc(h2_scaled, 1)
                if s == 24:
                    for name in ("y0", "y1"):
                        b, n = tp_use(name)
                        dve.wait_ge(tp_free[b], n + 1)
                    for m in range(MT):
                        own.done(dve.bn_stats(bn6[:, m, :], y_tok[:, m, :]))
                        own.done(dve.bn_aggr(bn2[:, m, :], bn6[:, m, :]))
                    dve.tensor_scalar(bn_var[:, :].unsqueeze(2), bn2[:, :, 1:2], EPS, None, ALU.add).then_inc(ln_var, 1)
                if s == 26:
                    dve.wait_ge(ln_root, 1)
                    own.done(dve.reciprocal(bn_inv[:, :], bn_root[:, :]))
                    for m in range(MT):
                        dve.tensor_scalar(y_tok[:, m, :], y_tok[:, m, :], bn2[:, m, 0:1], bn_inv[:, m:m + 1],
                                          ALU.subtract, ALU.mult).then_inc(ln_done, 1)
                if s == 31:
                    dve.wait_ge(conf_hi, 1)
                    dve.tensor_tensor(opA_lo[:, K_CONV:K_CONV + CT, :], silT[:, :, :],
                                      opA_hi[:, K_CONV:K_CONV + CT, :].bitcast(F32), ALU.subtract).then_inc(conf_lo, 1)
                if s - 2 in MIX2:
                    mix_turned_lo(*MIX2[s - 2])
                for a in attentions[1:]:
                    attention_side(a, s)
                if s == 45:
                    for m in range(MT):
                        mix_turned_lo(f"mix3{m}", 3, m)
                if s in (34, 36, 38, 40):
                    n = (s - 34) // 2
                    add_to_x(R_OUT2 + n, n, G_OUT2 * UN + 2 * (n + 1))
                if 41 <= s < 49:
                    u = s - 32
                    add_to_x(R_OUT2 + UN + u - 9, (u - 9) % UN, G_OUT2 * UN + u)
                if 47 <= s <= 50:
                    turned_lo(dve, T_XN4 + (s - 47) * MT, opB_hi, opB_lo, (s - 47) * CT)
                if s == 50:
                    mean_square(3)
                    inverse_rms(3)

            for u in range(12 * UN):
                lo_unit(dve, G_HEAD2 + u // UN, u % UN, head2_cols(HEAD2[u // UN]) if u < 8 * UN else NW)
                side2(u)

            def hidden(run, done, i=0):
                dve.wait_ge(units_used, done)
                dve.wait_ge(read_act, i * (CH2_LOOP * MT) + readers_before(run, "A") * MT)
                for m in range(MT):
                    dve.scalar_tensor_tensor(stage[:, m, :], acc[:, run % 2, m, :], rstd[:, m:m + 1], silu_gate[:, m, :],
                                             ALU.mult, ALU.mult).then_inc(read_dve, 1)

            for r in range(2 * CH2_FIRST):
                for j in range(UN):
                    lo_unit(dve, G_PAIR0 + r, j)
                    if r == 0:
                        side2(12 * UN + j)
                    if r and r % 2 == 0 and j == 0:
                        hidden(R_PAIR0 + r - 1, (G_PAIR0 + r) * UN)
                    if r and r % 2 == 0 and j == 2:
                        turned_lo(dve, T_HID2 + (r // 2 - 1) * MT, opA_hi, opA_lo, (r // 2 - 1) * CT)
            down0 = G_PAIR0 + 2 * CH2_FIRST
            for u in range(CH2_FIRST * UN):
                lo_unit(dve, down0 + u // UN, u % UN)
                if u == 0:
                    hidden(R_DOWN0 - 1, down0 * UN)
                if u == 2:
                    turned_lo(dve, T_HID2 + (CH2_FIRST - 1) * MT, opA_hi, opA_lo, (CH2_FIRST - 1) * CT)
                if u and u % CH2_FIRST == 0:
                    n = u // CH2_FIRST - 1
                    add_to_x(R_DOWN0 + n, n, down0 * UN + u)
            with dve.Fori(0, 2) as i:
                for r in range(LOOP2_RUNS):
                    c = r // 2
                    for j in range(UN):
                        lo_unit(dve, i * LOOP2_RUNS + (G_LOOP2 + r), j)
                        done = i * LOOP2_UNITS + (G_LOOP2 + r) * UN
                        if j == 0 and r == 0:
                            add_to_x(R_LOOP2 - 1, 3, done)
                        if j == 0 and r % 2 == 0 and 1 <= c <= CH2_LOOP:
                            hidden(R_LOOP2 + r - 1, done, i)
                        if j == 0 and r > 2 * CH2_LOOP:
                            n = r - 2 * CH2_LOOP - 1
                            add_to_x(R_LOOP2 + 2 * CH2_LOOP + n, n, done)
                        if j == 2 and r % 2 == 0 and 1 <= c <= CH2_LOOP:
                            before = T_HID2 + (CH2_FIRST + c - 1) * MT
                            turned_lo(dve, i * (CH2_LOOP * MT) + before, opA_hi, opA_lo, (c - 1) * CT)
            add_to_x(R_LOOP2 + LOOP2_RUNS - 1, 3, (G_LOOP2 + 2 * LOOP2_RUNS) * UN)


def kernel(**inputs):
    import concourse.bacc as bacc
    from concourse.bass_utils import run_bass_kernel_spmd

    nc = bacc.Bacc("TRN2", target_bir_lowering=False, num_devices=1, dynamic_dma_scratch_size=1024)
    arrays, t = {}, {}
    for name, a in inputs.items():
        a = np.ascontiguousarray(a)
        arrays[f"in_{name}"] = a
        t[name] = nc.dram_tensor(f"in_{name}", a.shape, mybir.dt.from_np(a.dtype), kind="ExternalInput").ap()
    out = nc.dram_tensor("out_x", (1, T, D), F32, kind="ExternalOutput").ap()
    build(nc, t, out)
    r = run_bass_kernel_spmd(nc, [arrays], core_ids=[0])
    return r.results[0]["out_x"]
```

```python
from contextlib import ExitStack

import numpy as np

import concourse.bass as bass
from concourse import mybir

F32 = mybir.dt.float32
F32R = mybir.dt.float32r
I32 = mybir.dt.int32
ALU = mybir.AluOpType
ACT = mybir.ActivationFunctionType
AX = mybir.AxisListType

P = 128
T = 256
MT = T // P
D = 2048
KT = D // P
NW = 512
UK = 4
UN = KT // UK
RAW = 4
SPL = 2
HV = 2
W = 512
CT = W // P
NB = 4
HEADS = 8
HD = 64
AUG = HD + 2
FF2 = 5632
EPS = 1e-6
NEG = -1e30
LRU_C = 8.0
LRU_TAPS, SC_TAPS, CONV_TAPS = 4, 3, 31
LP, PP, SP_, CP = LRU_TAPS - 1, 15, SC_TAPS - 1, CONV_TAPS - 1
KB = 1024

IN_XA, IN_POOL, IN_GB, IN_GC, IN_XC, IN_Q, IN_K, IN_V, IN_F, IN_GATE = (
    0, 512, 1024, 1536, 2048, 2560, 3072, 3584, 4096, 4104)
HEAD1 = [IN_XA, IN_POOL, IN_GC, IN_XC, IN_GB, IN_Q, IN_K, IN_V]
I2_AQ, I2_AK, I2_AV, I2_BU, I2_BG, I2_CQ0, I2_CQ1, I2_CKV = 0, 512, 1024, 1536, 2048, 2560, 3072, 3584
HEAD2 = [I2_BU, I2_BG, I2_CQ0, I2_CKV, I2_CQ1, I2_AQ, I2_AK, I2_AV]

R_CONV, R_CONVB, R_BR, R_BI, R_LAM, R_PSCALE, R_SC = 0, 4, 5, 6, 7, 8, 9
R_CONV2, R_CONV2B, R_LNG, R_LNB = 12, 43, 44, 45
NPAR = 46
B_QG, B_KG, B_AQG, B_AKG, B_CQG, B_CKG, B_FB, B_SINK = 0, 64, 128, 192, 256, 320, 384, 392
NBC = 408

READERS = (
    "AAADAAAA"
    + ("AAAA" + "DDDD") * 4
    + "DDDD"
    + "AAAA" + ("DDDD" + "AAAA") * 3 + "DDDD"
    + "AAAAAAAA"
    + "DDDD" * 3
    + "AD" * 3 + "DDDD"
    + ("AD" * 4 + "DDDD") * 2
)
GROUPS = [(0, (0, 2, 4, 6)), (0, (1, 3, 5, 7)), (1, (0, 2)), (1, (4, 6)), (1, (1, 3)), (1, (5, 7))]


K_DIL, K_CONV, K_WIN0, K_WIN1 = 0, 4, 8, 12
CH2_LOOP = 4
CH2_FIRST = FF2 // NW - 2 * CH2_LOOP


def readers_before(run, who):
    return READERS[:run].count(who)


def blocks_of(group):
    tile, heads = group
    return [(h, kt) for h in heads for kt in range(tile + 1)]


def build(nc, t, out):
    ctx = ExitStack()
    with ctx:
        sem = lambda name: ctx.enter_context(nc.semaphore(name))

        base = -(-nc.sbuf_base // 32) * 32
        room = (nc.sbuf_usable_end - base) // KB - 1
        ctx.enter_context(nc.sbuf_tensor("arena", [P, room * 256], F32))

        def at(name, kb, shape, dtype=F32):
            return nc.alloc_sbuf_tensor_at(name, shape, dtype, offset=base + int(kb * KB))

        raw = at("raw", 0, [P, RAW, UK, NW])
        whi = at("whi", 32, [P, SPL, UK, NW], F32R)
        wlo = at("wlo", 48, [P, SPL, UK, NW], F32R)
        opA_hi = at("opA_hi", 64, [P, KT, T], F32R)
        opA_lo = at("opA_lo", 80, [P, KT, T], F32R)
        opB_hi = at("opB_hi", 96, [P, KT, T], F32R)
        opB_lo = at("opB_lo", 112, [P, KT, T], F32R)
        xres = at("xres", 128, [P, MT, D])
        stage = at("stage", 144, [P, MT, NW])
        gainB = at("gainB", 148, [P, D])
        gates = at("gates", 156, [P, NB, MT, NW])
        x_gained = at("x_gained", 96, [P, MT, D])
        c0 = 172
        ident = at("ident", c0, [P, P])
        tri = at("tri", c0 + 0.5, [P, P])
        ones = at("ones", c0 + 1, [P, P])
        mask = at("mask", c0 + 1.5, [P, T])
        par = at("par", c0 + 2.5, [P, CT, NPAR])
        bcast = at("bcast", c0 + 3.25, [P, NBC])
        f_raw = at("f_raw", c0 + 5, [P, KT, HEADS])
        steps = at("steps", c0 + 8, [P, 16], I32)
        f_hi = at("f_hi", c0 + 5.5, [P, KT, HEADS], F32R)
        f_lo = at("f_lo", c0 + 6, [P, KT, HEADS], F32R)
        smalls = at("smalls", c0 + 6.5, [P, 384])
        f_heads = at("f_heads", c0 + 8.25 + 21, [P, T])
        c1 = c0 + 8.25
        used = [0]

        def small(n):
            used[0] += n
            assert used[0] <= 384
            return smalls[:, used[0] - n:used[0]]

        sumsq = small(8).rearrange("p (m c) -> p m c", m=MT)
        msq, rms, rstd = small(2), small(2), small(2)
        ftok = small(16)
        sp_neg, sp_abs, sp_e, sp_t, sp_r, sp_s, sp_s2, sp_p, logf = [small(16) for _ in range(9)]
        l_neg, l_abs, l_e, l_t, l_r, l_s, l_s2, l_p, l_c, l_c2 = [small(4) for _ in range(10)]
        recip_count = small(16 * CT).rearrange("p (g t) -> p g t", g=CT)
        negmax, rowsum, rinv = small(16), small(16), small(16)
        hsum, hroot, hinv = small(16), small(16), small(16)

        rows_par = at("rows_par", 156, [P, W])
        junk = at("junk", 160, [P, MT, NW])
        pool_a = at("pool_a", c1, [P, PP + T])
        pool_b = at("pool_b", c1 + 1.25, [P, PP + T])
        xaT = at("xaT", c1, [P, CT, LP + T])
        xpT = at("xpT", c1 + 4.25, [P, CT, PP + T])
        zT = at("zT", c1 + 8.75, [P, CT, SP_ + T])
        gbT = at("gbT", c1 + 13, [P, CT, T])
        lru_u = at("lru_u", c1 + 17, [P, CT, T])
        lru_om = at("lru_om", c1 + 21, [P, CT, T])
        lru_r = at("lru_r", 156, [P, CT, T])
        lru_g = at("lru_g", 160, [P, CT, T])
        lru_z = at("lru_z", 164, [P, CT, T])
        lru_p = at("lru_p", 168, [P, CT, T])
        wr_sb = at("wr_sb", c1 + 25, [P, CT, P])
        wi_sb = at("wi_sb", c1 + 27, [P, CT, P])
        pw_sb = at("pw_sb", c1 + 29, [P, CT, P])
        gc_sb = at("gc_sb", 148, [P, MT, NW])
        v_sb = at("v_sb", 152, [P, MT, NW])
        q_aug = at("q_aug", c1 + 31, [P, MT * HEADS, AUG])
        k_aug = at("k_aug", c1 + 35.25, [P, MT * HEADS, AUG])
        c2 = c1 + 39.5
        assert c2 <= room, (c2, room)
        qT = at("qT", c1, [P, HEADS, T])
        kT = at("kT", c1 + 8, [P, HEADS, T])
        scores = at("scores", c1 + 16, [P, NW])
        probs = at("probs", c1 + 18, [P, 2, NW])
        probsT = at("probsT", c1 + 22, [P, NW])

        acc = ctx.enter_context(nc.psum_tensor("acc", [P, 2, MT, NW], F32))
        tp = ctx.enter_context(nc.psum_tensor("tp", [P, 2, NW], F32))
        sd = ctx.enter_context(nc.psum_tensor("sd", [P, 2, NW], F32))

        u_sb = at("u_sb", 156, [P, MT, W])
        sig_sb = at("sig_sb", 160, [P, MT, W])
        tap_ring = [at("taps_a", 156, [P, 8, T]), at("taps_b", c1 + 24.5, [P, 4, T])]
        TAPS = 12
        hT = at("hT", c1, [P, CT, CP + T])
        yT = at("yT", c1 + 4.5, [P, CT, T])
        y_tok = at("y_tok", c1 + 8.5, [P, MT, W])
        silT = at("silT", c1, [P, CT, T])
        q_tok = at("q_tok", c1 + 12.5, [P, 2, MT, W])
        q2T = at("q2T", c1 + 20.5, [P, 2, CT, T])
        kv_tok = at("kv_tok", c1 + 28.5, [P, MT, 2 * P])
        k_dup = at("k_dup", c1 + 30.5, [P, MT, 2, 2, HD])
        kwT = at("kwT", c1 + 32.5, [P, 2, T])
        win_mask = at("win_mask", c1 + 34.5, [P, T])
        dil_mask = at("dil_mask", c1 + 35.5, [P, T])
        mult4 = at("mult4", c1 + 36.5, [P, P])
        mult16 = at("mult16", c1 + 37, [P, P])
        dist = at("dist", c1 + 37.5, [P, 2, P], I32)
        smalls2 = at("smalls2", c1 + 38.5, [P, 256])
        near = at("near", c1 + 39.5, [P, P])
        far = at("far", c1 + 40, [P, P])
        assert c1 + 40.5 <= room, (c1, room)
        k_tok = at("k_tok", 156, [P, MT, W])
        kdT = at("kdT", 160, [P, CT, T])
        vd_sb = at("vd_sb", 164, [P, MT, W])
        squares2 = at("squares2", 168, [P, MT, W])
        scores2 = at("scores2", 148, [P, NW])
        probs2 = at("probs2", 150, [P, 2, NW])
        probsT2 = at("probsT2", 154, [P, NW])
        gain2 = at("gain2", c1, [P, D])
        silu_gate = at("silu_gate", 156, [P, MT, NW])
        stat2 = lambda k: smalls2[:, k * 48:(k + 1) * 48].rearrange("p (s c) -> p s c", s=3)
        negmax2, rowsum2, rinv2, sink_e = [stat2(k) for k in range(4)]
        nsink = smalls2[:, 192:208]
        bn6 = smalls2[:, 208:220].rearrange("p (m c) -> p m c", m=MT)
        bn2 = smalls2[:, 220:224].rearrange("p (m c) -> p m c", m=MT)
        bn_var, bn_root, bn_inv = [smalls2[:, 224 + 2 * k:226 + 2 * k] for k in range(3)]

        landed = [sem(f"landed{s}") for s in range(RAW)]
        hi_split = sem("hi_split")
        lo_split = sem("lo_split")
        units_used = sem("units_used")
        read_act = sem("read_act")
        read_dve = sem("read_dve")
        turned = sem("turned")
        op_hi = sem("op_hi")
        op_lo = sem("op_lo")
        staged = sem("staged")
        x_in = [sem(f"x_in{j}") for j in range(UN)]
        x_back = [sem(f"x_back{j}") for j in range(UN)]
        gain_in = [sem(f"gain_in{n}") for n in range(1, 4)]
        sq_done = sem("sq_done")
        xg_done = sem("xg_done")
        msq_done, rms_done, rstd_done = sem("msq_done"), sem("rms_done"), sem("rstd_done")
        dve_own, pool_own = sem("dve_own"), sem("pool_own")
        consts, pads = sem("consts"), sem("pads")
        rc_ready = sem("rc_ready")
        rows_in, bc_in, f_in, sw_in = sem("rows_in"), sem("bc_in"), sem("f_in"), sem("sw_in")
        par_turned, par_ready = sem("par_turned"), sem("par_ready")
        stored = sem("stored")
        side_turned = sem("side_turned")
        side_read = sem("side_read")
        f_rows = sem("f_rows")
        u_ready, lru_mm, r_ready, g_ready, a_ready = (
            sem("u_ready"), sem("lru_mm"), sem("r_ready"), sem("g_ready"), sem("a_ready"))
        lam_abs, lam_exp = sem("lam_abs"), sem("lam_exp")
        c_ready, z_ready = sem("c_ready"), sem("z_ready")
        om_ready, root_ready, h_ready = sem("om_ready"), sem("root_ready"), sem("h_ready")
        gu_ready, asq_ready = sem("gu_ready"), sem("asq_ready")
        pooled, pool_mm, sc_ready, sc_gated = sem("pooled"), sem("pool_mm"), sem("sc_ready"), sem("sc_gated")
        y_hi, y_lo = sem("y_hi"), sem("y_lo")
        f_split, f_mm, f_tok, f_abs, f_exp, f_log, f_cum, cum_mm = [
            sem("f_" + n) for n in ("split", "mm", "tok", "abs", "exp", "log", "cum", "cumm")]
        head_sq, head_sum, head_root, head_scaled, aug_done = [
            sem("head_" + n) for n in ("sq", "sum", "root", "scaled", "aug")]
        qk_done, s_ready, max_ready, p_ready, p_turned, pT_ready, pv_done = [
            sem("at_" + n) for n in ("qk", "s", "max", "p", "turn", "pT", "pv")]
        o_ready = sem("o_ready")
        tp_full = [sem(f"tp_full{b}") for b in range(2)]
        tp_free = [sem(f"tp_free{b}") for b in range(2)]
        h2_sq, h2_sum, h2_root, h2_scaled, h2_gained = [
            sem("h2_" + n) for n in ("sq", "sum", "root", "scaled", "gained")]
        glu_ready, conv_dve = sem("glu_ready"), sem("conv_dve")
        tap_made = sem("tap_made")
        tap_first, tap_added = sem("tap_first"), sem("tap_added")
        ln_var, ln_root, ln_done = sem("ln_var"), sem("ln_root"), sem("ln_done")
        mix_hi, conf_hi, conf_lo = sem("mix_hi"), sem("conf_hi"), sem("conf_lo")
        masks_raw, mults_ready, masks_ready = sem("masks_raw"), sem("mults_ready"), sem("masks_ready")
        sink_arg, sink_exp = sem("sink_arg"), sem("sink_exp")
        pads2, silu_done = sem("pads2"), sem("silu_done")
        merged_ready = sem("merged_ready")

        class Chain:

            def __init__(self, eng, s):
                self.eng, self.s, self.n = eng, s, 0

            def mark(self, ins):
                ins.then_inc(self.s, 1)
                self.n += 1
                return self.n

            def need(self, n):
                self.eng.wait_ge(self.s, n)

            def done(self, ins):
                self.need(self.mark(ins))

        block = ctx.enter_context(nc.Block())

        def rows_of(w):
            return w.rearrange("(k p) n -> p k n", p=P)

        w_in = rows_of(t["w_in"][0])
        w_br = rows_of(t["w_branch"][0].rearrange("b w n -> (b w) n"))
        w_out = rows_of(t["w_out"][0])
        w_up = rows_of(t["w_mlp_up"][0])
        w_dn = rows_of(t["w_mlp_down"][0])
        w_in2, w_out2, w_gate2, w_up2, w_dn2 = [
            rows_of(t[n][0]) for n in ("w_in_2", "w_out_2", "w_gate_2", "w_up_2", "w_down_2")]

        def load_unit(eng, group, j, w, kt, col, cols=NW):
            if not (isinstance(group, int) and group == 0):
                eng.wait_ge(lo_split, group * (UN * HV) + (j - RAW + 1) * HV)
            src = w[:, kt:kt + UK, col:col + cols] if isinstance(col, int) else w[:, kt:kt + UK, bass.ds(col, cols)]
            eng.dma_start(raw[:, j, :, 0:cols], src).then_inc(landed[j], 16)

        halves = [slice(h * (UK // HV), (h + 1) * (UK // HV)) for h in range(HV)]

        def hi_unit(eng, group, j, cols=NW):
            eng.wait_ge(landed[j], group * 16 + 16)
            if not (isinstance(group, int) and group == 0 and j < SPL):
                eng.wait_ge(units_used, group * UN + j - SPL + 1)
            for half in range(HV):
                k = halves[half]
                eng.activation(whi[:, j % SPL, k, 0:cols], raw[:, j, k, 0:cols], ACT.Copy).then_inc(hi_split, 1)

        def lo_unit(eng, group, j, cols=NW):
            for half in range(HV):
                k = halves[half]
                eng.wait_ge(hi_split, group * (UN * HV) + j * HV + half + 1)
                eng.tensor_tensor(wlo[:, j % SPL, k, 0:cols], raw[:, j, k, 0:cols],
                                  whi[:, j % SPL, k, 0:cols].bitcast(F32), ALU.subtract).then_inc(lo_split, 1)

        def unit_products(eng, group, j, pair, hi, lo, kt, first, last, cols=NW, mid=None):
            s = j % SPL
            for i in range(UK):
                if mid and i == UK // HV:
                    mid()
                if i % (UK // HV) == 0:
                    eng.wait_ge(lo_split, group * (UN * HV) + j * HV + i // (UK // HV) + 1)
                for m in range(MT):
                    o = acc[:, pair, m, 0:cols]
                    a_hi = hi[:, kt + i, m * P:(m + 1) * P]
                    a_lo = lo[:, kt + i, m * P:(m + 1) * P]
                    eng.matmul(o, a_hi, whi[:, s, i, 0:cols], start=first and i == 0, stop=False)
                    eng.matmul(o, a_hi, wlo[:, s, i, 0:cols], start=False, stop=False)
                    mm = eng.matmul(o, a_lo, whi[:, s, i, 0:cols], start=False, stop=last and i == UK - 1)
            mm.then_inc(units_used, 1)

        def pair_free(eng, run, i=0, runs_a=0, runs_d=0):
            if run < 2:
                return
            who = READERS[run - 2]
            count = readers_before(run - 1, who)
            step = runs_a if who == "A" else runs_d
            eng.wait_ge(read_act if who == "A" else read_dve, count * MT + (i * (step * MT) if step else 0))

        def turn(eng, src, before):
            for m in range(MT):
                if not (isinstance(before, int) and before == 0):
                    eng.wait_ge(op_lo, before + m - 1)
                for c in range(CT):
                    tr = eng.transpose(tp[:, m, c * P:(c + 1) * P], src(m, c), ident[:, :])
                tr.then_inc(turned, 1)

        def turned_hi(eng, before, hi, kt):
            for m in range(MT):
                eng.wait_ge(turned, before + m + 1)
                eng.activation(hi[:, kt:kt + CT, m * P:(m + 1) * P],
                               tp[:, m].rearrange("p (c t) -> p c t", c=CT), ACT.Copy).then_inc(op_hi, 1)

        def turned_lo(eng, before, hi, lo, kt):
            for m in range(MT):
                eng.wait_ge(op_hi, before + m + 1)
                eng.tensor_tensor(lo[:, kt:kt + CT, m * P:(m + 1) * P],
                                  tp[:, m].rearrange("p (c t) -> p c t", c=CT),
                                  hi[:, kt:kt + CT, m * P:(m + 1) * P].bitcast(F32),
                                  ALU.subtract).then_inc(op_lo, 1)

        G_GATE0, G_LOOP, G_OUT, G_UP0, G_DLOOP, G_DLAST = 8, 13, 28, 32, 36, 60
        R_GATE0, R_LOOP, R_OUT, R_UP0, R_DLOOP, R_DLAST = 8, 16, 40, 44, 48, 72
        T_XN, T_YD, T_MERGED, T_XN2, T_HID, T_XN3 = 0, 8, 10, 18, 26, 58
        G_HEAD2, G_OUT2, G_PAIR0, G_LOOP2 = 64, 72, 76, 85
        R_HEAD2, R_OUT2, R_PAIR0, R_DOWN0, R_LOOP2 = 76, 84, 96, 102, 106
        T_XN4, T_HID2 = 66, 74
        LOOP2_RUNS, LOOP2_UNITS = 12, 12 * UN
        OUT2 = ([(k, n + m, k == K_CONV, k == K_WIN0) for n in (0, 2) for k in (K_CONV, K_WIN0) for m in range(2)]
                + [(k, n, True, True) for k in (K_WIN1, K_DIL) for n in range(UN)])
        TAPS_DVE = [0, 3, 7, 8, 9, 11, 11, 15, 17, 21, 22, 26, 28, CONV_TAPS]
        TAPS_ACT = [1, 3, 6, 7, 8, 8, 9, 13, 16, 19, 22, 25, 28, CONV_TAPS]

        def tap_product(k, c):
            r = (k - 1) * 2 + c - 2
            e = r % TAPS
            return r, tap_ring[e // 8][:, e % 8, :]

        TP0 = ["h0", "y0"] + [f"o{a}{m}" for a in (1, 2, 3) for m in range(MT)]
        TP1 = ["h1", "q10", "q11", "k1", "y1", "q20", "q21", "n0", "q30", "n1", "q31", "mix10", "mix11",
               "k30", "k31", "mix20", "mix21", "mix30", "mix31"]

        def tp_use(name):
            b = int(name in TP1)
            return b, (TP0, TP1)[b].index(name)

        A0 = [35, 20, 26, 33]
        LAST_MIX = 43

        class Attention:

            def __init__(self, set_, q, k, v, out, bufs, stats, masks, sinks=None):
                self.set, self.q, self.k, self.v, self.out = set_, q, k, v, out
                self.scores, self.probs, self.probsT = bufs
                self.negmax, self.rowsum, self.rinv = stats
                self.mask, self.sinks = masks, sinks
                self.first = set_ * len(GROUPS)
                self.cols = set_ * MT * HEADS

        def pair_of(x, h):
            return x[(h % 2) * HD:(h % 2 + 1) * HD, h // 2, :]

        attentions = [Attention(
            0, lambda h: qT[0:AUG, h, :], lambda h: kT[0:AUG, h, :], lambda h, kt: v_sb[:, kt, h * HD:(h + 1) * HD],
            lambda tile: tp[:, tile], (scores, probs, probsT), (negmax, rowsum, rinv), mask)]

        def windowed(a):
            return Attention(
                a, lambda h: pair_of(q2T[:, a - 1], h), lambda h: kwT[(h % 2) * HD:(h % 2 + 1) * HD, a - 1, :],
                lambda h, kt: kv_tok[:, kt, P + (a - 1) * HD:P + a * HD], lambda tile: tp[:, 0],
                (scores2, probs2, probsT2), [x[:, a - 1] for x in (negmax2, rowsum2, rinv2)], win_mask,
                (nsink[:, (a - 1) * HEADS:a * HEADS], sink_e[:, a - 1]))

        attentions += [windowed(1), windowed(2), Attention(
            3, lambda h: pair_of(q2T[:, 0], h), lambda h: pair_of(kdT, h),
            lambda h, kt: vd_sb[:, kt, h * HD:(h + 1) * HD], lambda tile: tp[:, 0],
            (scores2, probs2, probsT2), [x[:, 2] for x in (negmax2, rowsum2, rinv2)], dil_mask)]

        def same(x, width):
            return lambda m: [x[:, m, 0:width].rearrange("p (h d) -> p h d", d=HD)]

        NORMS2 = [(run, src, gain, same(src, W), W) for run, src, gain in (
            (HEAD2.index(I2_CQ0), q_tok[:, 0], B_CQG), (HEAD2.index(I2_CQ1), q_tok[:, 1], B_CQG),
            (HEAD2.index(I2_AQ), q_tok[:, 0], B_AQG), (HEAD2.index(I2_AK), k_tok[:, :, :], B_AKG))]
        NORMS2.insert(1, (HEAD2.index(I2_CKV), kv_tok[:, :, 0:P], B_CKG,
                          lambda m: [k_dup[:, m, :, d, :] for d in range(2)], P))
        GAINED2 = [MT, 3 * MT, 4 * MT, 5 * MT, 6 * MT]
        TURNS2 = {15: ("q10", 0, q_tok[:, 0], 0), 16: ("q11", 0, q_tok[:, 0], 1),
                  24: ("q20", 2, q_tok[:, 1], 0), 25: ("q21", 2, q_tok[:, 1], 1),
                  32: ("k30", 4, k_tok, 0), 33: ("k31", 4, k_tok, 1)}
        MID_TURNS2 = {29: ("q30", 3, q_tok[:, 0], 0), 30: ("q31", 3, q_tok[:, 0], 1)}
        TURNED2 = {15: q2T[:, 0], 16: q2T[:, 0], 24: q2T[:, 1], 25: q2T[:, 1], 29: q2T[:, 0], 30: q2T[:, 0],
                   32: kdT, 33: kdT}
        MIX2 = {30: ("mix10", 1, 0), 31: ("mix11", 1, 1), 36: ("mix20", 2, 0), 37: ("mix21", 2, 1),
                41: ("mix30", 3, 0)}
        MIX_KT = {1: K_WIN0, 2: K_WIN1, 3: K_DIL}

        def sink_step(a, tile):
            return (a - 1) * MT + tile + 1

        def first_column(g):
            return sum(len(heads) for _, heads in GROUPS[:g])

        def head2_cols(col):
            return 2 * P if col == I2_CKV else NW

        def chunk(n, width=NW):
            return slice(n * width, (n + 1) * width) if isinstance(n, int) else bass.ds(n * width, width)

        def head_view(x):
            return x.rearrange("p (a b d) -> p b a d", b=2, d=HD)

        @block.sync
        def _(sp):
            def rows_load():
                for r, name in ((R_CONV, "lru_conv_w"), (R_SC, "sconv_w"), (R_CONV2, "conv_w_2")):
                    w = t[name][0]
                    sp.dma_start(rows_par[r:r + w.shape[0], :], w).then_inc(rows_in, 16)
                for r, name in ((R_CONVB, "lru_conv_b"), (R_BR, "lru_br"), (R_BI, "lru_bi"), (R_LAM, "lru_lambda"),
                                (R_PSCALE, "pool_scale"), (R_CONV2B, "conv_b_2"), (R_LNG, "conv_ln_g_2"),
                                (R_LNB, "conv_ln_b_2")):
                    sp.dma_start(rows_par[r:r + 1, :], t[name]).then_inc(rows_in, 16)

            def broadcast_load():
                sp.dma_start(f_raw[:, :, :], w_in[:, :, IN_F:IN_GATE]).then_inc(f_in, 16)
                for c, name in ((B_QG, "q_norm_g"), (B_KG, "k_norm_g"), (B_AQG, "a_q_g_2"), (B_AKG, "a_k_g_2"),
                                (B_CQG, "c_q_g_2"), (B_CKG, "c_k_g_2"), (B_FB, "forget_b"), (B_SINK, "c_sinks_2")):
                    n = t[name].shape[1]
                    sp.dma_start(bcast[:, c:c + n], t[name][0].partition_broadcast(P)).then_inc(bc_in, 16)

            def group_weights_load():
                sp.wait_ge(pads, 2)
                for dst, name in ((wr_sb, "lru_wr"), (wi_sb, "lru_wi")):
                    for b in range(2):
                        sp.dma_start(dst[b * HD:(b + 1) * HD, :, b * HD:(b + 1) * HD],
                                     t[name][0, b::2].rearrange("h i j -> i h j")).then_inc(sw_in, 16)
                sp.dma_start(pw_sb[:, :, :], t["pool_w"][0].rearrange("g i j -> i g j")).then_inc(sw_in, 16)

            for j in range(UN):
                sp.dma_start(gainB[:, chunk(j)], t["norm_mix_g"][0, chunk(j)].partition_broadcast(P)).then_inc(x_in[j], 16)
                sp.dma_start(xres[:, :, chunk(j)],
                             t["x"][0].rearrange("(m p) d -> p m d", p=P)[:, :, chunk(j)]).then_inc(x_in[j], 16)
                load_unit(sp, 0, j, w_in, UK * j, HEAD1[0])
                if j < 3:
                    (rows_load, broadcast_load, group_weights_load)[j]()
            for r, col in enumerate(HEAD1[1:]):
                for j in range(UN):
                    load_unit(sp, r + 1, j, w_in, UK * j, col)
            for k in range(NB):
                for j in range(UN):
                    load_unit(sp, G_GATE0 + k, j, w_in, UK * j, IN_GATE + k * D)
            for k in range(NB):
                load_unit(sp, G_GATE0 + NB, k, w_br, CT * k, 0)
            with sp.Fori(0, 3) as i:
                for k in range(NB):
                    for j in range(UN):
                        load_unit(sp, G_LOOP + k + i * 5, j, w_in, UK * j, i * NW + (IN_GATE + k * D + NW))
                for k in range(NB):
                    load_unit(sp, G_LOOP + NB + i * 5, k, w_br, CT * k, i * NW + NW)
            for n in range(UN):
                for j in range(UN):
                    load_unit(sp, G_OUT + n, j, w_out, UK * j, n * NW)
            for c in range(UN):
                for j in range(UN):
                    load_unit(sp, G_UP0 + c, j, w_up, UK * j, c * NW)

            def down_loads(g, q):
                for n in range(UN):
                    for j in range(UN):
                        load_unit(sp, g + n, j, w_dn[:, q * KT:(q + 1) * KT] if isinstance(q, int) else
                                  w_dn[:, bass.ds(q * KT, KT)], UK * j, n * NW)

            with sp.Fori(0, 3) as i:
                down_loads(G_DLOOP + i * 8, i)
                for c in range(UN):
                    for j in range(UN):
                        load_unit(sp, G_DLOOP + UN + c + i * 8, j, w_up, UK * j, i * D + (D + c * NW))
            down_loads(G_DLAST, 3)

            for r, col in enumerate(HEAD2):
                for j in range(UN):
                    load_unit(sp, G_HEAD2 + r, j, w_in2, UK * j, col, head2_cols(col))
            for u, (kt, n, _, _) in enumerate(OUT2):
                load_unit(sp, G_OUT2 + u // UN, u % UN, w_out2, kt, n * NW)

            def pair_loads(g, col):
                for w in (w_gate2, w_up2):
                    for j in range(UN):
                        load_unit(sp, g, j, w, UK * j, col)
                    g = g + 1

            for c in range(CH2_FIRST):
                pair_loads(G_PAIR0 + 2 * c, c * NW)
            for n in range(UN):
                for k in range(CH2_FIRST):
                    u = n * CH2_FIRST + k
                    load_unit(sp, G_PAIR0 + 2 * CH2_FIRST + u // UN, u % UN, w_dn2, UK * k, n * NW)
            with sp.Fori(0, 2) as i:
                for c in range(CH2_LOOP):
                    pair_loads(i * LOOP2_RUNS + (G_LOOP2 + 2 * c), i * (CH2_LOOP * NW) + (CH2_FIRST + c) * NW)
                for n in range(UN):
                    for j in range(UN):
                        rows = w_dn2[:, bass.ds(i * (CH2_LOOP * CT) + CH2_FIRST * CT, CH2_LOOP * CT)]
                        load_unit(sp, i * LOOP2_RUNS + (G_LOOP2 + 2 * CH2_LOOP + n), j, rows, UK * j, n * NW)

            for n in range(UN):
                for m in range(MT):
                    sp.wait_ge(read_dve, (READERS.count("D") - UN + n) * MT + m + 1)
                    sp.dma_start(out[0, m * P:(m + 1) * P, chunk(n)], xres[:, m, chunk(n)]).then_inc(stored, 16)
            sp.wait_ge(stored, UN * MT * 16)

        @block.gpsimd
        def _(pool):
            own = Chain(pool, pool_own)
            n0 = own.mark(pool.memset(ident[:, :], 0.0))
            pool.memset(ones[:, :], 1.0).then_inc(consts, 1)
            n1 = own.mark(pool.memset(tri[:, :], 1.0))
            n2 = own.mark(pool.memset(mask[:, :], 0.0))
            own.need(n0)
            pool.affine_select(out=ident[:, :], in_=ident[:, :], compare_op=ALU.not_equal, fill=1.0, base=0,
                               pattern=[[-1, P]], channel_multiplier=1).then_inc(consts, 1)
            own.need(n1)
            pool.affine_select(out=tri[:, :], in_=tri[:, :], compare_op=ALU.is_ge, fill=0.0, base=0,
                               pattern=[[1, P]], channel_multiplier=-1).then_inc(consts, 1)
            own.need(n2)
            pool.affine_select(out=mask[:, P:T], in_=mask[:, P:T], compare_op=ALU.is_ge, fill=NEG, base=0,
                               pattern=[[-1, P]], channel_multiplier=1).then_inc(consts, 1)
            pool.memset(wr_sb[:, :, :], 0.0).then_inc(pads, 1)
            pool.memset(wi_sb[:, :, :], 0.0).then_inc(pads, 1)
            pool.memset(xaT[:, :, 0:LP], 0.0).then_inc(pads, 1)
            pool.memset(xpT[:, :, 0:PP], 0.0).then_inc(pads, 1)
            pool.memset(zT[:, :, 0:SP_], 0.0).then_inc(pads, 1)
            pool.memset(q_aug[:, :, HD + 1:AUG], 1.0).then_inc(pads, 1)
            pool.memset(k_aug[:, :, HD:HD + 1], 1.0).then_inc(pads, 1)
            pool.iota(steps[:, :], pattern=[[1, 16]], base=1, channel_multiplier=0).then_inc(pads, 1)

            pool.wait_ge(side_read, 4)
            pool.wait_ge(u_ready, CT)
            pool.wait_ge(rc_ready, 1)
            for g in range(CT):
                src, dst, width = xpT[:, g, :], pool_a, 1
                while width < 2 << g:
                    lo = 2 * width - 1
                    own.done(pool.tensor_tensor(dst[:, lo:], src[:, lo:], src[:, lo - width:PP + T - width], ALU.add))
                    src, dst, width = dst[:, :], (pool_b if dst is pool_a else pool_a), 2 * width
                head = own.mark(pool.tensor_tensor(dst[:, PP:PP + 16], src[:, PP:PP + 16], recip_count[:, g, :], ALU.mult))
                own.need(head)
                own.done(pool.tensor_scalar(dst[:, PP + 16:], src[:, PP + 16:], 1.0 / (2 << g), 1.0, ALU.mult, ALU.mult))
                pool.tensor_tensor(xpT[:, g, PP:], dst[:, PP:], xpT[:, g, PP:], ALU.subtract).then_inc(pooled, 1)
                pool.wait_ge(pooled, g + 1)

            pool.wait_ge(a_ready, CT)
            own.done(pool.tensor_tensor(lru_om[:, :, :], lru_r[:, :, :], lru_r[:, :, :], ALU.mult))
            pool.tensor_scalar(lru_om[:, :, :], lru_om[:, :, :], -1.0, 1.0, ALU.mult, ALU.add).then_inc(asq_ready, 1)
            pool.wait_ge(g_ready, CT)
            pool.tensor_tensor(lru_g[:, :, :], lru_g[:, :, :], lru_u[:, :, :], ALU.mult).then_inc(gu_ready, 1)

            def head_squares(before):
                pool.wait_ge(read_act, readers_before(HEAD1.index(IN_Q) + before + 1, "A") * MT)
                pool.tensor_tensor(lru_om[:, :, :].rearrange("p c t -> p (c t)"),
                                   stage[:, :, :].rearrange("p m n -> p (m n)"),
                                   stage[:, :, :].rearrange("p m n -> p (m n)"), ALU.mult).then_inc(head_sq, 1)

            pool.wait_ge(h_ready, CT)
            head_squares(0)
            pool.wait_ge(sc_ready, CT)
            pool.wait_ge(side_read, 8)
            pool.tensor_tensor(lru_z[:, :, :], lru_z[:, :, :], gbT[:, :, :], ALU.mult).then_inc(sc_gated, 1)
            pool.wait_ge(head_sum, 1)
            head_squares(1)

            def merge(n):
                for k in range(1, NB):
                    run = R_GATE0 + n * 2 * NB + NB + k
                    pool.wait_ge(read_dve, readers_before(run + 1, "D") * MT)
                    if k > 1:
                        pool.wait_ge(merged_ready, n * (NB - 1) + k - 1)
                    pool.tensor_tensor(xres[:, :, chunk(n)], xres[:, :, chunk(n)], stage[:, :, :],
                                       ALU.add).then_inc(merged_ready, 1)

            for n in range(UN):
                merge(n)

            def gained(run, n, gain=gainB):
                pool.wait_ge(read_dve, readers_before(run + 1, "D") * MT)
                for m in range(MT):
                    pool.tensor_tensor(stage[:, m, :], xres[:, m, chunk(n)], gain[:, chunk(n)],
                                       ALU.mult).then_inc(staged, 1)

            def squares(run, i=0):
                for m in range(MT):
                    pool.wait_ge(read_act, i * (UN * MT) + readers_before(run, "A") * MT + m + 1)
                    pool.tensor_tensor(stage[:, m, :], stage[:, m, :], stage[:, m, :], ALU.mult).then_inc(staged, 1)

            pool.wait_ge(gain_in[0], 16)
            for n in range(UN):
                gained(R_OUT + n, n)
            for c in range(UN):
                squares(R_UP0 + c)
            with pool.Fori(0, 3) as i:
                for c in range(UN):
                    squares(R_DLOOP + UN + c, i)

            pool.wait_ge(gain_in[1], 16)
            for n in range(UN):
                gained(R_DLAST + n, n)

            pool.memset(hT[:, :, 0:CP], 0.0).then_inc(pads2, 1)
            n0 = own.mark(pool.memset(win_mask[:, :], 0.0))
            pool.iota(dist[:, 0, :], pattern=[[-1, P]], base=NW, channel_multiplier=1).then_inc(masks_raw, 1)
            pool.iota(dist[:, 1, :], pattern=[[-1, P]], base=NW, channel_multiplier=1).then_inc(masks_raw, 1)
            own.need(n0)
            pool.affine_select(out=win_mask[:, 0:P], in_=win_mask[:, 0:P], compare_op=ALU.is_ge, fill=NEG, base=-1,
                               pattern=[[1, P]], channel_multiplier=-1).then_inc(masks_ready, 1)
            pool.affine_select(out=win_mask[:, P:T], in_=win_mask[:, P:T], compare_op=ALU.is_ge, fill=NEG, base=0,
                               pattern=[[-1, P]], channel_multiplier=1).then_inc(masks_ready, 1)
            pool.wait_ge(mults_ready, 2)
            pool.affine_select(out=dil_mask[:, P:T], in_=near[:, :], compare_op=ALU.is_ge, fill=NEG, base=0,
                               pattern=[[-1, P]], channel_multiplier=1).then_inc(masks_ready, 1)
            pool.wait_ge(masks_ready, 3)
            pool.affine_select(out=near[:, :], in_=near[:, :], compare_op=ALU.is_ge, fill=0.0, base=0,
                               pattern=[[1, P]], channel_multiplier=-1).then_inc(masks_ready, 1)
            pool.affine_select(out=far[:, :], in_=far[:, :], compare_op=ALU.is_ge, fill=0.0, base=-1,
                               pattern=[[-1, P]], channel_multiplier=1).then_inc(masks_ready, 1)
            pool.wait_ge(masks_ready, 5)
            pool.tensor_tensor(dil_mask[:, 0:P], near[:, :], far[:, :], ALU.add).then_inc(masks_ready, 1)

            def head2_squares(n):
                run, src, _, _, width = NORMS2[n]
                pool.wait_ge(read_act, readers_before(R_HEAD2 + run + 1, "A") * MT)
                if n:
                    pool.wait_ge(h2_sum, n)
                pool.tensor_tensor(squares2[:, :, 0:width], src, src, ALU.mult).then_inc(h2_sq, 1)

            def head2_gain(n):
                _, src, gain, dst, width = NORMS2[n]
                pool.wait_ge(h2_scaled, n + 1)
                g = bcast[:, gain:gain + HD].unsqueeze(1).to_broadcast([P, width // HD, HD])
                for m in range(MT):
                    x = src[:, m, :].rearrange("p (h d) -> p h d", d=HD)
                    for o in dst(m):
                        pool.tensor_tensor(o, x, g, ALU.mult).then_inc(h2_gained, 1)

            pool.wait_ge(read_act, readers_before(R_HEAD2 + 2, "A") * MT)
            pool.tensor_tensor(stage[:, :, :], u_sb[:, :, :], sig_sb[:, :, :], ALU.mult).then_inc(glu_ready, 1)
            pool.wait_ge(tp_free[0], 1)
            pool.wait_ge(tp_free[1], 1)
            pool.wait_ge(pads2, 1)
            for c in (2, 3):
                pool.tensor_scalar(yT[:, c, :], hT[:, c, 0:T], par[:, c, R_CONV2:R_CONV2 + 1],
                                   par[:, c, R_CONV2B:R_CONV2B + 1], ALU.mult, ALU.add).then_inc(tap_first, 1)

            def add_taps(k0, k1):
                for k in range(k0, k1):
                    for c in (2, 3):
                        r, product = tap_product(k, c)
                        pool.wait_ge(tap_made, r + 1)
                        if k == 1:
                            pool.wait_ge(tap_first, 2)
                        else:
                            pool.wait_ge(tap_added, r - 1)
                        pool.tensor_tensor(yT[:, c, :], yT[:, c, :], product, ALU.add).then_inc(tap_added, 1)

            add_taps(1, 6)
            head2_squares(0)
            add_taps(6, 8)
            head2_gain(0)
            head2_squares(1)
            add_taps(8, 18)
            head2_gain(1)
            add_taps(18, 23)
            head2_squares(2)
            add_taps(23, CONV_TAPS)
            head2_gain(2)
            head2_squares(3)
            head2_gain(3)
            head2_squares(4)
            head2_gain(4)

            pool.wait_ge(gain_in[2], 16)
            for n in range(UN):
                if n:
                    pool.wait_ge(turned, T_XN4 + n * MT)
                gained(R_OUT2 + 2 * UN + n, n, gain2)

        @block.scalar
        def _(act):
            def evac(run, out, func=ACT.Copy, done=None, cols=NW):
                act.wait_ge(units_used, UN * (run + 1) if done is None else done)
                for m in range(MT):
                    act.activation(out(m), acc[:, run % 2, m, 0:cols], func, scale=rstd[:, m:m + 1]).then_inc(read_act, 1)

            def relu_evac(run, done):
                evac(run, lambda m: stage[:, m, :], ACT.Relu, done)

            def side_copy(n, out):
                act.wait_ge(side_turned, n + 1)
                rows = out.shape[0]
                act.activation(out, tp[0:rows, n % 2].rearrange("p (c t) -> p c t", c=CT), ACT.Copy).then_inc(side_read, 1)

            def channel_copy(n, dst, pad):
                for m in range(MT):
                    side_copy(n + m, dst[:, :, pad + m * P:pad + (m + 1) * P])

            def norm_squares(norm, n):
                act.wait_ge(x_in[n], 32)
                if norm or n:
                    act.wait_ge(sq_done, (norm * UN + n) * MT)
                for m in range(MT):
                    act.activation(junk[:, m, :], xres[:, m, chunk(n)], ACT.Square,
                                   accum_out=sumsq[:, m, n:n + 1]).then_inc(sq_done, 1)

            def norm_root(norm):
                act.wait_ge(msq_done, norm + 1)
                act.activation(rms[:, :], msq[:, :], ACT.Sqrt).then_inc(rms_done, 1)

            def head_root_of(n):
                act.wait_ge(head_sum, n + 1)
                act.activation(hroot[:, :], hsum[:, :], ACT.Sqrt).then_inc(head_root, 1)

            def exps(a, g):
                tile, heads = GROUPS[g]
                width = (tile + 1) * P
                act.wait_ge(max_ready, a.first + g + 1)
                if a.first + g >= 2:
                    act.wait_ge(p_turned, a.first + g - 1)
                for i, h in enumerate(heads):
                    c = first_column(g) + i
                    act.activation(a.probs[:, g % 2, i * width:(i + 1) * width], a.scores[:, i * width:(i + 1) * width],
                                   ACT.Exp, bias=a.negmax[:, c:c + 1], accum_out=a.rowsum[:, c:c + 1]).then_inc(p_ready, 1)

            def copy_probsT(a, g):
                act.wait_ge(p_turned, a.first + g + 1)
                if a.first + g:
                    act.wait_ge(pv_done, a.first + g)
                act.activation(a.probsT[:, :], sd[:, 1, :], ACT.Copy).then_inc(pT_ready, 1)

            def attention_side(a, s):
                s = s - A0[a.set]
                if 2 <= s < 2 + len(GROUPS):
                    exps(a, s - 2)
                if 4 <= s < 4 + len(GROUPS):
                    copy_probsT(a, s - 4)
                if a.sinks and s in (5, 9):
                    tile = int(s == 9)
                    act.wait_ge(sink_arg, sink_step(a.set, tile))
                    e = a.sinks[1][:, tile * HEADS:(tile + 1) * HEADS]
                    act.activation(e, e, ACT.Exp).then_inc(sink_exp, 1)

            for j in range(UN):
                if j == 0:
                    turned_hi(act, T_XN, opA_hi, 0)
                hi_unit(act, 0, j)
                if j:
                    turned_hi(act, T_XN + j * MT, opA_hi, j * CT)
                norm_squares(0, j)
            norm_root(0)

            def side(s):
                if s == 3:
                    act.wait_ge(f_in, 16)
                    act.activation(f_hi[:, :, :], f_raw[:, :, :], ACT.Copy).then_inc(f_split, 1)
                if s == 4:
                    act.wait_ge(rstd_done, 1)
                    evac(0, lambda m: stage[:, m, :])
                    act.wait_ge(par_turned, 1)
                    act.activation(par[:, :, :], sd[:, 0, 0:CT * NPAR].rearrange("p (c r) -> p c r", c=CT),
                                   ACT.Copy).then_inc(par_ready, 1)
                if s == 5:
                    act.wait_ge(f_mm, 1)
                    act.activation(f_heads[0:HEADS, :], sd[0:HEADS, 1, 0:T], ACT.Copy).then_inc(f_rows, 1)
                if s == 6:
                    act.wait_ge(f_mm, 2)
                    for m in range(MT):
                        act.activation(ftok[:, m * HEADS:(m + 1) * HEADS], sd[:, 1, T + m * HEADS:T + (m + 1) * HEADS],
                                       ACT.Copy, scale=rstd[:, m:m + 1]).then_inc(f_tok, 1)
                    channel_copy(0, xaT, LP)
                if s == 8:
                    evac(1, lambda m: stage[:, m, :])
                    act.wait_ge(f_abs, 1)
                    act.activation(sp_e[:, :], sp_abs[:, :], ACT.Exp, scale=-1.0).then_inc(f_exp, 1)
                    act.wait_ge(lam_abs, 1)
                    act.activation(l_e[:, :], l_abs[:, :], ACT.Exp, scale=-1.0).then_inc(lam_exp, 1)
                if s == 10:
                    channel_copy(2, xpT, PP)
                if s == 12:
                    evac(2, lambda m: gc_sb[:, m, :])
                if s == 13:
                    act.wait_ge(lru_mm, 1)
                    for c in range(CT):
                        act.activation(lru_r[:, c, :], sd[:, c // 2, (c % 2) * T:(c % 2 + 1) * T], ACT.Sigmoid,
                                       bias=par[:, c, R_BR:R_BR + 1]).then_inc(r_ready, 1)
                if s == 16:
                    act.wait_ge(lru_mm, 2)
                    for c in range(CT):
                        act.activation(lru_g[:, c, :], sd[:, c // 2, (c % 2) * T:(c % 2 + 1) * T], ACT.Sigmoid,
                                       bias=par[:, c, R_BI:R_BI + 1]).then_inc(g_ready, 1)
                if s == 17:
                    act.wait_ge(z_ready, CT)
                    for c in range(CT):
                        act.activation(lru_r[:, c, :], lru_r[:, c, :], ACT.Exp, scale=l_c[:, c:c + 1]).then_inc(a_ready, 1)
                if s == 18:
                    channel_copy(4, zT, SP_)
                if s == 20:
                    evac(4, lambda m: stage[:, m, :])
                if s == 22:
                    act.wait_ge(om_ready, 1)
                    act.activation(lru_om[:, :, :], lru_om[:, :, :], ACT.Sqrt).then_inc(root_ready, 1)
                    channel_copy(6, gbT, 0)
                if s == 24:
                    evac(5, lambda m: stage[:, m, :])
                if s == 25:
                    act.wait_ge(h_ready, CT)
                    act.activation(opB_hi[:, 0:CT, :], lru_u[:, :, :], ACT.Copy).then_inc(y_hi, 1)
                if s == 26:
                    head_root_of(0)
                    act.wait_ge(pool_mm, 1)
                    for c in range(CT):
                        act.activation(opB_hi[:, CT + c, :], sd[:, c // 2, (c % 2) * T:(c % 2 + 1) * T], ACT.Copy,
                                       scale=par[:, c, R_PSCALE:R_PSCALE + 1]).then_inc(y_hi, 1)
                if s == 28:
                    act.wait_ge(head_scaled, 1)
                    evac(6, lambda m: stage[:, m, :])
                if s == 30:
                    head_root_of(1)
                if s == 31:
                    act.wait_ge(sc_gated, 1)
                    act.activation(opB_hi[:, 2 * CT:3 * CT, :], lru_z[:, :, :], ACT.Copy).then_inc(y_hi, 1)
                if s == 32:
                    evac(7, lambda m: v_sb[:, m, :])
                if s in (33, 34):
                    if s == 33:
                        act.wait_ge(y_lo, 6)
                    m = s - 33
                    for half in range(2):
                        side_copy(8 + 2 * m + half, qT[0:AUG, half * CT:(half + 1) * CT, m * P:(m + 1) * P])
                if s in (35, 36):
                    m = s - 35
                    for half in range(2):
                        side_copy(12 + 2 * m + half, kT[0:AUG, half * CT:(half + 1) * CT, m * P:(m + 1) * P])
                attention_side(attentions[0], s)
                if s == 36:
                    evac(8, lambda m: gates[:, 0, m, :], ACT.Sigmoid)
                if s in (40, 44):
                    k = (s - 36) // 4
                    evac(R_GATE0 + k, lambda m: gates[:, k, m, :], ACT.Sigmoid)
                if s == 48:
                    evac(R_GATE0 + 3, lambda m: gates[:, 3, m, :], ACT.Sigmoid)
                    turned_hi(act, T_YD, opB_hi, 3 * CT)

            side(3)
            for g in range(1, G_LOOP):
                for j in range(UN):
                    hi_unit(act, g, j)
                    side(g * UN + j)
            def merged_hi(c):
                turned_hi(act, T_MERGED + c * MT, opA_hi, c * CT)
                act.dma_start(xres[:, :, chunk(c)],
                              t["x"][0].rearrange("(m p) d -> p m d", p=P)[:, :, chunk(c)]).then_inc(x_back[c], 16)
                if c == 0:
                    act.dma_start(gainB[:, :], t["norm_mlp_g"][0].partition_broadcast(P)).then_inc(gain_in[0], 16)

            def gate_turn(i, last=False):
                for k in range(NB + 1):
                    for j in range(UN):
                        hi_unit(act, G_LOOP + k + i * 5, j)
                        if k and j == 0:
                            evac(R_LOOP + k - 1, lambda m: gates[:, k - 1, m, :], ACT.Sigmoid,
                                 done=i * (5 * UN) + (G_LOOP + k) * UN)
                        if last and k == NB and j >= 2:
                            merged_hi(j - 2)

            with act.Fori(0, 2) as i:
                gate_turn(i)
            gate_turn(2, last=True)
            for n in range(UN):
                for j in range(UN):
                    hi_unit(act, G_OUT + n, j)
                    if n == 0 and j in (0, 2):
                        merged_hi(2 + j // 2)
                    if n and j == 0:
                        act.wait_ge(read_dve, readers_before(R_OUT + n, "D") * MT)
                        norm_squares(1, n - 1)
                    if n and j == 2:
                        turned_hi(act, T_XN2 + (n - 1) * MT, opB_hi, (n - 1) * CT)

            for c in range(UN):
                for j in range(UN):
                    hi_unit(act, G_UP0 + c, j)
                    if j == 0 and c == 0:
                        act.wait_ge(read_dve, readers_before(R_UP0, "D") * MT)
                        norm_squares(1, 3)
                        norm_root(1)
                    if j == 0 and c == 1:
                        act.wait_ge(rstd_done, 2)
                    if j == 0 and c:
                        relu_evac(R_UP0 + c - 1, (G_UP0 + c) * UN)
                    if j == 3 and c == 1:
                        act.wait_ge(staged, 4 * MT)
                        act.dma_start(gainB[:, :], t["norm1_g_2"][0].partition_broadcast(P)).then_inc(gain_in[1], 16)
                    if j == 2 and c == 0:
                        turned_hi(act, T_XN2 + 3 * MT, opB_hi, 3 * CT)
                    if j == 2 and c:
                        turned_hi(act, T_HID + (c - 1) * MT, opA_hi, (c - 1) * CT)
            with act.Fori(0, 3) as i:
                for r in range(2 * UN):
                    g = i * 8 + (G_DLOOP + r)
                    for j in range(UN):
                        hi_unit(act, g, j)
                        up = UN - 1 if r == 0 else r - UN - 1
                        if up >= 0 and j == 0:
                            relu_evac(R_DLOOP + r - 1, i * (8 * UN) + (G_DLOOP + r) * UN)
                        if up >= 0 and j == 2:
                            before = T_HID + (up if r == 0 else UN + up) * MT
                            turned_hi(act, i * (UN * MT) + before, opA_hi, up * CT)
            for n in range(UN):
                for j in range(UN):
                    hi_unit(act, G_DLAST + n, j)
                    if n == 0 and j == 0:
                        relu_evac(R_DLAST - 1, G_DLAST * UN)
                    if n == 0 and j == 2:
                        turned_hi(act, T_HID + (4 * UN - 1) * MT, opA_hi, 3 * CT)
                    if n and j == 0:
                        act.wait_ge(read_dve, readers_before(R_DLAST + n, "D") * MT)
                        norm_squares(2, n - 1)
                    if n and j == 2:
                        turned_hi(act, T_XN3 + (n - 1) * MT, opB_hi, (n - 1) * CT)

            def evac2(r, out, func=ACT.Copy):
                evac(R_HEAD2 + r, out, func, (G_HEAD2 + r + 1) * UN, head2_cols(HEAD2[r]))

            def tp_copy(name, out, func=ACT.Copy):
                b, n = tp_use(name)
                act.wait_ge(tp_full[b], n + 1)
                act.activation(out, tp[:, b].rearrange("p (c t) -> p c t", c=CT), func).then_inc(tp_free[b], 1)

            def mix_turned_hi(name, a, m):
                b, n = tp_use(name)
                act.wait_ge(tp_full[b], n + 1)
                kt = MIX_KT[a]
                act.activation(opA_hi[:, kt:kt + CT, m * P:(m + 1) * P], tp[:, b].rearrange("p (c t) -> p c t", c=CT),
                               ACT.Copy).then_inc(mix_hi, 1)

            EVAC2 = [lambda m: u_sb[:, m, :], lambda m: sig_sb[:, m, :], lambda m: q_tok[:, 0, m, :],
                     lambda m: kv_tok[:, m, :], lambda m: q_tok[:, 1, m, :], lambda m: q_tok[:, 0, m, :],
                     lambda m: k_tok[:, m, :], lambda m: vd_sb[:, m, :]]

            def side2(s):
                if s == 0:
                    act.wait_ge(read_dve, readers_before(R_HEAD2, "D") * MT)
                    norm_squares(2, 3)
                    norm_root(2)
                if s == 2:
                    turned_hi(act, T_XN3 + 3 * MT, opB_hi, 3 * CT)
                if s == 10:
                    tp_copy("h0", hT[:, :, CP:CP + P])
                    tp_copy("h1", hT[:, :, CP + P:CP + T])
                if s - 2 in TURNS2:
                    name, _, _, m = TURNS2[s - 2]
                    tp_copy(name, TURNED2[s - 2][:, :, m * P:(m + 1) * P])
                if s == 21:
                    tp_copy("k1", kwT[:, :, :].rearrange("p v (m t) -> p v m t", m=MT).rearrange("p v m t -> p (v m) t"))
                if s == 25:
                    tp_copy("y0", y_tok[:, 0, :].rearrange("p (c t) -> p c t", c=CT))
                    tp_copy("y1", y_tok[:, 1, :].rearrange("p (c t) -> p c t", c=CT))
                if s in (30, 31):
                    tp_copy(f"n{s - 30}", silT[:, :, (s - 30) * P:(s - 29) * P])
                if s - 1 in MID_TURNS2:
                    name, _, _, m = MID_TURNS2[s - 1]
                    tp_copy(name, TURNED2[s - 1][:, :, m * P:(m + 1) * P])
                if s == 31:
                    b, n = tp_use("n1")
                    act.wait_ge(tp_free[b], n + 1)
                    for c in range(CT):
                        act.activation(silT[:, c, :], silT[:, c, :], ACT.Silu, bias=par[:, c, R_LNB:R_LNB + 1],
                                       scale=par[:, c, R_LNG:R_LNG + 1]).then_inc(silu_done, 1)
                    act.wait_ge(silu_done, CT)
                if s == 31:
                    act.activation(opA_hi[:, K_CONV:K_CONV + CT, :], silT[:, :, :], ACT.Copy).then_inc(conf_hi, 1)
                if s == 34:
                    act.wait_ge(conf_lo, 1)
                    act.dma_start(gain2[:, :], t["norm2_g_2"][0].partition_broadcast(P)).then_inc(gain_in[2], 16)
                if s in (14, 18, 22, 26, 30):
                    n = (s - 14) // 4
                    act.wait_ge(h2_sum, n + 1)
                    act.activation(hroot[:, :], hsum[:, :], ACT.Sqrt).then_inc(h2_root, 1)
                if s == 27:
                    act.wait_ge(ln_var, 1)
                    act.activation(bn_root[:, :], bn_var[:, :], ACT.Sqrt).then_inc(ln_root, 1)
                if 10 <= s < 9 + len(TAPS_ACT):
                    for k in range(TAPS_ACT[s - 10], TAPS_ACT[s - 9]):
                        for c in (2, 3):
                            r, product = tap_product(k, c)
                            if r == 0:
                                for b in range(2):
                                    act.wait_ge(tp_free[b], 1)
                                act.wait_ge(pads2, 1)
                            if r >= TAPS:
                                act.wait_ge(tap_added, r - TAPS + 1)
                            act.activation(product, hT[:, c, k:k + T], ACT.Copy,
                                           scale=par[:, c, R_CONV2 + k:R_CONV2 + k + 1]).then_inc(tap_made, 1)
                if s - 2 in MIX2:
                    mix_turned_hi(*MIX2[s - 2])
                for a in attentions[1:]:
                    attention_side(a, s)
                if s % UN == 0 and 0 < s <= 8 * UN:
                    r = s // UN - 1
                    if r == 0:
                        act.wait_ge(rstd_done, 3)
                    if r == 1:
                        act.wait_ge(sq_done, 3 * UN * MT)
                    evac2(r, EVAC2[r], ACT.Sigmoid if r == 1 else ACT.Copy)
                if s == LAST_MIX + 1:
                    mix_turned_hi("mix31", 3, 1)
                if 47 <= s <= 50:
                    turned_hi(act, T_XN4 + (s - 47) * MT, opB_hi, (s - 47) * CT)
                if 46 <= s <= 49:
                    n = s - 46
                    act.wait_ge(read_dve, readers_before(R_OUT2 + 2 * UN + n + 1, "D") * MT)
                    norm_squares(3, n)
                if s == 50:
                    norm_root(3)

            for u in range(12 * UN):
                hi_unit(act, G_HEAD2 + u // UN, u % UN, head2_cols(HEAD2[u // UN]) if u < 8 * UN else NW)
                side2(u)

            def gate_evac(run, done, i=0):
                act.wait_ge(read_dve, i * (2 * CH2_LOOP * MT) + readers_before(run, "D") * MT)
                evac(run, lambda m: silu_gate[:, m, :], ACT.Silu, done)

            for r in range(2 * CH2_FIRST):
                for j in range(UN):
                    hi_unit(act, G_PAIR0 + r, j)
                    if r == 0:
                        side2(12 * UN + j)
                    if r == 1 and j == 0:
                        act.wait_ge(rstd_done, 4)
                    if r % 2 and j == 0:
                        gate_evac(R_PAIR0 + r - 1, (G_PAIR0 + r) * UN)
                    if r and r % 2 == 0 and j == 2:
                        turned_hi(act, T_HID2 + (r // 2 - 1) * MT, opA_hi, (r // 2 - 1) * CT)
            for u in range(CH2_FIRST * UN):
                hi_unit(act, G_PAIR0 + 2 * CH2_FIRST + u // UN, u % UN)
                if u == 2:
                    turned_hi(act, T_HID2 + (CH2_FIRST - 1) * MT, opA_hi, (CH2_FIRST - 1) * CT)
            with act.Fori(0, 2) as i:
                for r in range(LOOP2_RUNS):
                    for j in range(UN):
                        hi_unit(act, i * LOOP2_RUNS + (G_LOOP2 + r), j)
                        c = r // 2
                        if r % 2 and c < CH2_LOOP and j == 0:
                            gate_evac(R_LOOP2 + r - 1, i * LOOP2_UNITS + (G_LOOP2 + r) * UN, i)
                        if r % 2 == 0 and 1 <= c <= CH2_LOOP and j == 2:
                            before = T_HID2 + (CH2_FIRST + c - 1) * MT
                            turned_hi(act, i * (CH2_LOOP * MT) + before, opA_hi, (c - 1) * CT)

        @block.tensor
        def _(pe):
            def products(group, run, j, hi, lo, kt, mid=None):
                if j == 0:
                    pair_free(pe, run)
                unit_products(pe, group, j, run % 2, hi, lo, kt, j == 0, j == UN - 1, mid=mid)

            def stage_operand(c, before, staged_by):
                pe.wait_ge(staged, staged_by)
                turn(pe, lambda m, b: stage[:, m, b * P:(b + 1) * P], before)

            def side_turn(n, blocks):
                if n < 2:
                    pe.wait_ge(op_lo, T_YD)
                else:
                    pe.wait_ge(side_read, n - 1)
                for c, b in enumerate(blocks):
                    w = b.shape[1]
                    tr = pe.transpose(tp[0:w, n % 2, c * P:(c + 1) * P], b, ident[:, :])
                tr.then_inc(side_turned, 1)

            def stage_turn(n):
                for m in range(MT):
                    side_turn(n + m, [stage[:, m, c * P:(c + 1) * P] for c in range(CT)])

            def aug_turn(n, aug, m):
                for half in range(2):
                    side_turn(n + half, [aug[:, m * HEADS + half * CT + c, :] for c in range(CT)])

            def lru_products(w):
                for c in range(CT):
                    mm = pe.matmul(sd[:, c // 2, (c % 2) * T:(c % 2 + 1) * T], w[:, c, :], lru_u[:, c, :],
                                   start=True, stop=True)
                mm.then_inc(lru_mm, 1)

            def qk(a, g):
                tile, heads = GROUPS[g]
                width = (tile + 1) * P
                if a.first + g:
                    pe.wait_ge(s_ready, a.first + g)
                for i, h in enumerate(heads):
                    mm = pe.matmul(sd[:, 0, i * width:(i + 1) * width], a.q(h)[:, tile * P:(tile + 1) * P],
                                   a.k(h)[:, 0:width], start=True, stop=True)
                mm.then_inc(qk_done, 1)

            def turn_probs(a, g):
                pe.wait_ge(p_ready, a.cols + first_column(g) + len(GROUPS[g][1]))
                if a.first + g:
                    pe.wait_ge(pT_ready, a.first + g)
                for b in range(CT):
                    tr = pe.transpose(sd[:, 1, b * P:(b + 1) * P], a.probs[:, g % 2, b * P:(b + 1) * P], ident[:, :])
                tr.then_inc(p_turned, 1)

            def pv(a, g):
                tile = GROUPS[g][0]
                pe.wait_ge(pT_ready, a.first + g + 1)
                for b, (h, kt) in enumerate(blocks_of(GROUPS[g])):
                    mm = pe.matmul(a.out(tile)[:, h * HD:(h + 1) * HD], a.probsT[:, b * P:(b + 1) * P],
                                   a.v(h, kt), start=kt == 0, stop=kt == tile)
                mm.then_inc(pv_done, 1)

            def attention_side(a, s, qk_wait, pv_wait):
                s = s - A0[a.set]
                if 0 <= s < len(GROUPS):
                    qk_wait(GROUPS[s][0])
                    qk(a, s)
                if 4 <= s < 4 + len(GROUPS):
                    pv_wait(s - 4)
                    pv(a, s - 4)

            def attention_mid(a, s):
                if 3 <= s - A0[a.set] < 3 + len(GROUPS):
                    turn_probs(a, s - A0[a.set] - 3)

            def side(s):
                if s == 2:
                    pe.wait_ge(rows_in, 11 * 16)
                    for c in range(CT):
                        tr = pe.transpose(sd[:, 0, c * NPAR:(c + 1) * NPAR], rows_par[0:NPAR, c * P:(c + 1) * P],
                                          ident[0:NPAR, 0:NPAR])
                    tr.then_inc(par_turned, 1)
                if s == 3:
                    pe.wait_ge(f_split, 2)
                    for kt in range(KT):
                        o = sd[0:HEADS, 1, 0:T]
                        pe.matmul(o, f_hi[:, kt, :], opA_hi[:, kt, :], start=kt == 0, stop=False)
                        pe.matmul(o, f_lo[:, kt, :], opA_hi[:, kt, :], start=False, stop=False)
                        mm = pe.matmul(o, f_hi[:, kt, :], opA_lo[:, kt, :], start=False, stop=kt == KT - 1)
                    mm.then_inc(f_mm, 1)
                if s == 4:
                    pe.wait_ge(f_rows, 1)
                    for m in range(MT):
                        tr = pe.transpose(sd[:, 1, T + m * HEADS:T + (m + 1) * HEADS], f_heads[0:HEADS, m * P:(m + 1) * P],
                                          ident[0:HEADS, 0:HEADS])
                    tr.then_inc(f_mm, 1)
                    pe.wait_ge(read_act, 2)
                    stage_turn(0)
                if s == 8:
                    pe.wait_ge(read_act, 4)
                    stage_turn(2)
                if s == 9:
                    pe.wait_ge(f_log, 1)
                    pe.matmul(sd[:, 1, 0:HEADS], tri[:, :], logf[:, 0:HEADS], start=True, stop=True)
                    pe.matmul(sd[:, 1, HEADS:2 * HEADS], tri[:, :], logf[:, HEADS:2 * HEADS], start=True, stop=False)
                    pe.matmul(sd[:, 1, HEADS:2 * HEADS], ones[:, :], logf[:, 0:HEADS],
                              start=False, stop=True).then_inc(cum_mm, 1)
                if s == 11:
                    pe.wait_ge(u_ready, CT)
                    pe.wait_ge(sw_in, 5 * 16)
                    pe.wait_ge(f_cum, 4)
                    lru_products(wr_sb)
                if s == 14:
                    pe.wait_ge(r_ready, CT)
                    lru_products(wi_sb)
                if s == 16:
                    pe.wait_ge(read_dve, 2)
                    stage_turn(4)
                if s == 20:
                    pe.wait_ge(read_act, 8)
                    stage_turn(6)
                if s == 24:
                    pe.wait_ge(pooled, CT)
                    pe.wait_ge(g_ready, CT)
                    for c in range(CT):
                        mm = pe.matmul(sd[:, c // 2, (c % 2) * T:(c % 2 + 1) * T], pw_sb[:, c, :],
                                       xpT[:, c, PP:], start=True, stop=True)
                    mm.then_inc(pool_mm, 1)
                if s in (31, 32):
                    pe.wait_ge(aug_done, 1)
                    aug_turn(8 + 2 * (s - 31), q_aug, s - 31)
                if s in (33, 34):
                    pe.wait_ge(aug_done, 2)
                    aug_turn(12 + 2 * (s - 33), k_aug, s - 33)
                attention_side(attentions[0], s,
                               lambda tile: pe.wait_ge(side_read, 14 + 2 * tile),
                               lambda g: pe.wait_ge(side_read, 16))
                if s == 47:
                    pe.wait_ge(o_ready, MT)
                    turn(pe, lambda m, c: stage[:, m, c * P:(c + 1) * P], T_YD)

            pe.wait_ge(consts, 4)

            def xn_turn(j):
                pe.wait_ge(xg_done, j + 1)
                turn(pe, lambda m, c: x_gained[:, m, j * NW + c * P:j * NW + (c + 1) * P], T_XN + j * MT)

            def xn_ready(j, before=T_XN):
                pe.wait_ge(op_lo, before + (j + 1) * MT)

            def mid(s):
                if s < UN - 1:
                    xn_turn(s + 1)
                attention_mid(attentions[0], s)

            xn_turn(0)
            for r in range(12):
                for j in range(UN):
                    if r == 0:
                        xn_ready(j)
                    products(r, r, j, opA_hi, opA_lo, UK * j, lambda: mid(r * UN + j))
                    side(r * UN + j)

            for k in range(NB):
                if k == 0:
                    pe.wait_ge(y_lo, 6)
                if k == NB - 1:
                    pe.wait_ge(op_lo, T_MERGED)
                pair_free(pe, R_GATE0 + NB + k)
                unit_products(pe, G_GATE0 + NB, k, k % 2, opB_hi, opB_lo, CT * k, True, True)
            def merged_turn(c):
                pe.wait_ge(merged_ready, (NB - 1) * (c + 1))
                turn(pe, lambda m, b: xres[:, m, c * NW + b * P:c * NW + (b + 1) * P], T_MERGED + c * MT)

            def gate_turn(i, last=False):
                for k in range(NB):
                    for j in range(UN):
                        if j == 0:
                            pair_free(pe, R_LOOP + k, i, NB, NB)
                        unit_products(pe, G_LOOP + k + i * 5, j, k % 2, opA_hi, opA_lo, UK * j, j == 0, j == UN - 1)
                for k in range(NB):
                    pair_free(pe, R_LOOP + NB + k, i, NB, NB)
                    unit_products(pe, G_LOOP + NB + i * 5, k, k % 2, opB_hi, opB_lo, CT * k, True, True)
                    if last and k < NB - 1:
                        merged_turn(k)

            with pe.Fori(0, 2) as i:
                gate_turn(i)
            gate_turn(2, last=True)
            for n in range(UN):
                for j in range(UN):
                    if n == 0:
                        xn_ready(j, T_MERGED)
                    products(G_OUT + n, R_OUT + n, j, opA_hi, opA_lo, UK * j)
                    if n == 0 and j == 0:
                        merged_turn(3)
                    if n and j == 0:
                        stage_operand(n - 1, T_XN2 + (n - 1) * MT, n * MT)
            for c in range(UN):
                for j in range(UN):
                    if c == 0:
                        xn_ready(j, T_XN2)
                    products(G_UP0 + c, R_UP0 + c, j, opB_hi, opB_lo, UK * j)
                    if j == 0:
                        if c == 0:
                            stage_operand(3, T_XN2 + 3 * MT, 4 * MT)
                        else:
                            stage_operand(c - 1, T_HID + (c - 1) * MT, (4 + c) * MT)
            with pe.Fori(0, 3) as i:
                for r in range(2 * UN):
                    down = r < UN
                    for j in range(UN):
                        if j == 0:
                            pair_free(pe, R_DLOOP + r, i, UN, UN)
                        if r == 0:
                            pe.wait_ge(op_lo, i * (UN * MT) + T_HID + (j + 1) * MT)
                        unit_products(pe, i * (2 * UN) + G_DLOOP + r, j, r % 2, opA_hi if down else opB_hi,
                                      opA_lo if down else opB_lo, UK * j, j == 0, j == UN - 1)
                        if j == 0 and r == 0:
                            stage_operand(3, i * (UN * MT) + (T_HID + 3 * MT), i * (UN * MT) + 8 * MT)
                        if j == 0 and r > UN:
                            c = r - UN - 1
                            stage_operand(c, i * (UN * MT) + (T_HID + (4 + c) * MT), i * (UN * MT) + (9 + c) * MT)
            for n in range(UN):
                for j in range(UN):
                    if n == 0:
                        xn_ready(j, T_HID + 12 * MT)
                    products(G_DLAST + n, R_DLAST + n, j, opA_hi, opA_lo, UK * j)
                    if n == 0 and j == 0:
                        stage_operand(3, T_HID + 15 * MT, 20 * MT)
                    if n and j == 0:
                        stage_operand(n - 1, T_XN3 + (n - 1) * MT, (20 + n) * MT)

            def tp_turn(name, blocks):
                b, n = tp_use(name)
                if n:
                    pe.wait_ge(tp_free[b], n)
                for c, x in enumerate(blocks):
                    tr = pe.transpose(tp[:, b, c * P:(c + 1) * P], x, ident[:, :])
                tr.then_inc(tp_full[b], 1)

            def tp_read(name):
                b, n = tp_use(name)
                pe.wait_ge(tp_free[b], n + 1)

            def quarters(x):
                return [x[:, c * P:(c + 1) * P] for c in range(CT)]

            def mix_turn(name, a, m):
                tp_read(f"o{a}{m}")
                tp_turn(name, quarters(stage[:, m, :]))

            def qk_turn(name, norm, src, m):
                pe.wait_ge(h2_gained, GAINED2[norm])
                tp_turn(name, quarters(src[:, m, :]))

            def qk_wait(a):
                names = {1: ("k1", "k1"), 2: ("q20", "q21"), 3: ("k30", "k31")}[a.set]
                return lambda tile: tp_read(names[tile])

            def pv_wait(a):
                def wait(g):
                    tile = GROUPS[g][0]
                    pe.wait_ge(tp_free[0], tp_use(f"o{a.set}{tile}")[1])
                    if a.set == 3:
                        pe.wait_ge(read_act, readers_before(R_HEAD2 + len(HEAD2), "A") * MT)
                return wait

            def side2(s):
                if s == 0:
                    stage_operand(3, T_XN3 + 3 * MT, 24 * MT)
                if s == 8:
                    pe.wait_ge(glu_ready, 1)
                    for m in range(MT):
                        tp_turn(f"h{m}", quarters(stage[:, m, :]))
                if s in TURNS2:
                    qk_turn(*TURNS2[s])
                if s == 19:
                    pe.wait_ge(h2_gained, GAINED2[1])
                    tp_turn("k1", [k_dup[:, m, v].rearrange("p d e -> p (d e)") for v in range(2) for m in range(MT)])
                if s == 23:
                    pe.wait_ge(conv_dve, 2)
                    pe.wait_ge(tap_added, 2 * (CONV_TAPS - 1))
                    for m in range(MT):
                        tp_turn(f"y{m}", [yT[:, c, m * P:(m + 1) * P] for c in range(CT)])
                if s in (28, 29):
                    pe.wait_ge(ln_done, s - 27)
                    tp_turn(f"n{s - 28}", quarters(y_tok[:, s - 28, :]))
                if s in MIX2:
                    mix_turn(*MIX2[s])
                for a in attentions[1:]:
                    attention_side(a, s, qk_wait(a), pv_wait(a))
                if 45 <= s < 49:
                    stage_operand(s - 45, T_XN4 + (s - 45) * MT, (25 + s - 45) * MT)

            def mid2(s):
                if s in MID_TURNS2:
                    qk_turn(*MID_TURNS2[s])
                if s == LAST_MIX:
                    mix_turn("mix31", 3, 1)
                for a in attentions[1:]:
                    attention_mid(a, s)

            for r, col in enumerate(HEAD2):
                for j in range(UN):
                    if r == 0:
                        xn_ready(j, T_XN3)
                    if j == 0:
                        pair_free(pe, R_HEAD2 + r)
                    unit_products(pe, G_HEAD2 + r, j, r % 2, opB_hi, opB_lo, UK * j, j == 0, j == UN - 1, head2_cols(col),
                                  lambda: mid2(r * UN + j))
                    side2(r * UN + j)
            for u, (kt, n, first, last) in enumerate(OUT2):
                run = R_OUT2 + (u - UN if u >= 2 * UN else n)
                if first:
                    pair_free(pe, run)
                if kt == K_CONV:
                    pe.wait_ge(conf_lo, 1)
                else:
                    tp_read({K_WIN0: "mix11", K_WIN1: "mix21", K_DIL: "mix31"}[kt])
                unit_products(pe, G_OUT2 + u // UN, u % UN, run % 2, opA_hi, opA_lo, kt, first, last,
                              mid=lambda: mid2(8 * UN + u))
                side2(8 * UN + u)

            def hidden_turn(before, run, i=0):
                pe.wait_ge(read_dve, i * (2 * CH2_LOOP * MT) + readers_before(run + 1, "D") * MT)
                turn(pe, lambda m, b: stage[:, m, b * P:(b + 1) * P], before)

            for r in range(2 * CH2_FIRST):
                for j in range(UN):
                    if r == 0:
                        xn_ready(j, T_XN4)
                    products(G_PAIR0 + r, R_PAIR0 + r, j, opB_hi, opB_lo, UK * j)
                    if r == 0:
                        side2(12 * UN + j)
                    if r and r % 2 == 0 and j == 0:
                        hidden_turn(T_HID2 + (r // 2 - 1) * MT, R_PAIR0 + r - 1)
            for n in range(UN):
                for k in range(CH2_FIRST):
                    u = n * CH2_FIRST + k
                    if n == 0:
                        xn_ready(k, T_HID2)
                    if k == 0:
                        pair_free(pe, R_DOWN0 + n)
                    unit_products(pe, G_PAIR0 + 2 * CH2_FIRST + u // UN, u % UN, n % 2, opA_hi, opA_lo, UK * k,
                                  k == 0, k == CH2_FIRST - 1)
                    if u == 0:
                        hidden_turn(T_HID2 + (CH2_FIRST - 1) * MT, R_DOWN0 - 1)
            with pe.Fori(0, 2) as i:
                for r in range(LOOP2_RUNS):
                    pairs = r < 2 * CH2_LOOP
                    c = r // 2
                    before = T_HID2 + CH2_FIRST * MT
                    for j in range(UN):
                        if j == 0:
                            pair_free(pe, R_LOOP2 + r, i, CH2_LOOP, 2 * CH2_LOOP)
                        if r == 2 * CH2_LOOP:
                            pe.wait_ge(op_lo, i * (CH2_LOOP * MT) + before + (j + 1) * MT)
                        unit_products(pe, i * LOOP2_RUNS + (G_LOOP2 + r), j, r % 2, opB_hi if pairs else opA_hi,
                                      opB_lo if pairs else opA_lo, UK * j, j == 0, j == UN - 1)
                        if r % 2 == 0 and 1 <= c <= CH2_LOOP and j == 0:
                            hidden_turn(i * (CH2_LOOP * MT) + before + (c - 1) * MT, R_LOOP2 + r - 1, i)

        @block.vector
        def _(dve):
            own = Chain(dve, dve_own)

            def first_gained(j):
                dve.wait_ge(x_in[j], 32)
                dve.tensor_tensor(x_gained[:, :, chunk(j)], xres[:, :, chunk(j)],
                                  gainB[:, chunk(j)].unsqueeze(1).to_broadcast([P, MT, NW]), ALU.mult).then_inc(xg_done, 1)

            def mean_square(norm):
                dve.wait_ge(sq_done, (norm + 1) * UN * MT)
                own.done(dve.tensor_reduce(msq[:, :], sumsq[:, :, :], AX.X, ALU.add))
                dve.tensor_scalar(msq[:, :], msq[:, :], 1.0 / D, EPS, ALU.mult, ALU.add).then_inc(msq_done, 1)

            def inverse_rms(norm):
                dve.wait_ge(rms_done, norm + 1)
                dve.reciprocal(rstd[:, :], rms[:, :]).then_inc(rstd_done, 1)

            def soft(z, neg, mag, done):
                own.done(dve.tensor_scalar(neg, z, -1.0, None, ALU.mult))
                dve.tensor_tensor(mag, z, neg, ALU.max).then_inc(done, 1)

            def softplus(out, neg, e, t_, r_, s_, s2, p_, times, done):
                own.done(dve.tensor_scalar(t_, e, 2.0, None, ALU.add))
                own.done(dve.reciprocal(r_, t_))
                own.done(dve.tensor_tensor(s_, e, r_, ALU.mult))
                own.done(dve.tensor_tensor(s2, s_, s_, ALU.mult))
                own.done(dve.tensor_scalar(p_, s2, 1.0 / 15, None, ALU.mult))
                for d in (13, 11, 9, 7, 5, 3):
                    own.done(dve.scalar_tensor_tensor(p_, p_, 1.0 / d, s2, ALU.add, ALU.mult))
                own.done(dve.scalar_tensor_tensor(p_, p_, 1.0, s_, ALU.add, ALU.mult))
                own.done(dve.tensor_scalar(neg, neg, 0.0, 0.5, ALU.max, ALU.mult))
                own.done(dve.tensor_tensor(p_, p_, neg, ALU.add))
                dve.tensor_scalar(out, p_, 2.0 * times, None, ALU.mult).then_inc(done, 1)

            def taps(out, src, row, k0, k1, taps_n, ready=None):
                for k in range(k0, k1):
                    for c in range(CT):
                        w = par[:, c, row + k:row + k + 1]
                        x = src[:, c, k:k + T]
                        if k == 0:
                            b = par[:, c, R_CONVB:R_CONVB + 1] if row == R_CONV else 0.0
                            ins = dve.tensor_scalar(out[:, c, :], x, w, b, ALU.mult, ALU.add)
                        else:
                            own.need(tap_marks[c])
                            ins = dve.scalar_tensor_tensor(out[:, c, :], x, w, out[:, c, :], ALU.mult, ALU.add)
                        if k == taps_n - 1:
                            ins.then_inc(ready, 1)
                        else:
                            tap_marks[c] = own.mark(ins)

            tap_marks = [0] * CT

            def head_sums(n):
                dve.wait_ge(head_sq, n + 1)
                own.done(dve.tensor_reduce(hsum[:, :], lru_om[:, :, :].rearrange("p c (b d) -> p (c b) d", d=HD),
                                           AX.X, ALU.add))
                dve.tensor_scalar(hsum[:, :], hsum[:, :], 1.0 / HD, EPS, ALU.mult, ALU.add).then_inc(head_sum, 1)

            def head_scale(n, aug, gain):
                dve.wait_ge(head_root, n + 1)
                own.done(dve.reciprocal(hinv[:, :], hroot[:, :]))
                dve.tensor_tensor(aug[:, :, 0:HD], stage[:, :, :].rearrange("p m (h d) -> p (m h) d", d=HD),
                                  hinv[:, :].unsqueeze(2).to_broadcast([P, MT * HEADS, HD]), ALU.mult).then_inc(head_scaled, 1)
                dve.wait_ge(head_scaled, n + 1)
                dve.tensor_tensor(aug[:, :, 0:HD], aug[:, :, 0:HD],
                                  bcast[:, gain:gain + HD].unsqueeze(1).to_broadcast([P, MT * HEADS, HD]),
                                  ALU.mult).then_inc(aug_done, 1)

            def score_step(a, g):
                tile, heads = GROUPS[g]
                width, n, c = (tile + 1) * P, len(heads), first_column(g)
                dve.wait_ge(qk_done, a.first + g + 1)
                if a.first + g:
                    dve.wait_ge(p_ready, a.cols + c)
                s_view = a.scores[:, :].rearrange("p (h k) -> p h k", k=width)
                dve.tensor_tensor(s_view, sd[:, 0, :].rearrange("p (h k) -> p h k", k=width),
                                  a.mask[:, T - width:T].unsqueeze(1).to_broadcast([P, n, width]), ALU.add).then_inc(s_ready, 1)
                dve.wait_ge(s_ready, a.first + g + 1)
                top = dve.tensor_reduce(a.negmax[:, c:c + n], s_view, AX.X, ALU.max, negate=True)
                if a.sinks:
                    own.done(top)
                    h = c % HEADS
                    top = dve.tensor_tensor(a.negmax[:, c:c + n], a.negmax[:, c:c + n], a.sinks[0][:, h:h + n], ALU.min)
                top.then_inc(max_ready, 1)

            def normalise(a, tile):
                cols = slice(tile * HEADS, (tile + 1) * HEADS)
                dve.wait_ge(pv_done, a.first + (2 if tile == 0 else len(GROUPS)))
                if a.sinks:
                    dve.wait_ge(sink_exp, sink_step(a.set, tile))
                    own.done(dve.tensor_tensor(a.rowsum[:, cols], a.rowsum[:, cols], a.sinks[1][:, cols], ALU.add))
                own.done(dve.reciprocal(a.rinv[:, cols], a.rowsum[:, cols]))
                r = a.rinv[:, cols].rearrange("p (b a) -> p b a", b=2).unsqueeze(3).to_broadcast([P, 2, HEADS // 2, HD])
                dve.tensor_tensor(head_view(stage[:, tile, :]), head_view(a.out(tile)), r, ALU.mult).then_inc(
                    tp_free[0] if a.set else o_ready, 1)

            def attention_first(a, s):
                if 2 <= s - A0[a.set] < 2 + len(GROUPS):
                    score_step(a, s - A0[a.set] - 2)

            def attention_side(a, s):
                s = s - A0[a.set]
                if a.sinks and s in (4, 8):
                    tile = int(s == 8)
                    cols = slice(tile * HEADS, (tile + 1) * HEADS)
                    dve.wait_ge(max_ready, a.first + (len(GROUPS) if tile else 2))
                    dve.tensor_tensor(a.sinks[1][:, cols], a.negmax[:, cols], a.sinks[0], ALU.subtract).then_inc(sink_arg, 1)
                if s == 7:
                    normalise(a, 0)
                if s == 11 and a.set < 3:
                    normalise(a, 1)

            def side(s):
                if s == 3:
                    dve.wait_ge(f_split, 1)
                    dve.tensor_tensor(f_lo[:, :, :], f_raw[:, :, :], f_hi[:, :, :].bitcast(F32), ALU.subtract).then_inc(f_split, 1)
                    dve.wait_ge(bc_in, 8 * 16)
                    dve.wait_ge(pads, 8)
                    for g in (B_QG, B_AQG, B_CQG):
                        own.done(dve.tensor_scalar(bcast[:, g:g + HD], bcast[:, g:g + HD], HD ** -0.5, None, ALU.mult))
                    marks = [own.mark(dve.tensor_scalar(recip_count[:, g, :], steps[:, :], float(2 << g), None, ALU.min))
                             for g in range(CT)]
                    own.need(marks[-1])
                    dve.reciprocal(recip_count[:, :, :], recip_count[:, :, :]).then_inc(rc_ready, 1)
                if s == 6:
                    dve.wait_ge(f_tok, 2)
                    z = ftok.rearrange("p (m h) -> p m h", m=MT)
                    own.done(dve.tensor_tensor(z, z, bcast[:, B_FB:B_FB + HEADS].unsqueeze(1).to_broadcast([P, MT, HEADS]), ALU.add))
                    soft(ftok[:, :], sp_neg[:, :], sp_abs[:, :], f_abs)
                    dve.wait_ge(par_ready, 1)
                    soft(par[:, :, R_LAM], l_neg[:, :], l_abs[:, :], lam_abs)
                if s == 7:
                    dve.wait_ge(side_read, 2)
                    dve.wait_ge(pads, 8)
                    taps(lru_u, xaT, R_CONV, 0, 2, LRU_TAPS, u_ready)
                if s == 8:
                    dve.wait_ge(f_exp, 1)
                    softplus(logf[:, :], sp_neg[:, :], sp_e[:, :], sp_t[:, :], sp_r[:, :], sp_s[:, :], sp_s2[:, :],
                             sp_p[:, :], -1.0, f_log)
                if s == 9:
                    taps(lru_u, xaT, R_CONV, 2, 4, LRU_TAPS, u_ready)
                if s == 10:
                    dve.wait_ge(lam_exp, 1)
                    softplus(l_c[:, :], l_neg[:, :], l_e[:, :], l_t[:, :], l_r[:, :], l_s[:, :], l_s2[:, :],
                             l_p[:, :], -LRU_C, c_ready)
                    dve.wait_ge(c_ready, 1)
                    dve.tensor_scalar(l_c2[:, :], l_c[:, :], 2.0, None, ALU.mult).then_inc(c_ready, 1)
                    dve.wait_ge(c_ready, 2)
                if s == 11:
                    dve.wait_ge(cum_mm, 1)
                    dve.wait_ge(pads, 8)
                    cum = sd[:, 1, 0:MT * HEADS]
                    dve.tensor_copy(q_aug[:, :, HD:HD + 1], cum.unsqueeze(2)).then_inc(f_cum, 2)
                    dve.tensor_scalar(k_aug[:, :, HD + 1:AUG], cum.unsqueeze(2), -1.0, None, ALU.mult).then_inc(f_cum, 2)
                if s == 13:
                    dve.wait_ge(r_ready, CT)
                    for c in range(CT):
                        dve.tensor_scalar(lru_z[:, c, :], lru_r[:, c, :], l_c2[:, c:c + 1], None, ALU.mult).then_inc(z_ready, 1)
                if s == 14:
                    dve.wait_ge(z_ready, CT)
                    own.done(dve.tensor_scalar(lru_p[:, :, :], lru_z[:, :, :], -1.0 / 720, None, ALU.mult))
                if s in (15, 17, 18, 19, 20):
                    d = {15: 120, 17: 24, 18: 6, 19: 2, 20: 1}[s]
                    own.done(dve.scalar_tensor_tensor(lru_p[:, :, :], lru_p[:, :, :], -1.0 / d, lru_z[:, :, :], ALU.add, ALU.mult))
                if s == 16:
                    dve.wait_ge(units_used, 16)
                    dve.wait_ge(read_act, 6)
                    dve.wait_ge(rstd_done, 1)
                    for m in range(MT):
                        dve.scalar_tensor_tensor(stage[:, m, :], acc[:, 1, m, :], rstd[:, m:m + 1], gc_sb[:, m, :],
                                                 ALU.mult, ALU.mult).then_inc(read_dve, 1)
                if s == 20:
                    own.done(dve.tensor_scalar(lru_z[:, :, :].bitcast(I32), lru_z[:, :, :], -0.25, None, ALU.is_gt))
                    dve.wait_ge(asq_ready, 1)
                    dve.copy_predicated(lru_om[:, :, :], lru_z[:, :, :].bitcast(I32), lru_p[:, :, :]).then_inc(om_ready, 1)
                if s == 23:
                    dve.wait_ge(root_ready, 1)
                    dve.wait_ge(gu_ready, 1)
                    own.done(dve.tensor_tensor(lru_p[:, :, :], lru_om[:, :, :], lru_g[:, :, :], ALU.mult))
                    for c in range(CT):
                        dve.tensor_tensor_scan(lru_u[:, c, :], lru_r[:, c, :], lru_p[:, c, :], 0.0, ALU.mult,
                                               ALU.add).then_inc(h_ready, 1)
                if s == 24:
                    dve.wait_ge(side_read, 6)
                    dve.wait_ge(om_ready, 1)
                    taps(lru_z, zT, R_SC, 0, 1, SC_TAPS, sc_ready)
                if s == 25:
                    taps(lru_z, zT, R_SC, 1, 2, SC_TAPS, sc_ready)
                    head_sums(0)
                if s == 26:
                    taps(lru_z, zT, R_SC, 2, 3, SC_TAPS, sc_ready)
                    dve.wait_ge(y_hi, 1)
                    dve.tensor_tensor(opB_lo[:, 0:CT, :], lru_u[:, :, :], opB_hi[:, 0:CT, :].bitcast(F32),
                                      ALU.subtract).then_inc(y_lo, 1)
                if s == 27:
                    head_scale(0, q_aug, B_QG)
                if s == 28:
                    dve.wait_ge(y_hi, 1 + CT)
                    for c in range(CT):
                        dve.scalar_tensor_tensor(opB_lo[:, CT + c, :], sd[:, c // 2, (c % 2) * T:(c % 2 + 1) * T],
                                                 par[:, c, R_PSCALE:R_PSCALE + 1],
                                                 opB_hi[:, CT + c, :].bitcast(F32), ALU.mult, ALU.subtract).then_inc(y_lo, 1)
                if s == 29:
                    head_sums(1)
                if s == 31:
                    head_scale(1, k_aug, B_KG)
                if s == 32:
                    dve.wait_ge(y_hi, 2 + CT)
                    dve.tensor_tensor(opB_lo[:, 2 * CT:3 * CT, :], lru_z[:, :, :], opB_hi[:, 2 * CT:3 * CT, :].bitcast(F32),
                                      ALU.subtract).then_inc(y_lo, 1)
                attention_side(attentions[0], s)
                if s == 48:
                    turned_lo(dve, T_YD, opB_hi, opB_lo, 3 * CT)

            def branch_part(n, k, run, done, i=0):
                dve.wait_ge(units_used, done)
                gates_before = (readers_before(R_GATE0, "A") + k + 1) * MT
                dve.wait_ge(read_act, i * (NB * MT) + gates_before)
                if k:
                    before = k - 1 if k > 1 else 0
                    if k > 1 or not isinstance(i, int) or i:
                        dve.wait_ge(merged_ready, i * (NB - 1) + before)
                for m in range(MT):
                    dve.tensor_tensor(stage[:, m, :] if k else xres[:, m, chunk(n)], acc[:, run % 2, m, :],
                                      gates[:, k, m, :], ALU.mult).then_inc(read_dve, 1)

            first_gained(0)
            for j in range(UN):
                if j == 0:
                    turned_lo(dve, T_XN, opA_hi, opA_lo, 0)
                lo_unit(dve, 0, j)
                if j:
                    turned_lo(dve, T_XN + j * MT, opA_hi, opA_lo, j * CT)
                if j < UN - 1:
                    first_gained(j + 1)
            mean_square(0)
            inverse_rms(0)
            side(3)
            for g in range(1, G_GATE0 + NB):
                for j in range(UN):
                    attention_first(attentions[0], g * UN + j)
                    lo_unit(dve, g, j)
                    side(g * UN + j)
            dve_g = G_GATE0 + NB
            for j in range(NB):
                lo_unit(dve, dve_g, j)
                side(dve_g * UN + j)
                if j:
                    branch_part(0, j - 1, R_GATE0 + NB + j - 1, dve_g * UN + j)
            def merged_lo(c):
                turned_lo(dve, T_MERGED + c * MT, opA_hi, opA_lo, c * CT)

            def gate_turn(i, last=False):
                for k in range(NB + 1):
                    for j in range(UN):
                        lo_unit(dve, G_LOOP + k + i * 5, j)
                        if last and k == NB and j >= 2:
                            merged_lo(j - 2)
                        if k == 0 and j == 0:
                            branch_part(i, NB - 1, R_LOOP - 1, i * (5 * UN) + G_LOOP * UN, i)
                        if k == NB and j:
                            branch_part(i + 1, j - 1, R_LOOP + NB + j - 1, i * (5 * UN) + (G_LOOP + NB) * UN + j, i + 1)

            with dve.Fori(0, 2) as i:
                gate_turn(i)
            gate_turn(2, last=True)

            def add_to_x(run, n, done):
                dve.wait_ge(units_used, done)
                for m in range(MT):
                    dve.tensor_tensor(xres[:, m, chunk(n)], acc[:, run % 2, m, :], xres[:, m, chunk(n)],
                                      ALU.add).then_inc(read_dve, 1)

            for n in range(UN):
                for j in range(UN):
                    lo_unit(dve, G_OUT + n, j)
                    if n == 0 and j == 0:
                        branch_part(3, NB - 1, R_OUT - 1, G_OUT * UN, 3)
                    if n == 0 and j in (0, 2):
                        merged_lo(2 + j // 2)
                    if n and j == 0:
                        dve.wait_ge(x_back[n - 1], 16)
                        add_to_x(R_OUT + n - 1, n - 1, (G_OUT + n) * UN)
                    if n and j == 2:
                        turned_lo(dve, T_XN2 + (n - 1) * MT, opB_hi, opB_lo, (n - 1) * CT)
            for c in range(UN):
                for j in range(UN):
                    lo_unit(dve, G_UP0 + c, j)
                    if j == 0 and c == 0:
                        dve.wait_ge(x_back[3], 16)
                        add_to_x(R_UP0 - 1, 3, G_UP0 * UN)
                        mean_square(1)
                        inverse_rms(1)
                    if j == 2 and c == 0:
                        turned_lo(dve, T_XN2 + 3 * MT, opB_hi, opB_lo, 3 * CT)
                    if j == 2 and c:
                        turned_lo(dve, T_HID + (c - 1) * MT, opA_hi, opA_lo, (c - 1) * CT)
            with dve.Fori(0, 3) as i:
                for r in range(2 * UN):
                    for j in range(UN):
                        lo_unit(dve, i * (2 * UN) + (G_DLOOP + r), j)
                        up = UN - 1 if r == 0 else r - UN - 1
                        if j == 2 and up >= 0:
                            before = T_HID + (up if r == 0 else UN + up) * MT
                            turned_lo(dve, i * (UN * MT) + before, opA_hi, opA_lo, up * CT)
                        if j == 0 and 1 <= r <= UN:
                            add_to_x(R_DLOOP + r - 1, r - 1, i * (8 * UN) + (G_DLOOP + r) * UN)
            for n in range(UN):
                for j in range(UN):
                    lo_unit(dve, G_DLAST + n, j)
                    if n == 0 and j == 2:
                        turned_lo(dve, T_HID + 15 * MT, opA_hi, opA_lo, 3 * CT)
                    if n and j == 0:
                        add_to_x(R_DLAST + n - 1, n - 1, (G_DLAST + n) * UN)
                    if n and j == 2:
                        turned_lo(dve, T_XN3 + (n - 1) * MT, opB_hi, opB_lo, (n - 1) * CT)

            conv_marks = [0] * CT

            def conv_taps(k0, k1):
                for k in range(k0, k1):
                    for c in (0, 1):
                        w, x = par[:, c, R_CONV2 + k:R_CONV2 + k + 1], hT[:, c, k:k + T]
                        if k == 0:
                            ins = dve.tensor_scalar(yT[:, c, :], x, w, par[:, c, R_CONV2B:R_CONV2B + 1], ALU.mult, ALU.add)
                        else:
                            own.need(conv_marks[c])
                            ins = dve.scalar_tensor_tensor(yT[:, c, :], x, w, yT[:, c, :], ALU.mult, ALU.add)
                        if k == CONV_TAPS - 1:
                            ins.then_inc(conv_dve, 1)
                        else:
                            conv_marks[c] = own.mark(ins)

            def head2_heads(n):
                _, src, _, _, width = NORMS2[n]
                heads = width // HD
                stat = lambda x: x[:, 0:MT * heads].rearrange("p (m h) -> p m h", m=MT)
                return src.rearrange("p m (h d) -> p m h d", d=HD), width, heads, stat

            def mix_turned_lo(name, a, m):
                b, n = tp_use(name)
                kt, tokens = MIX_KT[a], slice(m * P, (m + 1) * P)
                dve.wait_ge(mix_hi, [x for x in TP1 if x.startswith("mix")].index(name) + 1)
                dve.tensor_tensor(opA_lo[:, kt:kt + CT, tokens], tp[:, b].rearrange("p (c t) -> p c t", c=CT),
                                  opA_hi[:, kt:kt + CT, tokens].bitcast(F32), ALU.subtract).then_inc(tp_free[b], 1)

            def side2(s):
                for a in attentions[1:]:
                    attention_side(a, s)
                if s == 0:
                    add_to_x(R_DLAST + 3, 3, (G_DLAST + 4) * UN)
                    mean_square(2)
                    inverse_rms(2)
                if s == 2:
                    turned_lo(dve, T_XN3 + 3 * MT, opB_hi, opB_lo, 3 * CT)
                if s == 4:
                    dve.wait_ge(masks_raw, 2)
                    own.mark(dve.tensor_scalar(dist[:, 0, :], dist[:, 0, :], 3, None, ALU.bitwise_and))
                    own.done(dve.tensor_scalar(dist[:, 1, :], dist[:, 1, :], 15, None, ALU.bitwise_and))
                    own.mark(dve.tensor_scalar(mult4[:, :], dist[:, 0, :], 0.0, None, ALU.is_equal))
                    own.done(dve.tensor_scalar(mult16[:, :], dist[:, 1, :], 0.0, None, ALU.is_equal))
                    own.mark(dve.tensor_scalar(near[:, :], mult4[:, :], float(np.log(2)), None, ALU.mult))
                    own.done(dve.tensor_scalar(far[:, :], mult4[:, :], -NEG, NEG, ALU.mult, ALU.add))
                    dve.scalar_tensor_tensor(near[:, :], mult16[:, :], float(np.log(1.5)), near[:, :],
                                             ALU.mult, ALU.add).then_inc(mults_ready, 1)
                    dve.scalar_tensor_tensor(far[:, :], mult16[:, :], float(np.log(2)), far[:, :],
                                             ALU.mult, ALU.add).then_inc(mults_ready, 1)
                    for a in range(2):
                        own.done(dve.tensor_scalar(
                            nsink[:, a * HEADS:(a + 1) * HEADS].rearrange("p (b a) -> p b a", b=2),
                            bcast[:, B_SINK + a * HEADS:B_SINK + (a + 1) * HEADS].rearrange("p (a b) -> p b a", b=2),
                            -1.0, None, ALU.mult))
                if s == 10:
                    for b in range(2):
                        dve.wait_ge(tp_free[b], 1)
                    dve.wait_ge(pads2, 1)
                if 10 <= s < 9 + len(TAPS_DVE):
                    conv_taps(TAPS_DVE[s - 10], TAPS_DVE[s - 9])
                if s in (13, 17, 21, 25, 29):
                    n = (s - 13) // 4
                    _, width, heads, stat = head2_heads(n)
                    dve.wait_ge(h2_sq, n + 1)
                    own.done(dve.tensor_reduce(stat(hsum), squares2[:, :, 0:width].rearrange("p m (h d) -> p m h d", d=HD),
                                               AX.X, ALU.add))
                    dve.tensor_scalar(hsum[:, :], hsum[:, :], 1.0 / HD, EPS, ALU.mult, ALU.add).then_inc(h2_sum, 1)
                if s in (15, 19, 23, 27, 31):
                    n = (s - 15) // 4
                    x, width, heads, stat = head2_heads(n)
                    dve.wait_ge(h2_root, n + 1)
                    own.done(dve.reciprocal(hinv[:, :], hroot[:, :]))
                    dve.tensor_tensor(x, x, stat(hinv).unsqueeze(3).to_broadcast([P, MT, heads, HD]),
                                      ALU.mult).then_inc(h2_scaled, 1)
                if s == 26:
                    for name in ("y0", "y1"):
                        b, n = tp_use(name)
                        dve.wait_ge(tp_free[b], n + 1)
                    for m in range(MT):
                        own.done(dve.bn_stats(bn6[:, m, :], y_tok[:, m, :]))
                        own.done(dve.bn_aggr(bn2[:, m, :], bn6[:, m, :]))
                    dve.tensor_scalar(bn_var[:, :].unsqueeze(2), bn2[:, :, 1:2], EPS, None, ALU.add).then_inc(ln_var, 1)
                if s == 28:
                    dve.wait_ge(ln_root, 1)
                    own.done(dve.reciprocal(bn_inv[:, :], bn_root[:, :]))
                    for m in range(MT):
                        dve.tensor_scalar(y_tok[:, m, :], y_tok[:, m, :], bn2[:, m, 0:1], bn_inv[:, m:m + 1],
                                          ALU.subtract, ALU.mult).then_inc(ln_done, 1)
                if s == 31:
                    dve.wait_ge(conf_hi, 1)
                    dve.tensor_tensor(opA_lo[:, K_CONV:K_CONV + CT, :], silT[:, :, :],
                                      opA_hi[:, K_CONV:K_CONV + CT, :].bitcast(F32), ALU.subtract).then_inc(conf_lo, 1)
                if s - 2 in MIX2:
                    mix_turned_lo(*MIX2[s - 2])
                if s == LAST_MIX + 1:
                    mix_turned_lo("mix31", 3, 1)
                if 47 <= s <= 50:
                    turned_lo(dve, T_XN4 + (s - 47) * MT, opB_hi, opB_lo, (s - 47) * CT)
                if s in (35, 36, 39, 40):
                    n = (35, 36, 39, 40).index(s)
                    add_to_x(R_OUT2 + n, n, G_OUT2 * UN + s - 32)
                if 41 <= s < 49:
                    u = s - 32
                    add_to_x(R_OUT2 + UN + u - 9, (u - 9) % UN, G_OUT2 * UN + u)
                if s == 50:
                    mean_square(3)
                    inverse_rms(3)

            for u in range(12 * UN):
                for a in attentions[1:]:
                    attention_first(a, u)
                if u == LAST_MIX + 1:
                    normalise(attentions[3], 1)
                lo_unit(dve, G_HEAD2 + u // UN, u % UN, head2_cols(HEAD2[u // UN]) if u < 8 * UN else NW)
                side2(u)

            def hidden(run, done, i=0):
                dve.wait_ge(units_used, done)
                dve.wait_ge(read_act, i * (CH2_LOOP * MT) + readers_before(run, "A") * MT)
                for m in range(MT):
                    dve.scalar_tensor_tensor(stage[:, m, :], acc[:, run % 2, m, :], rstd[:, m:m + 1], silu_gate[:, m, :],
                                             ALU.mult, ALU.mult).then_inc(read_dve, 1)

            for r in range(2 * CH2_FIRST):
                for j in range(UN):
                    lo_unit(dve, G_PAIR0 + r, j)
                    if r == 0:
                        side2(12 * UN + j)
                    if r and r % 2 == 0 and j == 0:
                        hidden(R_PAIR0 + r - 1, (G_PAIR0 + r) * UN)
                    if r and r % 2 == 0 and j == 2:
                        turned_lo(dve, T_HID2 + (r // 2 - 1) * MT, opA_hi, opA_lo, (r // 2 - 1) * CT)
            down0 = G_PAIR0 + 2 * CH2_FIRST
            for u in range(CH2_FIRST * UN):
                lo_unit(dve, down0 + u // UN, u % UN)
                if u == 0:
                    hidden(R_DOWN0 - 1, down0 * UN)
                if u == 2:
                    turned_lo(dve, T_HID2 + (CH2_FIRST - 1) * MT, opA_hi, opA_lo, (CH2_FIRST - 1) * CT)
                if u and u % CH2_FIRST == 0:
                    n = u // CH2_FIRST - 1
                    add_to_x(R_DOWN0 + n, n, down0 * UN + u)
            with dve.Fori(0, 2) as i:
                for r in range(LOOP2_RUNS):
                    c = r // 2
                    for j in range(UN):
                        lo_unit(dve, i * LOOP2_RUNS + (G_LOOP2 + r), j)
                        done = i * LOOP2_UNITS + (G_LOOP2 + r) * UN
                        if j == 0 and r == 0:
                            add_to_x(R_LOOP2 - 1, 3, done)
                        if j == 0 and r % 2 == 0 and 1 <= c <= CH2_LOOP:
                            hidden(R_LOOP2 + r - 1, done, i)
                        if j == 0 and r > 2 * CH2_LOOP:
                            n = r - 2 * CH2_LOOP - 1
                            add_to_x(R_LOOP2 + 2 * CH2_LOOP + n, n, done)
                        if j == 2 and r % 2 == 0 and 1 <= c <= CH2_LOOP:
                            before = T_HID2 + (CH2_FIRST + c - 1) * MT
                            turned_lo(dve, i * (CH2_LOOP * MT) + before, opA_hi, opA_lo, (c - 1) * CT)
            add_to_x(R_LOOP2 + LOOP2_RUNS - 1, 3, (G_LOOP2 + 2 * LOOP2_RUNS) * UN)


def kernel(**inputs):
    import concourse.bacc as bacc
    from concourse.bass_utils import run_bass_kernel_spmd

    nc = bacc.Bacc("TRN2", target_bir_lowering=False, num_devices=1, dynamic_dma_scratch_size=1024)
    arrays, t = {}, {}
    for name, a in inputs.items():
        a = np.ascontiguousarray(a)
        arrays[f"in_{name}"] = a
        t[name] = nc.dram_tensor(f"in_{name}", a.shape, mybir.dt.from_np(a.dtype), kind="ExternalInput").ap()
    out = nc.dram_tensor("out_x", (1, T, D), F32, kind="ExternalOutput").ap()
    build(nc, t, out)
    r = run_bass_kernel_spmd(nc, [arrays], core_ids=[0])
    return r.results[0]["out_x"]
```
